# Optimizing a Trainium2 kernel written in Bass

```python
import math
import jax, jax.numpy as jnp
from jax import lax
import numpy as np

D_MODEL = 1024
BATCH = 1
SEQ = 2048
DEPTH = 1

MEM_LEN = 256
MLA_HEADS = 8
MLA_NOPE = 64
MLA_ROPE = 32
MLA_V = 64
MLA_Q_LORA = 256
MLA_KV_LORA = 128
MLA_WIDTH = MLA_HEADS * MLA_V
SB_HEADS = 8
SB_HEAD_DIM = 64
SB_WIDTH = SB_HEADS * SB_HEAD_DIM
MEM_HEADS = 4
MEM_HEAD_DIM = 128
MEM_WIDTH = MEM_HEADS * MEM_HEAD_DIM
N_BRANCHES = 3

BLOCK_Q = 128
ROPE_BASE = 10000.0
RMS_EPS = 1e-6
LN_EPS = 1e-5
DEEPNORM_ALPHA = (2.0 * DEPTH) ** 0.25
DEEPNORM_BETA = (8.0 * DEPTH) ** -0.25

IN_SIZES = [
    MLA_Q_LORA, MLA_KV_LORA, MLA_ROPE, MLA_WIDTH,
    SB_WIDTH, SB_WIDTH, SB_WIDTH, SB_WIDTH,
    MEM_WIDTH, MEM_WIDTH,
]
IN_WIDTH = int(sum(IN_SIZES))
IN_OFFSETS = [int(o) for o in np.cumsum(IN_SIZES)[:-1]]

kernel_name = "hybrid_mla_stickbreaking_memxattn_deepnorm"

def _rms_norm(x, g):
    x32 = x.astype(jnp.float32)
    y = x32 * lax.rsqrt(jnp.mean(x32 * x32, axis=-1, keepdims=True) + RMS_EPS)
    return (y * g.astype(jnp.float32)).astype(x.dtype)

def _layer_norm(x, g, b):
    x32 = x.astype(jnp.float32)
    mu = jnp.mean(x32, axis=-1, keepdims=True)
    xc = x32 - mu
    var = jnp.mean(xc * xc, axis=-1, keepdims=True)
    y = xc * lax.rsqrt(var + LN_EPS) * g.astype(jnp.float32) + b.astype(jnp.float32)
    return y.astype(x.dtype)

def _rope(x, pos):
    half = x.shape[-1] // 2
    freqs = ROPE_BASE ** (-jnp.arange(half, dtype=jnp.float32) / half)
    ang = pos.astype(jnp.float32)[:, None] * freqs[None, :]
    cos = jnp.cos(ang)[None, :, None, :]
    sin = jnp.sin(ang)[None, :, None, :]
    x32 = x.astype(jnp.float32)
    x1, x2 = x32[..., :half], x32[..., half:]
    out = jnp.concatenate([x1 * cos - x2 * sin, x1 * sin + x2 * cos], axis=-1)
    return out.astype(x.dtype)

def _sweep_query_blocks(q, k, v, weights_fn):
    seq = q.shape[1]
    outs = []
    for start in range(0, seq, BLOCK_Q):
        end = start + BLOCK_Q
        scores = jnp.einsum('bqhd,bkhd->bhqk', q[:, start:end], k[:, :end]).astype(jnp.float32)
        q_pos = (start + jnp.arange(BLOCK_Q))[:, None]
        k_pos = jnp.arange(end)[None, :]
        w = weights_fn(scores, q_pos, k_pos)
        outs.append(jnp.einsum('bhqk,bkhd->bqhd', w.astype(v.dtype), v[:, :end]))
    return jnp.concatenate(outs, axis=1)

def _softmax_causal_weights(scale):
    def fn(scores, q_pos, k_pos):
        s = jnp.where(k_pos <= q_pos, scores * scale, jnp.finfo(jnp.float32).min)
        return jax.nn.softmax(s, axis=-1)
    return fn

def _stick_breaking_weights(scale):
    def fn(scores, q_pos, k_pos):
        z = scores * scale
        strict = k_pos < q_pos
        log_beta = jax.nn.log_sigmoid(z)
        log_keep = jnp.where(strict, jax.nn.log_sigmoid(-z), 0.0)
        after = lax.cumsum(log_keep, axis=log_keep.ndim - 1, reverse=True) - log_keep
        return jnp.where(strict, jnp.exp(log_beta + after), 0.0)
    return fn

def _hybrid_layer(x, mem, w_in, w_mem_kv, q_a_gain, w_q_b, kv_a_gain, w_kv_b,
                  w_branch_mla, w_branch_sb, w_branch_mem, w_merge_gate, b_merge_gate,
                  w_out, ln_gain, ln_bias):
    b, s, _ = x.shape
    pos = jnp.arange(s, dtype=jnp.int32)
    proj = x @ w_in
    (c_q, c_kv, k_rope, gate_a, q_b, k_b, v_b, gate_b, q_m, gate_m) = jnp.split(proj, IN_OFFSETS, axis=-1)

    q_a = (_rms_norm(c_q, q_a_gain) @ w_q_b).reshape(b, s, MLA_HEADS, MLA_NOPE + MLA_ROPE)
    kv_a = (_rms_norm(c_kv, kv_a_gain) @ w_kv_b).reshape(b, s, MLA_HEADS, MLA_NOPE + MLA_V)
    q_nope, q_pe = q_a[..., :MLA_NOPE], q_a[..., MLA_NOPE:]
    k_nope, v_a = kv_a[..., :MLA_NOPE], kv_a[..., MLA_NOPE:]
    k_pe = _rope(k_rope.reshape(b, s, 1, MLA_ROPE), pos)
    q_full = jnp.concatenate([q_nope, _rope(q_pe, pos)], axis=-1)
    k_full = jnp.concatenate([k_nope, jnp.broadcast_to(k_pe, (b, s, MLA_HEADS, MLA_ROPE))], axis=-1)
    o_a = _sweep_query_blocks(q_full, k_full, v_a,
                              _softmax_causal_weights(1.0 / math.sqrt(MLA_NOPE + MLA_ROPE)))
    y_a = (o_a.reshape(b, s, MLA_WIDTH) * jax.nn.silu(gate_a)) @ w_branch_mla

    q_sb = q_b.reshape(b, s, SB_HEADS, SB_HEAD_DIM)
    k_sb = k_b.reshape(b, s, SB_HEADS, SB_HEAD_DIM)
    v_sb = v_b.reshape(b, s, SB_HEADS, SB_HEAD_DIM)
    o_b = _sweep_query_blocks(q_sb, k_sb, v_sb, _stick_breaking_weights(1.0 / math.sqrt(SB_HEAD_DIM)))
    y_b = (o_b.reshape(b, s, SB_WIDTH) * jax.nn.silu(gate_b)) @ w_branch_sb

    mem_kv = (mem @ w_mem_kv).reshape(b, mem.shape[1], 2, MEM_HEADS, MEM_HEAD_DIM)
    k_m, v_m = mem_kv[:, :, 0], mem_kv[:, :, 1]
    q_mh = q_m.reshape(b, s, MEM_HEADS, MEM_HEAD_DIM)
    sc = jnp.einsum('bshd,bmhd->bhsm', q_mh, k_m).astype(jnp.float32) / math.sqrt(MEM_HEAD_DIM)
    p_m = jax.nn.softmax(sc, axis=-1).astype(v_m.dtype)
    o_m = jnp.einsum('bhsm,bmhd->bshd', p_m, v_m).reshape(b, s, MEM_WIDTH)
    y_m = (o_m * jax.nn.silu(gate_m)) @ w_branch_mem

    g = jax.nn.sigmoid(x @ w_merge_gate + b_merge_gate)
    g_a, g_b, g_m = jnp.split(g, N_BRANCHES, axis=-1)
    merged = g_a * y_a + g_b * y_b + g_m * y_m
    out = merged @ w_out

    return _layer_norm(DEEPNORM_ALPHA * x + out, ln_gain, ln_bias)

def setup_inputs(seed: int = 0) -> dict:
    key = jax.random.key(seed)
    ks = jax.random.split(key, 18)
    f32 = jnp.float32

    def nrm(k, shape, fan_in, gain=1.0):
        return jax.random.normal(k, shape, f32) * (gain * fan_in ** -0.5)

    L = DEPTH
    return {
        "x": jax.random.normal(ks[0], (BATCH, SEQ, D_MODEL), f32),
        "mem": jax.random.normal(ks[1], (BATCH, MEM_LEN, D_MODEL), f32),
        "w_in": nrm(ks[2], (L, D_MODEL, IN_WIDTH), D_MODEL),
        "w_mem_kv": nrm(ks[3], (L, D_MODEL, 2 * MEM_WIDTH), D_MODEL),
        "q_a_gain": 1.0 + 0.01 * jax.random.normal(ks[4], (L, MLA_Q_LORA), f32),
        "w_q_b": nrm(ks[5], (L, MLA_Q_LORA, MLA_HEADS * (MLA_NOPE + MLA_ROPE)), MLA_Q_LORA),
        "kv_a_gain": 1.0 + 0.01 * jax.random.normal(ks[6], (L, MLA_KV_LORA), f32),
        "w_kv_b": nrm(ks[7], (L, MLA_KV_LORA, MLA_HEADS * (MLA_NOPE + MLA_V)), MLA_KV_LORA),
        "w_branch_mla": nrm(ks[8], (L, MLA_WIDTH, D_MODEL), MLA_WIDTH, DEEPNORM_BETA),
        "w_branch_sb": nrm(ks[9], (L, SB_WIDTH, D_MODEL), SB_WIDTH, DEEPNORM_BETA),
        "w_branch_mem": nrm(ks[10], (L, MEM_WIDTH, D_MODEL), MEM_WIDTH, DEEPNORM_BETA),
        "w_merge_gate": nrm(ks[11], (L, D_MODEL, N_BRANCHES * D_MODEL), D_MODEL),
        "b_merge_gate": 0.01 * jax.random.normal(ks[12], (L, N_BRANCHES * D_MODEL), f32),
        "w_out": nrm(ks[13], (L, D_MODEL, D_MODEL), D_MODEL, DEEPNORM_BETA),
        "ln_gain": 1.0 + 0.01 * jax.random.normal(ks[14], (L, D_MODEL), f32),
        "ln_bias": 0.01 * jax.random.normal(ks[15], (L, D_MODEL), f32),
    }

def reference(x, mem, w_in, w_mem_kv, q_a_gain, w_q_b, kv_a_gain, w_kv_b,
              w_branch_mla, w_branch_sb, w_branch_mem, w_merge_gate, b_merge_gate,
              w_out, ln_gain, ln_bias):
    h = x
    for l in range(DEPTH):
        h = _hybrid_layer(h, mem, w_in[l], w_mem_kv[l], q_a_gain[l], w_q_b[l], kv_a_gain[l], w_kv_b[l],
                          w_branch_mla[l], w_branch_sb[l], w_branch_mem[l], w_merge_gate[l],
                          b_merge_gate[l], w_out[l], ln_gain[l], ln_bias[l])
    return h


_drawn_inputs = setup_inputs


def setup_inputs(seed=0):
    import zlib

    import numpy as np

    out = dict(_drawn_inputs(seed))
    spreads = {}
    factors = {'mem': 5.913,
     'w_mem_kv': 5.516,
     'q_a_gain': 8.0,
     'w_q_b': 5.948,
     'kv_a_gain': 8.0,
     'w_kv_b': 4.973,
     'w_branch_mla': 5.036,
     'w_branch_mem': 5.565,
     'b_merge_gate': 8.0,
     'ln_gain': 189.647,
     'ln_bias': 189.058,
     'w_branch_sb': 22.994}
    for name, (base, spread) in spreads.items():
        noise = np.random.default_rng([zlib.crc32(name.encode()), seed]).standard_normal(out[name].shape)
        drawn = base * np.exp(spread * noise) if base else spread * noise
        out[name] = __import__('jax').numpy.asarray(drawn.astype(out[name].dtype))
    for name, factor in factors.items():
        out[name] = (out[name] * factor).astype(out[name].dtype)
    return out
```

```python
from contextlib import ExitStack

import numpy as np
import concourse.bass as bass
from concourse import mybir

P = 128
D = 1024
S = 2048
KT = D // P
CH = 512
NCH = S // CH
TT = S // P
MEM = 256
MT = MEM // P
QL, KVL, ROPE, NOPE, VD, H = 256, 128, 32, 64, 64, 8
SBD = 64
MH, MD = 4, 128
NB_LAT, NB_GATE, NB_COPY, NB_MERGE = 4, 12, 16, 24
NBLK = NB_LAT + NB_GATE + NB_COPY + NB_MERGE
B_GATE, B_COPY, B_MERGE = NB_LAT, NB_LAT + NB_GATE, NB_LAT + NB_GATE + NB_COPY
RMS_EPS, LN_EPS = 1e-6, 1e-5
ALPHA = 2.0 ** 0.25
BIG = 3.0e38

F32 = mybir.dt.float32
F32R = mybir.dt.float32r
ALU = mybir.AluOpType
ACT = mybir.ActivationFunctionType
AX_X = mybir.AxisListType.X


def as_f32(ap):
    return ap.bitcast(F32)


class Scope:

    def __init__(self, nc):
        self.nc, self.ctx, self.sems = nc, ExitStack(), []

    def __enter__(self):
        return self

    def __exit__(self, *a):
        self.ctx.__exit__(*a)
        if self.sems and a[0] is None:
            self.nc.clear_and_free_semaphores(self.sems)
            self.nc.all_engine_barrier()

    def sb(self, name, shape, dt=F32):
        return self.ctx.enter_context(self.nc.sbuf_tensor(name, shape, dt))

    def ps(self, name, shape, dt=F32):
        return self.ctx.enter_context(self.nc.psum_tensor(name, shape, dt))

    def sem(self, name):
        self.sems.append(self.nc.alloc_semaphore(name=name))
        return self.sems[-1]

    def block(self):
        return self.ctx.enter_context(self.nc.Block())


def load_x_transposed(nc, x, ident, xTh, xTl):
    NBANK = 8
    with Scope(nc) as c:
        xin = c.sb("xin", [P, 2, 4, D])
        bank = [c.ps(f"xT_ps{i}", [P, CH]) for i in range(NBANK)]
        loaded = [c.sem(f"x_loaded{i}") for i in range(2)]
        turned = c.sem("x_turned")
        high_done = c.sem("x_high_done")
        low_done = c.sem("x_low_done")
        ident_zero = c.sem("ident_zero")
        ident_ready = c.sem("ident_ready")
        block = c.block()
        xg = x.rearrange("b (g t p) d -> (b g) p t d", t=4, p=P)

        @block.sync
        def _(sp):
            for g in range(NCH):
                if g >= 2:
                    sp.wait_ge(turned, KT * (g - 1))
                sp.dma_start(xin[:, g % 2], xg[g]).then_inc(loaded[g % 2], 16)

        @block.gpsimd
        def _(pool):
            pool.memset(ident[:], 0.0).then_inc(ident_zero, 1)
            pool.wait_ge(ident_zero, 1)
            pool.affine_select(out=ident[:], in_=ident[:], compare_op=ALU.not_equal, fill=1.0, base=0,
                               pattern=[[-1, P]], channel_multiplier=1).then_inc(ident_ready, 1)

        @block.tensor
        def _(pe):
            pe.wait_ge(ident_ready, 1)
            for g in range(NCH):
                pe.wait_ge(loaded[g % 2], 16 * (g // 2 + 1))
                for k in range(KT):
                    n = g * KT + k
                    if n >= NBANK:
                        pe.wait_ge(low_done, n - NBANK + 1)
                    for t in range(4):
                        mm = pe.transpose(bank[n % NBANK][:, t * P:(t + 1) * P],
                                          xin[:, g % 2, t, k * P:(k + 1) * P], ident[:])
                    mm.then_inc(turned, 1)

        @block.scalar
        def _(act):
            for n in range(NCH * KT):
                g, k = divmod(n, KT)
                act.wait_ge(turned, n + 1)
                act.activation(xTh[:, k, g * CH:(g + 1) * CH], bank[n % NBANK][:],
                               ACT.Copy).then_inc(high_done, 1)

        @block.vector
        def _(dve):
            for n in range(NCH * KT):
                g, k = divmod(n, KT)
                cols = slice(g * CH, (g + 1) * CH)
                dve.wait_ge(high_done, n + 1)
                dve.tensor_tensor(xTl[:, k, cols], bank[n % NBANK][:], as_f32(xTh[:, k, cols]),
                                  ALU.subtract).then_inc(low_done, 1)


def project_x(nc, w_all, projT, xTh, xTl):
    NPAIR = NBLK // 2
    with Scope(nc) as c:
        wraw = c.sb("wraw", [P, 2, KT * P + 1])
        wh = c.sb("wh", [P, 2, KT * P], F32R)
        wl = c.sb("wl", [P, 2, KT * P], F32R)
        bias = c.sb("proj_bias", [P, 2])
        ones = c.sb("ones", [P, 1])
        ones_row = ones[:, 0:1].broadcast_to([P, KT * P])
        stage = c.sb("proj_stage", [P, 2, S])
        sig = c.sb("gate_sigmoid", [P, 2, CH])
        acc = [[c.ps(f"proj_ps{u}{n}", [P, CH]) for n in range(NCH)] for u in range(2)]
        w_loaded = [c.sem(f"w_loaded{u}") for u in range(2)]
        ones_set = c.sem("ones_set")
        high_done = c.sem("w_high_done")
        low_done = c.sem("w_low_done")
        product = c.sem("proj_product")
        sig_done = c.sem("sig_done")
        evac = c.sem("proj_evac")
        stored = [c.sem(f"proj_stored{u}") for u in range(2)]
        block = c.block()

        @block.sync
        def _(sp):
            for u in range(2):
                sp.dma_start(wraw[:, u], w_all[u]).then_inc(w_loaded[u], 16)

            def pair(i, last):
                for u in range(2):
                    b = 2 * i + u
                    if not last:
                        sp.wait_ge(low_done, b + 1)
                        sp.dma_start(wraw[:, u], w_all[bass.ds(b + 2, 1)].squeeze(0)
                                     ).then_inc(w_loaded[u], 16)
                    sp.wait_ge(evac, NCH * (b + 1))
                    sp.dma_start(projT[bass.ds(b, 1)].squeeze(0), stage[:, u]).then_inc(stored[u], 16)

            with sp.Fori(0, NPAIR - 1) as i:
                pair(i, False)
            pair(NPAIR - 1, True)
            for u in range(2):
                sp.wait_ge(stored[u], 16 * NPAIR)

        @block.gpsimd
        def _(pool):
            def pair(i, first):
                for u in range(2):
                    b = 2 * i + u
                    pool.wait_ge(w_loaded[u], 16 * (i + 1))
                    if not first:
                        pool.wait_ge(evac, NCH * (b - 1))
                    pool.tensor_tensor(bias[:, u:u + 1], wraw[:, u, KT * P:], ones[:, 0:1], ALU.mult)
                    pool.tensor_tensor(wh[:, u], wraw[:, u, 0:KT * P], ones_row, ALU.mult
                                       ).then_inc(high_done, 1)
                    pool.wait_ge(high_done, b + 1)
                    pool.tensor_tensor(wl[:, u], wraw[:, u, 0:KT * P], as_f32(wh[:, u]), ALU.subtract
                                       ).then_inc(low_done, 1)

            pool.memset(ones[:], 1.0).then_inc(ones_set, 1)
            pool.wait_ge(ones_set, 1)
            pair(0, True)
            with pool.Fori(1, NPAIR) as i:
                pair(i, False)

        @block.tensor
        def _(pe):
            def pair(i, first):
                for u in range(2):
                    b = 2 * i + u
                    pe.wait_ge(low_done, b + 1)
                    for n in range(NCH):
                        if not first:
                            pe.wait_ge(evac, NCH * (b - 2) + n + 1)
                        cols = slice(n * CH, (n + 1) * CH)
                        for k in range(KT):
                            pe.matmul(acc[u][n][:], wh[:, u, k * P:(k + 1) * P], xTh[:, k, cols],
                                      start=(k == 0), stop=False)
                            pe.matmul(acc[u][n][:], wh[:, u, k * P:(k + 1) * P], xTl[:, k, cols],
                                      start=False, stop=False)
                            mm = pe.matmul(acc[u][n][:], wl[:, u, k * P:(k + 1) * P], xTh[:, k, cols],
                                           start=False, stop=(k == KT - 1))
                        mm.then_inc(product, 1)

            pair(0, True)
            with pe.Fori(1, NPAIR) as i:
                pair(i, False)

        @block.scalar
        def _(act):
            with act.Fori(B_GATE // 2, B_COPY // 2) as i:
                for u in range(2):
                    b = 2 * i + u
                    for n in range(NCH):
                        act.wait_ge(product, NCH * b + n + 1)
                        act.wait_ge(evac, NCH * b + n - 1)
                        act.activation(sig[:, n % 2], acc[u][n][:], ACT.Sigmoid).then_inc(sig_done, 1)
            with act.Fori(B_MERGE // 2, NPAIR) as i:
                for u in range(2):
                    b = 2 * i + u
                    act.wait_ge(stored[u], 16 * i)
                    for n in range(NCH):
                        act.wait_ge(product, NCH * b + n + 1)
                        act.wait_ge(evac, NCH * b + n)
                        act.activation(stage[:, u, n * CH:(n + 1) * CH], acc[u][n][:], ACT.Sigmoid,
                                       bias=bias[:, u:u + 1]).then_inc(evac, 1)

        @block.vector
        def _(dve):
            def copies(i, first):
                for u in range(2):
                    b = 2 * i + u
                    if not first:
                        dve.wait_ge(stored[u], 16 * i)
                    for n in range(NCH):
                        dve.wait_ge(product, NCH * b + n + 1)
                        dve.tensor_copy(stage[:, u, n * CH:(n + 1) * CH], acc[u][n][:]).then_inc(evac, 1)

            copies(0, True)
            with dve.Fori(1, B_GATE // 2) as i:
                copies(i, False)
            with dve.Fori(B_GATE // 2, B_COPY // 2) as i:
                for u in range(2):
                    b = 2 * i + u
                    dve.wait_ge(stored[u], 16 * i)
                    for n in range(NCH):
                        dve.wait_ge(sig_done, NCH * (b - B_GATE) + n + 1)
                        dve.tensor_tensor(stage[:, u, n * CH:(n + 1) * CH], acc[u][n][:], sig[:, n % 2],
                                          ALU.mult).then_inc(evac, 1)
            with dve.Fori(B_COPY // 2, B_MERGE // 2) as i:
                copies(i, False)


def latent_heads(nc, projT, rotary, gains, w_q, w_kv, ident, qn, qp, kn, kp, va, vb):
    QB = 8
    PLAIN = 12
    with Scope(nc) as c:
        wq_raw = c.sb("wq_raw", [P, 2, D])
        wq_h = c.sb("wq_h", [P, 2, D], F32R)
        wq_l = c.sb("wq_l", [P, 2, D], F32R)
        wkv_raw = c.sb("wkv_raw", [P, D])
        wkv_h = c.sb("wkv_h", [P, D], F32R)
        wkv_l = c.sb("wkv_l", [P, D], F32R)
        gain = c.sb("gain", [P, 3])
        eps = c.sb("eps", [P, 1])
        ones = c.sb("ones_sq", [P, P])
        lat = c.sb("lat", [P, 2, 3, CH])
        kr = c.sb("k_rope", [ROPE, 2, 2, CH])
        cs = c.sb("cos_sin", [P, 2, 2, CH])
        sq = c.sb("lat_sq", [P, 3, CH])
        rstd = c.sb("lat_rstd", [P, 2, CH])
        norm = c.sb("lat_norm", [P, 3, CH])
        norm_h = c.sb("lat_norm_h", [P, 3, CH], F32R)
        norm_l = c.sb("lat_norm_l", [P, 3, CH], F32R)
        plain = c.sb("plain_out", [P, 2, PLAIN, CH])
        rot = c.sb("rot_out", [P, 2, 2, CH])
        part = c.sb("rot_part", [P, 2, CH])
        krot = c.sb("k_rot_out", [ROPE, 2, CH])
        kpart = c.sb("k_rot_part", [ROPE, 2, CH])
        vT = c.sb("vT", [P, 2, S])
        ssq = [c.ps(f"ssq{i}", [P, CH]) for i in range(2)]
        pbank = [c.ps(f"plain_ps{i}", [P, CH]) for i in range(4)]
        rbank = [c.ps(f"rot_ps{i}", [P, CH]) for i in range(2)]
        w_loaded = c.sem("lat_w_loaded")
        consts = c.sem("lat_consts")
        w_split = c.sem("lat_w_split")
        loaded = [c.sem(f"lat_loaded{u}") for u in range(2)]
        v_loaded = [c.sem(f"vT_loaded{u}") for u in range(2)]
        sq_done = c.sem("lat_sq_done")
        ssq_done = c.sem("ssq_done")
        root_done = c.sem("root_done")
        rstd_done = c.sem("rstd_done")
        norm_done = c.sem("norm_done")
        norm_high = c.sem("norm_high")
        norm_low = c.sem("norm_low")
        plain_done = c.sem("plain_done")
        plain_out = c.sem("plain_out")
        rot_done = c.sem("rot_done")
        rot_parts = c.sem("rot_parts")
        rot_out = c.sem("rot_out")
        krot_parts = c.sem("krot_parts")
        stored = [c.sem(f"lat_stored{u}") for u in range(2)]
        v_stored = [c.sem(f"vb_stored{u}") for u in range(2)]
        block = c.block()
        NST = 5
        NV = 4
        base = NCH * PLAIN
        order = [4, 6, 5, 7]

        @block.sync
        def _(sp):
            sp.dma_start(wq_raw[:], w_q).then_inc(w_loaded, 16)
            sp.dma_start(wkv_raw[:], w_kv).then_inc(w_loaded, 16)
            sp.dma_start(gain[:], gains).then_inc(w_loaded, 16)

            def load(n):
                u, cols = n % 2, slice(n * CH, (n + 1) * CH)
                if n >= 2:
                    sp.wait_ge(norm_done, 3 * (n - 1))
                    sp.wait_ge(rot_parts, 4 * (n - 1))
                    sp.wait_ge(krot_parts, 2 * (n - 1))
                sp.dma_start(lat[:, u], projT[0:3, :, cols].rearrange("b p c -> p b c")
                             ).then_inc(loaded[u], 16)
                sp.dma_start(kr[:, u], projT[3, 0:2 * ROPE, cols].rearrange("(a p) c -> p a c", p=ROPE)
                             ).then_inc(loaded[u], 16)
                sp.dma_start(cs[:, u], rotary[:, :, cols].rearrange("a p c -> p a c")
                             ).then_inc(loaded[u], 16)

            load(0)
            load(1)
            for n in range(NCH):
                u, cols = n % 2, slice(n * CH, (n + 1) * CH)
                if n + 2 < NCH:
                    load(n + 2)
                sp.wait_ge(plain_out, PLAIN * (n + 1))
                sp.wait_ge(rot_out, 3 * (n + 1))
                for dst, src in ((qn, 0), (kn, 4)):
                    sp.dma_start(dst[:, cols].rearrange("(b p) c -> p b c", p=P),
                                 plain[:, u, src:src + 4]).then_inc(stored[u], 16)
                sp.dma_start(va[cols].rearrange("(t p) f -> p t f", p=P), plain[:, u, 8:12]
                             ).then_inc(stored[u], 16)
                sp.dma_start(qp[:, cols].rearrange("(b p) c -> p b c", p=P), rot[:, u]
                             ).then_inc(stored[u], 16)
                sp.dma_start(kp[:, cols], krot[:, u]).then_inc(stored[u], 16)
            for b in range(2):
                sp.dma_start(vT[:, b], projT[B_COPY + 8 + b]).then_inc(v_loaded[b], 16)
            for b in range(NV):
                u = b % 2
                sp.wait_ge(plain_out, base + NCH * (b + 1))
                if b + 2 < NV:
                    sp.dma_start(vT[:, u], projT[B_COPY + 10 + b]).then_inc(v_loaded[u], 16)
                sp.dma_start(vb[:, b * P:(b + 1) * P].rearrange("(t p) f -> p t f", p=P),
                             plain[:, u, 0:4].rearrange("p n (t f) -> p (n t) f", f=P)
                             ).then_inc(v_stored[u], 16)
            for u in range(2):
                sp.wait_ge(stored[u], 16 * NST * 2)
                sp.wait_ge(v_stored[u], 32)

        @block.gpsimd
        def _(pool):
            pool.memset(eps[:], RMS_EPS).then_inc(consts, 1)
            pool.memset(ones[:], 1.0).then_inc(consts, 1)
            for n in range(NCH):
                u = n % 2
                pool.wait_ge(loaded[u], 48 * (n // 2 + 1))
                if n:
                    pool.wait_ge(ssq_done, 2 * n)
                pool.tensor_tensor(sq[:], lat[:, u], lat[:, u], ALU.mult).then_inc(sq_done, 1)
                for j in range(2):
                    if n >= 2:
                        pool.wait_ge(stored[u], 16 * NST * (n // 2))
                    pool.wait_ge(rot_parts, 4 * n + 2 * j + 2)
                    pool.tensor_tensor(rot[:, u, j], rot[:, u, j], part[:, j], ALU.add
                                       ).then_inc(rot_out, 1)
                pool.wait_ge(krot_parts, 2 * (n + 1))
                pool.tensor_tensor(krot[:, u], krot[:, u], kpart[:, u], ALU.add).then_inc(rot_out, 1)

        @block.tensor
        def _(pe):
            pe.wait_ge(consts, 2)
            for n in range(NCH):
                pe.wait_ge(sq_done, n + 1)
                if n:
                    pe.wait_ge(root_done, 2 * n)
                pe.matmul(ssq[0][:], ones[:], sq[:, 0], start=True, stop=False)
                pe.matmul(ssq[0][:], ones[:], sq[:, 1], start=False, stop=True).then_inc(ssq_done, 1)
                pe.matmul(ssq[1][:], ones[:], sq[:, 2], start=True, stop=True).then_inc(ssq_done, 1)
                pe.wait_ge(w_split, 2)
                pe.wait_ge(norm_low, 3 * (n + 1))

                def up(bank, pairs, done):
                    last = 3 * len(pairs) - 1
                    at = 0
                    for (ah, al), (bh, bl) in pairs:
                        for a, b in ((ah, bh), (ah, bl), (al, bh)):
                            mm = pe.matmul(bank, a, b, start=(at == 0), stop=(at == last))
                            at += 1
                    mm.then_inc(done, 1)

                for j in range(PLAIN):
                    r = n * PLAIN + j
                    if r >= 4:
                        pe.wait_ge(plain_out, r - 3)
                    cols = slice((j % 4) * P, (j % 4 + 1) * P)
                    if j < 4:
                        pairs = [((wq_h[:, k, cols], wq_l[:, k, cols]), (norm_h[:, k], norm_l[:, k]))
                                 for k in range(2)]
                    elif j < 8:
                        pairs = [((wkv_h[:, cols], wkv_l[:, cols]), (norm_h[:, 2], norm_l[:, 2]))]
                    else:
                        pairs = [((norm_h[:, 2, cols], norm_l[:, 2, cols]), (wkv_h[:, CH:], wkv_l[:, CH:]))]
                    up(pbank[r % 4][:], pairs, plain_done)
                    if j % 3 == 2:
                        m = j // 3
                        if n or m >= 2:
                            pe.wait_ge(rot_parts, 4 * n + m - 1)
                        cols = slice(order[m] * P, (order[m] + 1) * P)
                        pairs = [((wq_h[:, k, cols], wq_l[:, k, cols]), (norm_h[:, k], norm_l[:, k]))
                                 for k in range(2)]
                        up(rbank[m % 2][:], pairs, rot_done)
            for b in range(NV):
                pe.wait_ge(v_loaded[b % 2], 16 * (b // 2 + 1))
                for n in range(NCH):
                    r = base + NCH * b + n
                    pe.wait_ge(plain_out, r - 3)
                    for t in range(4):
                        at = (4 * n + t) * P
                        mm = pe.transpose(pbank[r % 4][:, t * P:(t + 1) * P], vT[:, b % 2, at:at + P],
                                          ident[:])
                    mm.then_inc(plain_done, 1)

        @block.scalar
        def _(act):
            act.wait_ge(w_loaded, 48)
            act.activation(wq_h[:], wq_raw[:], ACT.Copy).then_inc(norm_high, 1)
            act.activation(wkv_h[:], wkv_raw[:], ACT.Copy).then_inc(norm_high, 1)
            act.wait_ge(consts, 2)
            for n in range(NCH):
                u = n % 2
                if n:
                    act.wait_ge(norm_done, 3 * n)
                for j, width in ((0, QL), (1, KVL)):
                    act.wait_ge(ssq_done, 2 * n + j + 1)
                    act.activation(rstd[:, j], ssq[j][:], ACT.Sqrt, bias=eps[:, 0:1], scale=1.0 / width
                                   ).then_inc(root_done, 1)
                for k in range(3):
                    act.wait_ge(norm_done, 3 * n + k + 1)
                    if n:
                        act.wait_ge(plain_done, PLAIN * n)
                        act.wait_ge(rot_done, 4 * n)
                    act.activation(norm_h[:, k], norm[:, k], ACT.Copy).then_inc(norm_high, 1)
                if n >= 2:
                    act.wait_ge(stored[u], 16 * NST * (n // 2))
                for j in range(PLAIN):
                    r = n * PLAIN + j
                    act.wait_ge(plain_done, r + 1)
                    act.activation(plain[:, u, j], pbank[r % 4][:], ACT.Copy).then_inc(plain_out, 1)
            for b in range(NV):
                if b >= 2:
                    act.wait_ge(v_stored[b % 2], 16)
                else:
                    act.wait_ge(stored[b], 32 * NST)
                for n in range(NCH):
                    r = base + NCH * b + n
                    act.wait_ge(plain_done, r + 1)
                    act.activation(plain[:, b % 2, n], pbank[r % 4][:], ACT.Copy).then_inc(plain_out, 1)

        @block.vector
        def _(dve):
            dve.wait_ge(norm_high, 2)
            dve.tensor_tensor(wq_l[:], wq_raw[:], as_f32(wq_h[:]), ALU.subtract).then_inc(w_split, 1)
            dve.tensor_tensor(wkv_l[:], wkv_raw[:], as_f32(wkv_h[:]), ALU.subtract).then_inc(w_split, 1)
            for n in range(NCH):
                u = n % 2
                dve.wait_ge(root_done, 2 * (n + 1))
                dve.reciprocal(rstd[:], rstd[:]).then_inc(rstd_done, 1)
                dve.wait_ge(loaded[u], 48 * (n // 2 + 1))
                dve.wait_ge(rstd_done, n + 1)
                if n:
                    dve.wait_ge(norm_high, 2 + 3 * n)
                for k in range(3):
                    dve.scalar_tensor_tensor(out=norm[:, k], in0=lat[:, u, k], scalar=gain[:, k:k + 1],
                                             in1=rstd[:, k // 2], op0=ALU.mult, op1=ALU.mult
                                             ).then_inc(norm_done, 1)
                for k in range(3):
                    dve.wait_ge(norm_high, 2 + 3 * n + k + 1)
                    dve.tensor_tensor(norm_l[:, k], norm[:, k], as_f32(norm_h[:, k]), ALU.subtract
                                      ).then_inc(norm_low, 1)
                if n >= 2:
                    dve.wait_ge(stored[u], 16 * NST * (n // 2))
                if n:
                    dve.wait_ge(rot_out, 3 * n)
                dve.tensor_tensor(krot[:, u], kr[:, u, 0], cs[0:ROPE, u, 0], ALU.mult
                                  ).then_inc(krot_parts, 1)
                dve.tensor_tensor(kpart[:, u], kr[:, u, 1], cs[0:ROPE, u, 1], ALU.mult
                                  ).then_inc(krot_parts, 1)
                for m in range(4):
                    dve.wait_ge(rot_done, 4 * n + m + 1)
                    dst = part[:, m // 2] if m % 2 else rot[:, u, m // 2]
                    dve.tensor_tensor(dst, rbank[m % 2][:], cs[:, u, m % 2], ALU.mult
                                      ).then_inc(rot_parts, 1)


ORDER = [1, 3, 2, 0]
START = [sum(4 * (g + 1) for g in ORDER[:o]) for o in range(4)]
PER_HEAD = sum(4 * (g + 1) for g in ORDER)
RING = 4
PIECES = 12
HEAD = 64


def attend(nc, soft, q_src, k_src, v_src, projT, gate_block, ogT, ident):
    scale = float(NOPE + ROPE) ** -0.5 if soft else float(SBD) ** -0.5
    rows = NOPE + ROPE if soft else P
    loads = 5
    items = PER_HEAD + 4 if soft else PER_HEAD
    per_pos = [4 * (g + 1) + (1 if soft else 0) for g in ORDER]
    item_at = [sum(per_pos[:o]) for o in range(4)]

    with Scope(nc) as c:
        n = "mla_" if soft else "sb_"
        q_raw = c.sb(n + "q_raw", [rows, S])
        k_raw = c.sb(n + "k_raw", [rows, S])
        v_raw = c.sb(n + "v_raw", [P, TT, HEAD])
        q_hi = [c.sb(n + f"q_hi{u}", [rows, S], F32R) for u in range(2)]
        q_lo = [c.sb(n + f"q_lo{u}", [rows, S], F32R) for u in range(2)] if soft else None
        k_hi = [c.sb(n + f"k_hi{u}", [rows, S], F32R) for u in range(2)]
        k_lo = [c.sb(n + f"k_lo{u}", [rows, S], F32R) for u in range(2)]
        v_two = [c.sb(n + f"v_two{u}", [P, TT, 2 * HEAD], F32R) for u in range(2)]
        w = [c.sb(n + "w_even", [P, 4, 3 * CH]), c.sb(n + "w_odd", [P, 4, 4 * CH])]
        wT_hi = [c.sb(n + f"wT_hi{b}", [P, CH], F32R) for b in range(2)]
        wT_lo = [c.sb(n + f"wT_lo{b}", [P, CH], F32R) for b in range(2)]
        gate = c.sb(n + "gate", [HEAD, 2, CH])
        o_low = c.sb(n + "o_low", [HEAD, 2, CH])
        o_sum = c.sb(n + "o_sum", [HEAD, 2, CH])
        og = c.sb(n + "og", [HEAD, 2, CH])
        mask = c.sb(n + "mask", [P, P])
        ones = c.sb(n + "ones", [P, P])
        if soft:
            maxes = c.sb(n + "maxes", [P, 16, 4])
            neg_max = c.sb(n + "neg_max", [P, 16])
            sums = c.sb(n + "sums", [P, 16])
            top = c.sb(n + "top", [P, 16])
            inv_sum = c.sb(n + "inv_sum", [P, 16])
            diag = c.sb(n + "diag", [P, 4, P])
            gate_n = c.sb(n + "gate_n", [HEAD, 2, CH])
        else:
            keep = c.sb(n + "keep", [P, RING, CH])
            after = c.sb(n + "after", [P, 2, S + 1])
        score = [c.ps(n + f"score{b}", [P, CH]) for b in range(RING)]
        turn = [c.ps(n + f"turn{b}", [P, CH]) for b in range(2)]
        o_ps = [c.ps(n + f"o_ps{b}", [P, CH]) for b in range(2)]

        consts = c.sem(n + "consts")
        raw_loaded = c.sem(n + "raw_loaded")
        split_high = c.sem(n + "split_high")
        split = c.sem(n + "split")
        scored = c.sem(n + "scored")
        masked = c.sem(n + "masked")
        top_done = c.sem(n + "top_done")
        shift_ready = c.sem(n + "shift_ready")
        freed = c.sem(n + "freed")
        scanned = c.sem(n + "scanned")
        weighted = c.sem(n + "weighted")
        exp_done = c.sem(n + "exp_done")
        inverted = c.sem(n + "inverted")
        diag_ready = c.sem(n + "diag_ready")
        turned = c.sem(n + "turned")
        turn_high = c.sem(n + "turn_high")
        turn_freed = c.sem(n + "turn_freed")
        pv_done = c.sem(n + "pv_done")
        low_copied = c.sem(n + "low_copied")
        o_summed = c.sem(n + "o_summed")
        gated = c.sem(n + "gated")
        gate_loaded = [c.sem(n + f"gate_loaded{b}") for b in range(2)]
        stored = [c.sem(n + f"og_stored{b}") for b in range(2)]
        passed = c.sem(n + "passed")
        block = c.block()

        def weights_ready(h, o):
            return (exp_done, 16 * h + 4 * o + 4) if soft else (weighted, 2 + number(h, o, 3, ORDER[o] + 1))

        def heads(engine, body):
            with engine.Fori(0, H // 2 - 1) as i:
                body(i, 0, False)
                body(i, 1, False)
            body(H // 2 - 1, 0, False)
            body(H // 2 - 1, 1, True)

        def chunks(g, t):
            both = [(k, CH if k < g else (t + 1) * P) for k in range(g + 1)]
            return both if soft else both[::-1]

        def schedule(o, nxt):
            tiles = [("tile", j) for j in range(4 * (ORDER[o] + 1))] + ([("sums",)] if soft else [])
            if not nxt:
                return tiles
            g = ORDER[nxt[2]]
            new = [("chunk", t, j, k, width) for t in range(4) for j, (k, width) in enumerate(chunks(g, t))]
            total = len(tiles) + len(new)
            mixed, a, b = [], 0, 0
            for _ in range(total):
                if b < len(new) and (a == len(tiles) or b * len(tiles) <= a * len(new)):
                    mixed.append(new[b])
                    b += 1
                else:
                    mixed.append(tiles[a])
                    a += 1
            return mixed

        def all_chunks(o):
            return [(t, j, k, width) for t in range(4) for j, (k, width) in enumerate(chunks(ORDER[o], t))]

        def number(h, o, t, j=0):
            return PER_HEAD * h + START[o] + t * (ORDER[o] + 1) + j

        def following(h, u, o, last):
            if o < 3:
                return h, u, o + 1
            return None if last else (h + 1, 1 - u, 0)

        @block.sync
        def _(sp):
            def load_operands(h):
                if soft:
                    sp.dma_start(q_raw[0:NOPE], q_src[0][bass.ds(h * NOPE, NOPE)]).then_inc(raw_loaded, 16)
                    sp.dma_start(q_raw[NOPE:], q_src[1][bass.ds(h * ROPE, ROPE)]).then_inc(raw_loaded, 16)
                    sp.dma_start(k_raw[0:NOPE], k_src[0][bass.ds(h * NOPE, NOPE)]).then_inc(raw_loaded, 16)
                    sp.dma_start(k_raw[NOPE:], k_src[1]).then_inc(raw_loaded, 16)
                else:
                    for half in range(2):
                        part = slice(half * SBD, (half + 1) * SBD)
                        sp.dma_start(q_raw[part], q_src[bass.ds(h * SBD, SBD)]).then_inc(raw_loaded, 16)
                        sp.dma_start(k_raw[part], k_src[bass.ds(h * SBD, SBD)]).then_inc(raw_loaded, 16)
                sp.dma_start(v_raw[:], v_src[:, bass.ds(h * HEAD, HEAD)].rearrange("(t p) f -> p t f", p=P)
                             ).then_inc(raw_loaded, 16)

            def load_gate(i, u, o):
                g = ORDER[o]
                sp.wait_ge(gated, 4 * (2 * i + u) + o + 1)
                sp.sem_inc(passed, 1)
                sp.dma_start(gate[:, o % 2],
                             projT[bass.ds(gate_block + i, 1), u * HEAD:(u + 1) * HEAD, g * CH:(g + 1) * CH
                                   ].squeeze(0)).then_inc(gate_loaded[o % 2], 16)

            def body(i, u, last):
                h = 2 * i + u
                for o in range(4):
                    g = ORDER[o]
                    nxt = following(h, u, o, last)
                    if nxt:
                        load_gate(i + int(o == 3 and u == 1), nxt[1], nxt[2])
                    sp.wait_ge(gated, 2 + 4 * h + o + 1)
                    sp.sem_inc(passed, 1)
                    sp.dma_start(ogT[bass.ds(h * HEAD, HEAD), g * CH:(g + 1) * CH], og[:, o % 2]
                                 ).then_inc(stored[o % 2], 16)
                    if o == 2 and not last and not (isinstance(i, int) and u == 0):
                        sp.wait_ge(split, PIECES * (h + 2))
                        sp.sem_inc(passed, 1)
                        load_operands(h + 2)

            for b in range(2):
                sp.sem_inc(stored[b], 16)
            load_operands(0)
            load_gate(0, 0, 0)
            sp.wait_ge(split, PIECES)
            load_operands(1)
            heads(sp, body)
            for b in range(2):
                sp.wait_ge(stored[b], 16 + 16 * 2 * H)

        @block.gpsimd
        def _(pool):
            pool.sem_inc(weighted, 2)
            pool.sem_inc(gated, 2)
            pool.memset(mask[:], BIG).then_inc(consts, 1)
            pool.memset(ones[:], 1.0).then_inc(consts, 1)
            if not soft:
                pool.memset(after[:, :, S:S + 1], 1.0).then_inc(consts, 1)
            pool.wait_ge(consts, 2 if soft else 3)
            pool.affine_select(out=mask[:], in_=mask[:], compare_op=ALU.is_ge if soft else ALU.is_gt,
                               fill=-BIG, base=0, pattern=[[-1, P]], channel_multiplier=1
                               ).then_inc(consts, 1)

            def split_piece(h, u, p):
                if p < 8:
                    cols = slice(p // 2 * CH, (p // 2 + 1) * CH)
                    raw, hi, lo, part = ((q_raw, q_hi, q_lo, slice(None)), (k_raw, k_hi, k_lo, slice(None))
                                         )[p % 2]
                    src, high = raw[:, cols], hi[u][:, cols]
                    if lo is None:
                        src_l, high_l, low = raw[SBD:, cols], hi[u][SBD:, cols], hi[u][SBD:, cols]
                    else:
                        src_l, high_l, low = src, high, lo[u][:, cols]
                else:
                    tiles = slice((p - 8) * 4, (p - 7) * 4)
                    src = src_l = v_raw[:, tiles]
                    high = high_l = v_two[u][:, tiles, 0:HEAD]
                    low = v_two[u][:, tiles, HEAD:]
                one = ones[0:src.shape[0], 0:1]
                if p < 8:
                    one = one.broadcast_to([src.shape[0], CH])
                else:
                    one = one.unsqueeze(2).broadcast_to([P, 4, HEAD])
                pool.tensor_tensor(high, src, one, ALU.mult).then_inc(split_high, 1)
                pool.wait_ge(split_high, PIECES * h + p + 1)
                pool.tensor_tensor(low, src_l, as_f32(high_l), ALU.subtract).then_inc(split, 1)
                if p < 8 and src_l is not src:
                    pool.wait_ge(split, PIECES * h + p + 1)

            def weigh(h, o, t, j, k, width):
                at, off = k * CH, S - (4 * ORDER[o] + t + 1) * P
                pool.wait_ge(scanned, RING + number(h, o, t, j) + 1)
                pool.tensor_tensor(w[o % 2][:, t, at:at + width], w[o % 2][:, t, at:at + width],
                                   after[:, t % 2, off + at + 1:off + at + width + 1], ALU.mult
                                   ).then_inc(weighted, 1)

            def body(i, u, last):
                h = 2 * i + u
                for o in range(4):
                    nxt = following(h, u, o, last)

                    def pieces(t):
                        if o < 3 and not last:
                            p = 4 * o + t
                            if p == 0:
                                pool.wait_ge(raw_loaded, 16 * loads * (h + 2))
                                pool.wait_ge(scored, number(h, 0, 3, ORDER[0] + 1))
                            if p == 8:
                                pool.wait_ge(pv_done, PER_HEAD * h + 2)
                            split_piece(h + 1, 1 - u, p)

                    if soft:
                        for t in range(4):
                            if t == 1:
                                for tt in range(4):
                                    pool.wait_ge(inverted, 4 * h + o + 1)
                                    pool.wait_ge(turned, items * h + item_at[o] + 1)
                                    at = 4 * o + tt
                                    pool.tensor_tensor(diag[:, tt], ident[:],
                                                       inv_sum[:, at:at + 1].broadcast_to([P, P]), ALU.mult
                                                       ).then_inc(diag_ready, 1)
                            pieces(t)
                    else:
                        new = all_chunks(nxt[2]) if nxt else []
                        quarter = len(new) // 4
                        for t in range(4):
                            pieces(t)
                            for it in new[t * quarter:(t + 1) * quarter]:
                                weigh(nxt[0], nxt[2], *it)
                    seq = 4 * h + o
                    pool.wait_ge(stored[o % 2], 16 * (2 * h + o // 2 + 1))
                    if soft:
                        pool.wait_ge(turn_freed, 2 + items * h + item_at[o] + per_pos[o])
                    else:
                        pool.wait_ge(gate_loaded[o % 2], 16 * (2 * h + o // 2 + 1))
                    pool.wait_ge(o_summed, 2 + seq + 1)
                    by = gate_n if soft else gate
                    pool.tensor_tensor(og[:, o % 2], o_sum[:, o % 2], by[:, o % 2], ALU.mult
                                       ).then_inc(gated, 1)

            pool.wait_ge(raw_loaded, 16 * loads)
            for p in range(PIECES):
                split_piece(0, 0, p)
            if not soft:
                for it in all_chunks(0):
                    weigh(0, 0, *it)
            heads(pool, body)

        @block.tensor
        def _(pe):
            pe.sem_inc(pv_done, 2)
            pe.wait_ge(consts, 3 if soft else 4)

            def scores(h, u, o, t, j, key, width):
                g = ORDER[o]
                q_cols = slice((4 * g + t) * P, (4 * g + t + 1) * P)
                if t == 0 and j == 0 and o == 0:
                    pe.wait_ge(split, PIECES * (h + 1))
                pe.wait_ge(freed, number(h, o, t, j) + 1)
                bank = score[number(0, o, t, j) % RING][:, 0:width]
                keys = slice(key * CH, key * CH + width)
                if soft:
                    passes = [(q_hi, k_hi), (q_hi, k_lo), (q_lo, k_hi)]
                else:
                    passes = [(q_hi, k_hi), (q_hi, k_lo)]
                for m, (a, b) in enumerate(passes):
                    mm = pe.matmul(bank, a[u][:, q_cols], b[u][:, keys], start=(m == 0),
                                   stop=(m == len(passes) - 1))
                mm.then_inc(scored, 1)

            def times_v(h, u, o, j):
                g = ORDER[o]
                seq = PER_HEAD * h + START[o] + j
                b = (START[o] + j) % 2
                first = max(0, j - 4 * g) * P
                pe.wait_ge(turn_freed, 2 + items * h + item_at[o] + j + 1)
                if j == 0:
                    pe.wait_ge(o_summed, 4 * h + o + 1)
                for m, part in enumerate((wT_hi, wT_lo)):
                    mm = pe.matmul(o_ps[o % 2][:, first:], v_two[u][:, j], part[b][:, first:],
                                   start=(j == 0 and m == 0), stop=(j == 4 * g + 3 and m == 1))
                mm.then_inc(pv_done, 1)

            def body(i, u, last):
                h = 2 * i + u
                for o in range(4):
                    g = ORDER[o]
                    nxt = following(h, u, o, last)
                    for what in schedule(o, nxt):
                        if what[0] == "chunk":
                            scores(nxt[0], nxt[1], nxt[2], *what[1:])
                            continue
                        if what[0] == "sums":
                            it = item_at[o] + 4 * (g + 1)
                            pe.wait_ge(turn_freed, items * h + it + 1)
                            pe.wait_ge(diag_ready, 16 * h + 4 * o + 4)
                            for tt in range(4):
                                mm = pe.matmul(turn[it % 2][:, tt * P:(tt + 1) * P], ones[:], diag[:, tt],
                                               start=True, stop=True)
                            mm.then_inc(turned, 1)
                            continue
                        j = what[1]
                        it = item_at[o] + j
                        if j == 0:
                            pe.wait_ge(*weights_ready(h, o))
                        pe.wait_ge(turn_freed, items * h + it + 1)
                        for tt in range(max(0, j - 4 * g), 4):
                            mm = pe.transpose(turn[it % 2][:, tt * P:(tt + 1) * P],
                                              w[o % 2][:, tt, j * P:(j + 1) * P], ident[:])
                        mm.then_inc(turned, 1)
                        if j:
                            times_v(h, u, o, j - 1)
                    times_v(h, u, o, 4 * g + 3)

            for it in all_chunks(0):
                scores(0, 0, 0, *it)
            heads(pe, body)

        @block.scalar
        def _(act):
            if not soft:
                act.sem_inc(freed, RING)

            def weights(h, o, t, j, key, width):
                g, pos = ORDER[o], 4 * o + t
                if soft:
                    if j == g:
                        row = w[o % 2][:, t, 0:(4 * g + t + 1) * P]
                        act.wait_ge(shift_ready, 16 * h + pos + 1)
                        act.activation(row, row, ACT.Exp, scale=scale, bias=neg_max[:, pos:pos + 1],
                                       accum_out=sums[:, pos:pos + 1]).then_inc(exp_done, 1)
                    return
                if key == g:
                    act.wait_ge(masked, 16 * h + pos + 1)
                else:
                    act.wait_ge(scored, number(h, o, t, j) + 1)
                act.wait_ge(scanned, number(h, o, t, j) + 1)
                r = number(0, o, t, j) % RING
                bank = score[r][:, 0:width]
                act.activation(keep[:, r, 0:width], bank, ACT.Sigmoid, scale=-scale)
                act.activation(w[o % 2][:, t, key * CH:key * CH + width], bank, ACT.Sigmoid, scale=scale
                               ).then_inc(freed, 1)

            def body(i, u, last):
                h = 2 * i + u
                for o in range(4):
                    g = ORDER[o]
                    nxt = following(h, u, o, last)
                    for what in schedule(o, nxt):
                        if what[0] == "chunk":
                            weights(nxt[0], nxt[2], *what[1:])
                        if what[0] == "tile":
                            j = what[1]
                            it, b = item_at[o] + j, (START[o] + j) % 2
                            first = max(0, j - 4 * g) * P
                            act.wait_ge(turned, items * h + it + 1)
                            act.wait_ge(pv_done, PER_HEAD * h + START[o] + j + 1)
                            act.activation(wT_hi[b][:, first:], turn[it % 2][:, first:], ACT.Copy
                                           ).then_inc(turn_high, 1)
                    act.wait_ge(pv_done, 2 + PER_HEAD * h + START[o] + 4 * (g + 1))
                    act.activation(o_low[:, o % 2], o_ps[o % 2][HEAD:], ACT.Copy).then_inc(low_copied, 1)

            for it in all_chunks(0):
                weights(0, 0, *it)
            heads(act, body)

        @block.vector
        def _(dve):
            dve.sem_inc(turn_freed, 2)
            dve.sem_inc(o_summed, 2)
            if not soft:
                dve.sem_inc(scanned, RING)
            dve.wait_ge(consts, 3 if soft else 4)

            def after_scores(h, o, t, j, key, width):
                g, pos = ORDER[o], 4 * o + t
                bank = score[number(0, o, t, j) % RING]
                dve.wait_ge(scored, number(h, o, t, j) + 1)
                if key == g:
                    diagonal = bank[:, t * P:(t + 1) * P]
                    dve.tensor_tensor(diagonal, diagonal, mask[:], ALU.min).then_inc(masked, 1)
                if soft:
                    if key == g:
                        dve.wait_ge(masked, 16 * h + pos + 1)
                    dve.tensor_scalar(w[o % 2][:, t, key * CH:key * CH + width], bank[:, 0:width], 1.0, None,
                                      ALU.mult, ALU.max, accum_out=maxes[:, pos, key:key + 1]
                                      ).then_inc(freed, 1)
                    if key == g:
                        dve.wait_ge(freed, RING + number(h, o, t, g + 1))
                        dve.tensor_reduce(top[:, pos:pos + 1], maxes[:, pos, 0:g + 1], AX_X, ALU.max
                                          ).then_inc(top_done, 1)
                        dve.wait_ge(top_done, 16 * h + pos + 1)
                        dve.tensor_scalar(neg_max[:, pos:pos + 1], top[:, pos:pos + 1], -scale, None,
                                          ALU.mult).then_inc(shift_ready, 1)

            def scan(h, o, t, j, key, width):
                g = ORDER[o]
                off = S - (4 * g + t + 1) * P
                r = number(0, o, t, j) % RING
                dve.wait_ge(freed, RING + number(h, o, t, j) + 1)
                if j == 0:
                    prev = number(h, o, t - 2) if t >= 2 else (
                        number(h, o - 1, t + 2) if o else number(h, 0, 0) - (2 - t) * (ORDER[3] + 1))
                    size = ORDER[o if t >= 2 else o - 1] + 1
                    dve.wait_ge(weighted, 2 + prev + size)
                else:
                    dve.wait_ge(scanned, RING + number(h, o, t, j))
                at = off + key * CH
                dve.tensor_tensor_scan(after[:, t % 2, at:at + width][:, ::-1], keep[:, r, 0:width][:, ::-1],
                                       keep[:, r, 0:width][:, ::-1],
                                       after[:, t % 2, at + width:at + width + 1], ALU.mult, ALU.bypass
                                       ).then_inc(scanned, 1)

            def body(i, u, last):
                h = 2 * i + u
                for o in range(4):
                    g = ORDER[o]
                    nxt = following(h, u, o, last)
                    seq = 4 * h + o
                    behind = []
                    for what in schedule(o, nxt):
                        if what[0] == "chunk":
                            after_scores(nxt[0], nxt[2], *what[1:])
                            if not soft:
                                behind.append(what[1:])
                                if len(behind) == 2:
                                    scan(nxt[0], nxt[2], *behind.pop(0))
                        if what[0] == "tile":
                            j = what[1]
                            it, b = item_at[o] + j, (START[o] + j) % 2
                            first = max(0, j - 4 * g) * P
                            dve.wait_ge(turn_high, PER_HEAD * h + START[o] + j + 1)
                            dve.tensor_tensor(wT_lo[b][:, first:], turn[it % 2][:, first:],
                                              as_f32(wT_hi[b][:, first:]), ALU.subtract
                                              ).then_inc(turn_freed, 1)
                            if soft and j == 0:
                                at = 4 * o
                                dve.wait_ge(*weights_ready(h, o))
                                dve.reciprocal(inv_sum[:, at:at + 4], sums[:, at:at + 4]).then_inc(inverted, 1)
                        if what[0] == "sums":
                            it = item_at[o] + 4 * (g + 1)
                            dve.wait_ge(gate_loaded[o % 2], 16 * (2 * h + o // 2 + 1))
                            dve.wait_ge(gated, seq + 1)
                            dve.wait_ge(turned, items * h + it + 1)
                            dve.tensor_tensor(gate_n[:, o % 2], turn[it % 2][0:HEAD], gate[:, o % 2],
                                              ALU.mult).then_inc(turn_freed, 1)
                    for it in behind:
                        scan(nxt[0], nxt[2], *it)
                    dve.wait_ge(low_copied, seq + 1)
                    dve.wait_ge(gated, seq + 1)
                    dve.tensor_tensor(o_sum[:, o % 2], o_ps[o % 2][0:HEAD], o_low[:, o % 2], ALU.add
                                      ).then_inc(o_summed, 1)

            if soft:
                dve.sem_inc(freed, RING)
            for it in all_chunks(0):
                after_scores(0, 0, *it)
                if not soft:
                    scan(0, 0, *it)
            heads(dve, body)


def attend_memory(nc, mem, w_mem, projT, ogT, ident):
    scale = float(MD) ** -0.5
    ITEMS = MT + 1
    with Scope(nc) as c:
        mem_raw = c.sb("mem_raw", [P, MT, D])
        memT_hi = c.sb("memT_hi", [P, KT, MEM], F32R)
        memT_lo = c.sb("memT_lo", [P, KT, MEM], F32R)
        w_raw = c.sb("wm_raw", [P, 2, D])
        w_hi = c.sb("wm_hi", [P, KT, D], F32R)
        w_lo = c.sb("wm_lo", [P, KT, D], F32R)
        k_hi = c.sb("mem_k_hi", [P, MH, MEM], F32R)
        k_lo = c.sb("mem_k_lo", [P, MH, MEM], F32R)
        v_hi = c.sb("mem_v_hi", [P, MT, MH * MD], F32R)
        v_lo = c.sb("mem_v_lo", [P, MT, MH * MD], F32R)
        q_raw = c.sb("mem_q_raw", [P, 2, CH])
        q_hi = [c.sb(f"mem_q_hi{b}", [P, CH], F32R) for b in range(2)]
        q_lo = [c.sb(f"mem_q_lo{b}", [P, CH], F32R) for b in range(2)]
        gate = c.sb("mem_gate", [P, 2, CH])
        w = c.sb("mem_w", [P, 2, 4, MEM])
        wT_hi = [c.sb(f"mem_wT_hi{b}", [P, CH], F32R) for b in range(2)]
        wT_lo = [c.sb(f"mem_wT_lo{b}", [P, CH], F32R) for b in range(2)]
        top = c.sb("mem_top", [P, 2, 4])
        neg_max = c.sb("mem_neg_max", [P, 2, 4])
        sums = c.sb("mem_sums", [P, 2, 4])
        inv_sum = c.sb("mem_inv_sum", [P, 2, 4])
        diag = c.sb("mem_diag", [P, 2, 4, P])
        gate_n = c.sb("mem_gate_n", [P, 2, CH])
        og = c.sb("mem_og", [P, 2, CH])
        ones = c.sb("mem_ones", [P, P])
        score = [c.ps(f"mem_score{b}", [P, 2, 2, MEM]) for b in range(2)]
        turn = [c.ps(f"mem_turn{b}", [P, CH]) for b in range(2)]
        o_ps = [c.ps(f"mem_o{b}", [P, CH]) for b in range(2)]

        mem_loaded = c.sem("mem_loaded")
        wm_loaded = [c.sem(f"wm_loaded{b}") for b in range(2)]
        ones_set = c.sem("mem_ones_set")
        wm_high = c.sem("wm_high")
        wm_low = c.sem("wm_low")
        mem_turned = c.sem("mem_turned")
        mem_high = c.sem("mem_high")
        mem_low = c.sem("mem_low")
        kv_done = c.sem("mem_kv_done")
        kv_high = c.sem("mem_kv_high")
        kv_low = c.sem("mem_kv_low")
        q_loaded = [c.sem(f"mem_q_loaded{b}") for b in range(2)]
        gate_loaded = [c.sem(f"mem_gate_loaded{b}") for b in range(2)]
        q_high = c.sem("mem_q_high")
        q_split = c.sem("mem_q_split")
        scored = c.sem("mem_scored")
        top_done = c.sem("mem_top_done")
        shift_ready = c.sem("mem_shift_ready")
        exp_done = c.sem("mem_exp_done")
        inverted = c.sem("mem_inverted")
        diag_ready = c.sem("mem_diag_ready")
        turned = c.sem("mem_item_turned")
        turn_high = c.sem("mem_turn_high")
        turn_freed = c.sem("mem_turn_freed")
        pv_done = c.sem("mem_pv_done")
        gated = c.sem("mem_gated")
        stored = [c.sem(f"mem_stored{b}") for b in range(2)]
        passed = c.sem("mem_passed")
        block = c.block()

        prep = [turn[0], turn[1], o_ps[0], o_ps[1]]
        NPREP = KT // 2

        def chunks_of(engine, body):
            with engine.Fori(0, NCH - 1) as n:
                body(n, False)
            body(NCH - 1, True)

        def following(n, h, last):
            if h < MH - 1:
                return n, h + 1
            return None if last else (n + 1, 0)

        @block.sync
        def _(sp):
            sp.dma_start(mem_raw[:], mem.rearrange("b (t p) d -> p (b t) d", p=P)).then_inc(mem_loaded, 16)
            for k in range(KT):
                if k >= 2:
                    sp.wait_ge(wm_low, k - 1)
                sp.dma_start(w_raw[:, k % 2], w_mem[k]).then_inc(wm_loaded[k % 2], 16)
            for b in range(2):
                sp.sem_inc(stored[b], 16)

            def load(n, h):
                cols = bass.ds(n * CH, CH)
                sp.wait_ge(gated, MH * n + h + 1)
                sp.sem_inc(passed, 1)
                sp.dma_start(q_raw[:, h % 2], projT[B_COPY + 12 + h, :, cols]).then_inc(q_loaded[h % 2], 16)
                sp.dma_start(gate[:, h % 2], projT[B_GATE + 8 + h, :, cols]).then_inc(gate_loaded[h % 2], 16)

            def body(n, last):
                for h in range(MH):
                    nxt = following(n, h, last)
                    if nxt:
                        load(*nxt)
                    sp.wait_ge(gated, 2 + MH * n + h + 1)
                    sp.sem_inc(passed, 1)
                    sp.dma_start(ogT[h * MD:(h + 1) * MD, bass.ds(n * CH, CH)], og[:, h % 2]
                                 ).then_inc(stored[h % 2], 16)

            load(0, 0)
            chunks_of(sp, body)
            for b in range(2):
                sp.wait_ge(stored[b], 16 + 16 * NCH * MH // 2)

        @block.gpsimd
        def _(pool):
            pool.memset(ones[:], 1.0).then_inc(ones_set, 1)
            pool.wait_ge(ones_set, 1)

            def split_q(n, h):
                b = h % 2
                pool.wait_ge(q_loaded[b], 16 * (2 * n + h // 2 + 1))
                pool.tensor_tensor(q_hi[b][:], q_raw[:, b], ones[:, 0:1].broadcast_to([P, CH]), ALU.mult
                                   ).then_inc(q_high, 1)
                pool.wait_ge(q_high, MH * n + h + 1)
                pool.tensor_tensor(q_lo[b][:], q_raw[:, b], as_f32(q_hi[b][:]), ALU.subtract
                                   ).then_inc(q_split, 1)

            def body(n, last):
                for h in range(MH):
                    b, unit = h % 2, MH * n + h
                    nxt = following(n, h, last)
                    if nxt:
                        split_q(*nxt)
                    for t in range(4):
                        pool.wait_ge(inverted, unit + 1)
                        pool.tensor_tensor(diag[:, b, t], ident[:],
                                           inv_sum[:, b, t:t + 1].broadcast_to([P, P]), ALU.mult
                                           ).then_inc(diag_ready, 1)

            split_q(0, 0)
            chunks_of(pool, body)

        @block.tensor
        def _(pe):
            pe.sem_inc(pv_done, 2)
            pe.wait_ge(mem_loaded, 16)
            for m in range(NPREP):
                for j in range(2):
                    for t in range(MT):
                        at = (2 * j + t) * P
                        k = 2 * m + j
                        mm = pe.transpose(prep[m][:, at:at + P], mem_raw[:, t, k * P:(k + 1) * P], ident[:])
                mm.then_inc(mem_turned, 1)
            for m in range(MH + MT):
                bank = prep[m % 4][:]
                if m < 4:
                    pe.wait_ge(mem_low, m + 1)
                    bank = bank[:, 0:MEM]
                else:
                    pe.wait_ge(kv_low, m - 3)
                for k in range(KT):
                    if m == 0:
                        pe.wait_ge(mem_low, k // 2 + 1)
                        pe.wait_ge(wm_low, k + 1)
                    if m < MH:
                        cols = slice(m * MD, (m + 1) * MD)
                        a, b = (w_hi[:, k, cols], w_lo[:, k, cols]), (memT_hi[:, k], memT_lo[:, k])
                    else:
                        rows, cols = slice((m - MH) * P, (m - MH + 1) * P), slice(MH * MD, D)
                        a = memT_hi[:, k, rows], memT_lo[:, k, rows]
                        b = w_hi[:, k, cols], w_lo[:, k, cols]
                    pe.matmul(bank, a[0], b[0], start=(k == 0), stop=False)
                    pe.matmul(bank, a[0], b[1], start=False, stop=False)
                    mm = pe.matmul(bank, a[1], b[0], start=False, stop=(k == KT - 1))
                mm.then_inc(kv_done, 1)
            pe.wait_ge(kv_low, MH + MT)

            def scores(n, h):
                b, unit = h % 2, MH * n + h
                pe.wait_ge(q_split, unit + 1)
                pe.wait_ge(exp_done, unit + 1)
                for t in range(4):
                    rows = slice(t * P, (t + 1) * P)
                    bank = score[b][:, t // 2, t % 2]
                    pe.matmul(bank, q_hi[b][:, rows], k_hi[:, h], start=True, stop=False)
                    pe.matmul(bank, q_hi[b][:, rows], k_lo[:, h], start=False, stop=False)
                    mm = pe.matmul(bank, q_lo[b][:, rows], k_hi[:, h], start=False, stop=True)
                mm.then_inc(scored, 1)

            def body(n, last):
                for h in range(MH):
                    b, unit = h % 2, MH * n + h
                    nxt = following(n, h, last)
                    if nxt:
                        scores(*nxt)
                    feat = slice(h * MD, (h + 1) * MD)
                    pe.wait_ge(exp_done, 2 + unit + 1)
                    for m in range(MT):
                        it = ITEMS * h + m
                        pe.wait_ge(turn_freed, ITEMS * MH * n + it + 1)
                        for t in range(4):
                            mm = pe.transpose(turn[it % 2][:, t * P:(t + 1) * P],
                                              w[:, b, t, m * P:(m + 1) * P], ident[:])
                        mm.then_inc(turned, 1)
                    it = ITEMS * h + MT
                    pe.wait_ge(turn_freed, ITEMS * MH * n + it + 1)
                    pe.wait_ge(diag_ready, 4 * (unit + 1))
                    for t in range(4):
                        mm = pe.matmul(turn[it % 2][:, t * P:(t + 1) * P], ones[:], diag[:, b, t],
                                       start=True, stop=True)
                    mm.then_inc(turned, 1)
                    pe.wait_ge(gated, unit + 1)
                    for m in range(MT):
                        it = ITEMS * h + m
                        pe.wait_ge(turn_freed, 2 + ITEMS * MH * n + it + 1)
                        pe.matmul(o_ps[b][:], v_hi[:, m, feat], wT_hi[m][:], start=(m == 0), stop=False)
                        pe.matmul(o_ps[b][:], v_hi[:, m, feat], wT_lo[m][:], start=False, stop=False)
                        mm = pe.matmul(o_ps[b][:], v_lo[:, m, feat], wT_hi[m][:], start=False,
                                       stop=(m == MT - 1))
                        mm.then_inc(pv_done, 1)

            pe.wait_ge(ones_set, 1)
            scores(0, 0)
            chunks_of(pe, body)

        @block.scalar
        def _(act):
            for m in range(NPREP):
                act.wait_ge(mem_turned, m + 1)
                act.activation(memT_hi[:, 2 * m:2 * m + 2].rearrange("p k s -> p (k s)"), prep[m][:], ACT.Copy
                               ).then_inc(mem_high, 1)
            for k in range(KT):
                act.wait_ge(wm_loaded[k % 2], 16 * (k // 2 + 1))
                act.activation(w_hi[:, k], w_raw[:, k % 2], ACT.Copy).then_inc(wm_high, 1)
            for m in range(MH + MT):
                act.wait_ge(kv_done, m + 1)
                src, dst = ((prep[m % 4][:, 0:MEM], k_hi[:, m]) if m < MH
                            else (prep[m % 4][:], v_hi[:, m - MH]))
                act.activation(dst, src, ACT.Copy).then_inc(kv_high, 1)

            def exps(n, h):
                b, unit = h % 2, MH * n + h
                act.wait_ge(shift_ready, unit + 1)
                for t in range(4):
                    ex = act.activation(w[:, b, t], score[b][:, t // 2, t % 2], ACT.Exp, scale=scale,
                                        bias=neg_max[:, b, t:t + 1], accum_out=sums[:, b, t:t + 1])
                ex.then_inc(exp_done, 1)

            def body(n, last):
                for h in range(MH):
                    nxt = following(n, h, last)
                    if nxt:
                        exps(*nxt)
                    for m in range(MT):
                        it = ITEMS * h + m
                        act.wait_ge(turned, ITEMS * MH * n + it + 1)
                        act.wait_ge(pv_done, MT * (MH * n + h) + m + 1)
                        act.activation(wT_hi[m][:], turn[it % 2][:], ACT.Copy).then_inc(turn_high, 1)

            act.sem_inc(exp_done, 2)
            exps(0, 0)
            chunks_of(act, body)

        @block.vector
        def _(dve):
            dve.sem_inc(turn_freed, 2)
            dve.sem_inc(gated, 2)
            for m in range(NPREP):
                dve.wait_ge(mem_high, m + 1)
                part = slice(2 * m, 2 * m + 2)
                dve.tensor_tensor(memT_lo[:, part].rearrange("p k s -> p (k s)"), prep[m][:],
                                  as_f32(memT_hi[:, part]).rearrange("p k s -> p (k s)"), ALU.subtract
                                  ).then_inc(mem_low, 1)
            for k in range(KT):
                dve.wait_ge(wm_high, k + 1)
                dve.tensor_tensor(w_lo[:, k], w_raw[:, k % 2], as_f32(w_hi[:, k]), ALU.subtract
                                  ).then_inc(wm_low, 1)
            for m in range(MH + MT):
                dve.wait_ge(kv_high, m + 1)
                src, hi, lo = ((prep[m % 4][:, 0:MEM], k_hi[:, m], k_lo[:, m]) if m < MH
                               else (prep[m % 4][:], v_hi[:, m - MH], v_lo[:, m - MH]))
                dve.tensor_tensor(lo, src, as_f32(hi), ALU.subtract).then_inc(kv_low, 1)

            def maxima(n, h):
                b, unit = h % 2, MH * n + h
                dve.wait_ge(scored, unit + 1)
                for half in range(2):
                    dve.tensor_reduce(top[:, b, 2 * half:2 * half + 2], score[b][:, half], AX_X, ALU.max
                                      ).then_inc(top_done, 1)
                dve.wait_ge(top_done, 2 * (unit + 1))
                dve.tensor_scalar(neg_max[:, b], top[:, b], -scale, None, ALU.mult).then_inc(shift_ready, 1)

            def body(n, last):
                for h in range(MH):
                    b, unit = h % 2, MH * n + h
                    dve.wait_ge(exp_done, 2 + unit + 1)
                    dve.reciprocal(inv_sum[:, b], sums[:, b]).then_inc(inverted, 1)
                    nxt = following(n, h, last)
                    if nxt:
                        maxima(*nxt)
                    for m in range(MT):
                        it = ITEMS * h + m
                        dve.wait_ge(turn_high, MT * unit + m + 1)
                        dve.tensor_tensor(wT_lo[m][:], turn[it % 2][:], as_f32(wT_hi[m][:]), ALU.subtract
                                          ).then_inc(turn_freed, 1)
                    it = ITEMS * h + MT
                    dve.wait_ge(gate_loaded[b], 16 * (2 * n + h // 2 + 1))
                    dve.wait_ge(turned, ITEMS * MH * n + it + 1)
                    dve.tensor_tensor(gate_n[:, b], turn[it % 2][:], gate[:, b], ALU.mult
                                      ).then_inc(turn_freed, 1)
                    dve.wait_ge(stored[b], 16 * (2 * n + h // 2 + 1))
                    dve.wait_ge(turn_freed, 2 + ITEMS * MH * n + it + 1)
                    dve.wait_ge(pv_done, 2 + MT * (unit + 1))
                    dve.tensor_tensor(og[:, b], o_ps[b][:], gate_n[:, b], ALU.mult).then_inc(gated, 1)

            maxima(0, 0)
            chunks_of(dve, body)


def merge_branches(nc, ogT, w_branch, projT, mergedT):
    NBR, KB, FB = 3, 4, D // P
    PARTS = NBR * KB
    with Scope(nc) as c:
        w_raw = c.sb("wb_raw", [P, 2, D])
        w_hi = c.sb("wb_hi", [P, PARTS, D], F32R)
        w_lo = c.sb("wb_lo", [P, PARTS, D], F32R)
        o_raw = c.sb("mo_raw", [P, 2, KB, CH])
        o_hi = c.sb("mo_hi", [P, PARTS, CH], F32R)
        o_lo = c.sb("mo_lo", [P, PARTS, CH], F32R)
        gate = c.sb("mg_gate", [P, 2, NBR, CH])
        prod = c.sb("mg_prod", [P, NBR, CH])
        merged = c.sb("merged", [P, CH])
        m_hi = c.sb("merged_hi", [P, 2, CH], F32R)
        m_lo = c.sb("merged_lo", [P, 2, CH], F32R)
        ps = [[c.ps(f"mg_ps{s}{b}", [P, CH]) for b in range(NBR)] for s in range(2)]
        w_loaded = [c.sem(f"wb_loaded{b}") for b in range(2)]
        w_high = c.sem("wb_high")
        w_low = c.sem("wb_low")
        o_loaded = [c.sem(f"mo_loaded{b}") for b in range(2)]
        o_high = c.sem("mo_high")
        o_split = c.sem("mo_split")
        g_loaded = [c.sem(f"mg_loaded{b}") for b in range(2)]
        product = c.sem("mg_product")
        scaled = c.sem("mg_scaled")
        added = c.sem("mg_added")
        high = c.sem("mg_high")
        low = c.sem("mg_low")
        stored = [c.sem(f"mg_stored{b}") for b in range(2)]
        passed = c.sem("mg_passed")
        block = c.block()
        gates = projT[B_MERGE:].rearrange("(b f) p s -> f p b s", b=NBR)

        def chunks_of(engine, body):
            body(0, True)
            with engine.Fori(1, NCH) as n:
                body(n, False)

        @block.sync
        def _(sp):
            def load_gates(n, f):
                sp.dma_start(gate[:, f % 2], gates[f][:, :, bass.ds(n * CH, CH)]).then_inc(g_loaded[f % 2], 16)

            def load_outputs(n, b, slot):
                sp.dma_start(o_raw[:, slot],
                             ogT[b, :, bass.ds(n * CH, CH)].rearrange("(k p) s -> p k s", p=P)
                             ).then_inc(o_loaded[slot], 16)

            def body(n, first):
                for b in range(NBR):
                    if not (first and b < 2):
                        sp.wait_ge(o_split, PARTS * n + KB * (0, -1, 1)[b])
                        sp.sem_inc(passed, 1)
                    load_outputs(n, b, b % 2)
                    if first:
                        for k in range(KB):
                            part = b * KB + k
                            if part >= 2:
                                sp.wait_ge(w_low, part - 1)
                            sp.dma_start(w_raw[:, part % 2], w_branch[part]).then_inc(w_loaded[part % 2], 16)
                for f in range(FB):
                    unit = FB * n + f
                    if not (first and f < 2):
                        sp.wait_ge(scaled, 3 * unit + 3)
                        sp.sem_inc(passed, 1)
                    load_gates(n, f)
                    if f:
                        store(n, f - 1)
                store(n, FB - 1)

            def store(n, f):
                cols = bass.ds(n * CH, CH)
                sp.wait_ge(low, FB * n + f + 1)
                sp.sem_inc(passed, 1)
                for part, src in ((0, m_hi), (1, m_lo)):
                    sp.dma_start(mergedT[part, f * P:(f + 1) * P, cols], as_f32(src[:, f % 2])
                                 ).then_inc(stored[f % 2], 16)

            chunks_of(sp, body)
            for b in range(2):
                sp.wait_ge(stored[b], 32 + 16 * NCH * FB)

        @block.tensor
        def _(pe):
            def body(n, first):
                for f in range(FB):
                    unit = FB * n + f
                    cols = slice(f * P, (f + 1) * P)
                    for b in range(NBR):
                        bank = ps[f % 2][b]
                        pe.wait_ge(scaled, 3 * unit + b + 1)
                        for k in range(KB):
                            part = b * KB + k
                            if f == 0:
                                pe.wait_ge(o_split, PARTS * n + part + 1)
                                if first:
                                    pe.wait_ge(w_low, part + 1)
                            pe.matmul(bank[:], w_hi[:, part, cols], o_hi[:, part], start=(k == 0), stop=False)
                            pe.matmul(bank[:], w_hi[:, part, cols], o_lo[:, part], start=False, stop=False)
                            mm = pe.matmul(bank[:], w_lo[:, part, cols], o_hi[:, part], start=False,
                                           stop=(k == KB - 1))
                        mm.then_inc(product, 1)

            chunks_of(pe, body)

        def slot_loads(n, b):
            return 2 * n + b // 2 + 1 if b % 2 == 0 else n + 1

        @block.scalar
        def _(act):
            for b in range(2):
                act.sem_inc(stored[b], 32)

            def body(n, first):
                for part in range(PARTS):
                    b, k = divmod(part, KB)
                    if first:
                        act.wait_ge(w_loaded[part % 2], 16 * (part // 2 + 1))
                        act.activation(w_hi[:, part], w_raw[:, part % 2], ACT.Copy).then_inc(w_high, 1)
                    act.wait_ge(o_loaded[b % 2], 16 * slot_loads(n, b))
                    if not first:
                        act.wait_ge(product, NBR * FB * n)
                    act.activation(o_hi[:, part], o_raw[:, b % 2, k], ACT.Copy).then_inc(o_high, 1)
                for f in range(FB):
                    act.wait_ge(added, 2 * (FB * n + f + 1))
                    act.wait_ge(stored[f % 2], 32 * (FB // 2 * n + f // 2 + 1))
                    act.activation(m_hi[:, f % 2], merged[:], ACT.Copy).then_inc(high, 1)

            chunks_of(act, body)

        @block.vector
        def _(dve):
            dve.sem_inc(scaled, 6)

            def body(n, first):
                for part in range(PARTS):
                    b, k = divmod(part, KB)
                    if first:
                        dve.wait_ge(w_high, part + 1)
                        dve.tensor_tensor(w_lo[:, part], w_raw[:, part % 2], as_f32(w_hi[:, part]),
                                          ALU.subtract).then_inc(w_low, 1)
                    dve.wait_ge(o_high, PARTS * n + part + 1)
                    dve.tensor_tensor(o_lo[:, part], o_raw[:, b % 2, k], as_f32(o_hi[:, part]), ALU.subtract
                                      ).then_inc(o_split, 1)
                for f in range(FB):
                    unit = FB * n + f
                    dve.wait_ge(g_loaded[f % 2], 16 * (FB // 2 * n + f // 2 + 1))
                    if not (first and f == 0):
                        dve.wait_ge(added, 2 * unit)
                    for b in range(NBR):
                        dve.wait_ge(product, NBR * unit + b + 1)
                        dve.tensor_tensor(prod[:, b], ps[f % 2][b][:], gate[:, f % 2, b], ALU.mult
                                          ).then_inc(scaled, 1)

            chunks_of(dve, body)

        @block.gpsimd
        def _(pool):
            def body(n, first):
                for f in range(FB):
                    unit = FB * n + f
                    pool.wait_ge(scaled, 6 + 3 * unit + 2)
                    if not (first and f == 0):
                        pool.wait_ge(low, unit)
                    pool.tensor_tensor(merged[:], prod[:, 0], prod[:, 1], ALU.add).then_inc(added, 1)
                    pool.wait_ge(scaled, 6 + 3 * unit + 3)
                    pool.wait_ge(added, 2 * unit + 1)
                    pool.tensor_tensor(merged[:], merged[:], prod[:, 2], ALU.add).then_inc(added, 1)
                    pool.wait_ge(high, unit + 1)
                    pool.tensor_tensor(m_lo[:, f % 2], merged[:], as_f32(m_hi[:, f % 2]), ALU.subtract
                                       ).then_inc(low, 1)

            chunks_of(pool, body)


def project_out(nc, mergedT, w_out, x, ln, out):
    with Scope(nc) as c:
        w_raw = c.sb("wo_raw", [P, 2, D])
        w_hi = c.sb("wo_hi", [P, KT, D], F32R)
        w_lo = c.sb("wo_lo", [P, KT, D], F32R)
        m_hi = [c.sb(f"m_hi{u}", [P, KT, CH], F32R) for u in range(2)]
        m_lo = [c.sb(f"m_lo{u}", [P, KT, CH], F32R) for u in range(2)]
        x_sb = c.sb("x_out", [P, 2, D])
        ln_sb = c.sb("ln_gain_bias", [P, 2, D])
        y = c.sb("y", [P, 2, D])
        sq = c.sb("y_sq", [P, D])
        z = c.sb("z", [P, 2, D])
        stat = c.sb("ln_stat", [P, 2, 5])
        eps = c.sb("ln_eps", [P, 1])
        SUM, NEG_MEAN, SSQ, STD, RSTD = range(5)
        ps = [c.ps(f"out_ps{s}", [P, D]) for s in range(4)]
        w_loaded = [c.sem(f"wo_loaded{b}") for b in range(2)]
        ln_loaded = c.sem("ln_loaded")
        eps_set = c.sem("ln_eps_set")
        w_high = c.sem("wo_high")
        w_low = c.sem("wo_low")
        m_loaded = [c.sem(f"m_loaded{u}") for u in range(2)]
        x_loaded = [c.sem(f"x_out_loaded{u}") for u in range(2)]
        product = c.sem("out_product")
        y_done = c.sem("y_done")
        mean_done = c.sem("mean_done")
        ssq_done = c.sem("ln_ssq_done")
        std_done = c.sem("std_done")
        rstd_done = c.sem("ln_rstd_done")
        normed = c.sem("normed")
        gained = c.sem("gained")
        shifted = c.sem("shifted")
        stored = [c.sem(f"out_stored{u}") for u in range(2)]
        passed = c.sem("out_passed")
        block = c.block()
        xf = x.rearrange("b s d -> (b s) d")
        of = out.rearrange("b s d -> (b s) d")
        NT = 8

        def turns(engine, body):
            with engine.Fori(0, NCH // 2) as i:
                body(i)

        @block.sync
        def _(sp):
            sp.dma_start(ln_sb[:], ln).then_inc(ln_loaded, 16)

            def load_chunk(n, u):
                for src, dst in ((0, m_hi), (1, m_lo)):
                    sp.dma_start(as_f32(dst[u][:]),
                                 mergedT[src, :, n * CH:(n + 1) * CH].rearrange("(k p) s -> p k s", p=P)
                                 ).then_inc(m_loaded[u], 16)

            load_chunk(0, 0)
            for k in range(KT):
                if k >= 2:
                    sp.wait_ge(w_low, k - 1)
                sp.dma_start(w_raw[:, k % 2], w_out[k]).then_inc(w_loaded[k % 2], 16)
            load_chunk(1, 1)
            for u in range(2):
                sp.sem_inc(stored[u], 16)

            def body(i):
                for j in range(NT):
                    tile = NT * i + j
                    sp.wait_ge(shifted, tile + 1)
                    sp.sem_inc(passed, 1)
                    sp.dma_start(x_sb[:, j % 2], xf[bass.ds(tile * P, P)]).then_inc(x_loaded[j % 2], 16)
                    if j:
                        store(i, j - 1)
                store(i, NT - 1)

            def store(i, j):
                tile = NT * i + j
                sp.wait_ge(shifted, 2 + tile + 1)
                sp.sem_inc(passed, 1)
                sp.dma_start(of[bass.ds(tile * P, P)], z[:, j % 2]).then_inc(stored[j % 2], 16)

            body(0)
            sp.wait_ge(product, 4)
            load_chunk(2, 0)
            sp.wait_ge(product, 8)
            load_chunk(3, 1)
            body(1)
            for u in range(2):
                sp.wait_ge(stored[u], 16 + 16 * TT // 2)

        @block.tensor
        def _(pe):
            def body(i):
                for j in range(NT):
                    tile, u = NT * i + j, j // 4
                    rows = slice(j % 4 * P, (j % 4 + 1) * P)
                    if j % 4 == 0:
                        pe.wait_ge(m_loaded[u], 32 * (i + 1))
                    pe.wait_ge(y_done, tile + 1)
                    for half in range(2):
                        bank = ps[j % 4][:, half * CH:(half + 1) * CH]
                        cols = slice(half * CH, (half + 1) * CH)
                        for k in range(KT):
                            pe.matmul(bank, m_hi[u][:, k, rows], w_hi[:, k, cols], start=(k == 0), stop=False)
                            pe.matmul(bank, m_hi[u][:, k, rows], w_lo[:, k, cols], start=False, stop=False)
                            mm = pe.matmul(bank, m_lo[u][:, k, rows], w_hi[:, k, cols], start=False,
                                           stop=(k == KT - 1))
                    mm.then_inc(product, 1)

            pe.wait_ge(w_low, KT)
            turns(pe, body)

        @block.scalar
        def _(act):
            for k in range(KT):
                act.wait_ge(w_loaded[k % 2], 16 * (k // 2 + 1))
                act.activation(w_hi[:, k], w_raw[:, k % 2], ACT.Copy).then_inc(w_high, 1)
            act.wait_ge(eps_set, 1)

            def body(i):
                for j in range(NT):
                    tile, u = NT * i + j, j % 2
                    act.wait_ge(mean_done, tile + 1)
                    act.activation(sq[:], y[:, u], ACT.Square, bias=stat[:, u, NEG_MEAN:NEG_MEAN + 1],
                                   accum_out=stat[:, u, SSQ:SSQ + 1]).then_inc(ssq_done, 1)
                    act.wait_ge(ssq_done, tile + 1)
                    act.activation(stat[:, u, STD:STD + 1], stat[:, u, SSQ:SSQ + 1], ACT.Sqrt,
                                   bias=eps[:, 0:1], scale=1.0 / D).then_inc(std_done, 1)

            turns(act, body)

        @block.vector
        def _(dve):
            dve.sem_inc(y_done, 4)
            for k in range(KT):
                dve.wait_ge(w_high, k + 1)
                dve.tensor_tensor(w_lo[:, k], w_raw[:, k % 2], as_f32(w_hi[:, k]), ALU.subtract
                                  ).then_inc(w_low, 1)

            def body(i):
                for j in range(NT):
                    tile, u = NT * i + j, j % 2

                    def s(at):
                        return stat[:, u, at:at + 1]

                    dve.wait_ge(x_loaded[u], 16 * (NT // 2 * i + j // 2 + 1))
                    dve.wait_ge(product, tile + 1)
                    dve.scalar_tensor_tensor(out=y[:, u], in0=x_sb[:, u], scalar=ALPHA, in1=ps[j % 4][:],
                                             op0=ALU.mult, op1=ALU.add, accum_out=s(SUM)).then_inc(y_done, 1)
                    dve.wait_ge(y_done, 4 + tile + 1)
                    dve.tensor_scalar(s(NEG_MEAN), s(SUM), -1.0 / D, None, ALU.mult).then_inc(mean_done, 1)
                    dve.wait_ge(std_done, tile + 1)
                    dve.reciprocal(s(RSTD), s(STD)).then_inc(rstd_done, 1)
                    dve.wait_ge(rstd_done, tile + 1)
                    dve.wait_ge(stored[u], 16 * (NT // 2 * i + j // 2 + 1))
                    dve.tensor_scalar(z[:, u], y[:, u], s(NEG_MEAN), s(RSTD), ALU.add, ALU.mult
                                      ).then_inc(normed, 1)

            turns(dve, body)

        @block.gpsimd
        def _(pool):
            pool.memset(eps[:], LN_EPS).then_inc(eps_set, 1)
            pool.sem_inc(shifted, 2)
            pool.wait_ge(ln_loaded, 16)

            def body(i):
                for j in range(NT):
                    tile, u = NT * i + j, j % 2
                    pool.wait_ge(normed, tile + 1)
                    pool.tensor_tensor(z[:, u], z[:, u], ln_sb[:, 0], ALU.mult).then_inc(gained, 1)
                    pool.wait_ge(gained, tile + 1)
                    pool.tensor_tensor(z[:, u], z[:, u], ln_sb[:, 1], ALU.add).then_inc(shifted, 1)

            turns(pool, body)


def build(nc, x, mem, w_all, rotary, gains, w_q, w_kv, w_mem, w_branch, w_out, ln, out, scratch):
    projT, qn, qp, kn, kp, va, vb, ogT, mergedT = scratch
    with Scope(nc) as c:
        ident = c.sb("ident", [P, P])
        with Scope(nc) as r:
            xTh = r.sb("xTh", [P, KT, S], F32R)
            xTl = r.sb("xTl", [P, KT, S], F32R)
            load_x_transposed(nc, x, ident, xTh, xTl)
            project_x(nc, w_all, projT, xTh, xTl)
        latent_heads(nc, projT, rotary, gains, w_q, w_kv, ident, qn, qp, kn, kp, va, vb)
        attend(nc, True, (qn, qp), (kn, kp), va, projT, B_GATE, ogT[0], ident)
        sb_q = projT[B_COPY:B_COPY + 4].rearrange("b p s -> (b p) s")
        sb_k = projT[B_COPY + 4:B_COPY + 8].rearrange("b p s -> (b p) s")
        attend(nc, False, sb_q, sb_k, vb, projT, B_GATE + 4, ogT[1], ident)
        attend_memory(nc, mem, w_mem, projT, ogT[2], ident)
    merge_branches(nc, ogT, w_branch, projT, mergedT)
    project_out(nc, mergedT, w_out, x, ln, out)


def rotary_table():
    half = ROPE // 2
    freqs = np.float32(10000.0) ** (-np.arange(half, dtype=np.float32) / np.float32(half))
    ang = freqs[:, None] * np.arange(S, dtype=np.float32)[None, :]
    cos, sin = np.cos(ang), np.sin(ang)
    return np.stack([np.tile(np.concatenate([cos, cos]), (4, 1)),
                     np.tile(np.concatenate([-sin, sin]), (4, 1))]).astype(np.float32)


def lay_out(inputs):
    w = np.asarray(inputs["w_in"])[0]
    rope = w[:, 384:416]
    swapped = np.concatenate([rope[:, 16:], rope[:, :16]], axis=1)
    col = lambda a, b: w[:, a:b]
    g = 416
    parts = [col(0, 384), rope, swapped, rope, swapped,
             col(g, g + 512), col(g + 2048, g + 2560), col(g + 3072, g + 3584),
             col(g + 512, g + 2048), col(g + 2560, g + 3072),
             np.asarray(inputs["w_merge_gate"])[0]]
    w_all = np.concatenate(parts, axis=1)
    w_all = w_all.reshape(KT, P, NBLK, P).transpose(2, 1, 0, 3).reshape(NBLK, P, KT * P)
    bias = np.zeros((NBLK, P, 1), w_all.dtype)
    bias[B_MERGE:, :, 0] = np.asarray(inputs["b_merge_gate"])[0].reshape(NB_MERGE, P)
    w_all = np.concatenate([w_all, bias], axis=2)
    q = np.asarray(inputs["w_q_b"])[0].reshape(QL, H, NOPE + ROPE)
    pe = q[..., NOPE:]
    swapped = np.concatenate([pe[..., ROPE // 2:], pe[..., :ROPE // 2]], axis=-1)
    w_q = np.concatenate([q[..., :NOPE].reshape(QL, -1), pe.reshape(QL, -1), swapped.reshape(QL, -1)], axis=1)
    kv = np.asarray(inputs["w_kv_b"])[0].reshape(KVL, H, NOPE + VD)
    w_kv = np.concatenate([kv[..., :NOPE].reshape(KVL, -1), kv[..., NOPE:].reshape(KVL, -1)], axis=1)
    gains = np.concatenate([np.asarray(inputs["q_a_gain"])[0], np.asarray(inputs["kv_a_gain"])[0]])
    gains = gains.reshape(3, P).T
    w_branch = np.concatenate([np.asarray(inputs[n])[0] for n in
                               ("w_branch_mla", "w_branch_sb", "w_branch_mem")])
    ln = np.stack([np.asarray(inputs["ln_gain"])[0], np.asarray(inputs["ln_bias"])[0]])
    return {
        "x": inputs["x"],
        "mem": inputs["mem"],
        "w_all": w_all,
        "rotary": rotary_table(),
        "gains": gains,
        "w_q": w_q.reshape(2, P, D).transpose(1, 0, 2),
        "w_kv": w_kv,
        "w_mem": np.asarray(inputs["w_mem_kv"])[0].reshape(KT, P, D),
        "w_branch": w_branch.reshape(12, P, D),
        "w_out": np.asarray(inputs["w_out"])[0].reshape(KT, P, D),
        "ln": np.broadcast_to(ln, (P, 2, D)),
    }


def kernel(**inputs):
    import concourse.bacc as bacc
    from concourse.bass_utils import run_bass_kernel_spmd
    nc = bacc.Bacc("TRN2", target_bir_lowering=False, num_devices=1)
    arrays, args = {}, []
    for name, a in lay_out(inputs).items():
        a = np.ascontiguousarray(a)
        arrays[f"in_{name}_dram"] = a
        args.append(nc.dram_tensor(f"in_{name}_dram", a.shape, mybir.dt.from_np(a.dtype),
                                   kind="ExternalInput").ap())
    shapes = dict(projT=(NBLK, P, S), qn=(512, S), qp=(256, S), kn=(512, S), kp=(ROPE, S), va=(S, 512),
                  vb=(S, 512), ogT=(3, 512, S), mergedT=(2, D, S))
    scratch = [nc.dram_tensor(n, sh, F32).ap() for n, sh in shapes.items()]
    out = nc.dram_tensor("out_dram", (1, S, D), F32, kind="ExternalOutput").ap()
    build(nc, *args, out, scratch)
    r = run_bass_kernel_spmd(nc, [arrays], core_ids=[0])
    return r.results[0]["out_dram"]
```

```python
from contextlib import ExitStack

import numpy as np
import concourse.bass as bass
from concourse import mybir

P = 128
D = 1024
S = 2048
KT = D // P
CH = 512
NCH = S // CH
TT = S // P
MEM = 256
MT = MEM // P
QL, KVL, ROPE, NOPE, VD, H = 256, 128, 32, 64, 64, 8
SBD = 64
MH, MD = 4, 128
NB_LAT, NB_GATE, NB_COPY, NB_MERGE = 4, 12, 16, 24
NBLK = NB_LAT + NB_GATE + NB_COPY + NB_MERGE
B_GATE, B_COPY, B_MERGE = NB_LAT, NB_LAT + NB_GATE, NB_LAT + NB_GATE + NB_COPY
RMS_EPS, LN_EPS = 1e-6, 1e-5
ALPHA = 2.0 ** 0.25
BIG = 3.0e38

F32 = mybir.dt.float32
F32R = mybir.dt.float32r
ALU = mybir.AluOpType
ACT = mybir.ActivationFunctionType
AX_X = mybir.AxisListType.X


def as_f32(ap):
    return ap.bitcast(F32)


class Scope:

    def __init__(self, nc):
        self.nc, self.ctx, self.sems = nc, ExitStack(), []

    def __enter__(self):
        return self

    def __exit__(self, *a):
        self.ctx.__exit__(*a)
        if self.sems and a[0] is None:
            self.nc.clear_and_free_semaphores(self.sems)
            self.nc.all_engine_barrier()

    def sb(self, name, shape, dt=F32):
        return self.ctx.enter_context(self.nc.sbuf_tensor(name, shape, dt))

    def ps(self, name, shape, dt=F32):
        return self.ctx.enter_context(self.nc.psum_tensor(name, shape, dt))

    def sem(self, name):
        self.sems.append(self.nc.alloc_semaphore(name=name))
        return self.sems[-1]

    def block(self):
        return self.ctx.enter_context(self.nc.Block())


def load_x_transposed(nc, x, ident, xTh, xTl):
    NBANK = 8
    with Scope(nc) as c:
        xin = c.sb("xin", [P, 2, 4, D])
        bank = [c.ps(f"xT_ps{i}", [P, CH]) for i in range(NBANK)]
        loaded = [c.sem(f"x_loaded{i}") for i in range(2)]
        turned = c.sem("x_turned")
        high_done = c.sem("x_high_done")
        low_done = c.sem("x_low_done")
        ident_zero = c.sem("ident_zero")
        ident_ready = c.sem("ident_ready")
        block = c.block()
        xg = x.rearrange("b (g t p) d -> (b g) p t d", t=4, p=P)

        @block.sync
        def _(sp):
            for g in range(NCH):
                if g >= 2:
                    sp.wait_ge(turned, KT * (g - 1))
                sp.dma_start(xin[:, g % 2], xg[g]).then_inc(loaded[g % 2], 16)

        @block.gpsimd
        def _(pool):
            pool.memset(ident[:], 0.0).then_inc(ident_zero, 1)
            pool.wait_ge(ident_zero, 1)
            pool.affine_select(out=ident[:], in_=ident[:], compare_op=ALU.not_equal, fill=1.0, base=0,
                               pattern=[[-1, P]], channel_multiplier=1).then_inc(ident_ready, 1)

        @block.tensor
        def _(pe):
            pe.wait_ge(ident_ready, 1)
            for g in range(NCH):
                pe.wait_ge(loaded[g % 2], 16 * (g // 2 + 1))
                for k in range(KT):
                    n = g * KT + k
                    if n >= NBANK:
                        pe.wait_ge(low_done, n - NBANK + 1)
                    for t in range(4):
                        mm = pe.transpose(bank[n % NBANK][:, t * P:(t + 1) * P],
                                          xin[:, g % 2, t, k * P:(k + 1) * P], ident[:])
                    mm.then_inc(turned, 1)

        @block.scalar
        def _(act):
            for n in range(NCH * KT):
                g, k = divmod(n, KT)
                act.wait_ge(turned, n + 1)
                act.activation(xTh[:, k, g * CH:(g + 1) * CH], bank[n % NBANK][:],
                               ACT.Copy).then_inc(high_done, 1)

        @block.vector
        def _(dve):
            for n in range(NCH * KT):
                g, k = divmod(n, KT)
                cols = slice(g * CH, (g + 1) * CH)
                dve.wait_ge(high_done, n + 1)
                dve.tensor_tensor(xTl[:, k, cols], bank[n % NBANK][:], as_f32(xTh[:, k, cols]),
                                  ALU.subtract).then_inc(low_done, 1)


def project_x(nc, w_all, projT, xTh, xTl):
    NPAIR = NBLK // 2
    with Scope(nc) as c:
        wraw = c.sb("wraw", [P, 2, KT * P + 1])
        wh = c.sb("wh", [P, 2, KT * P], F32R)
        wl = c.sb("wl", [P, 2, KT * P], F32R)
        bias = c.sb("proj_bias", [P, 2])
        ones = c.sb("ones", [P, 1])
        ones_row = ones[:, 0:1].broadcast_to([P, KT * P])
        stage = c.sb("proj_stage", [P, 2, S])
        sig = c.sb("gate_sigmoid", [P, 2, CH])
        acc = [[c.ps(f"proj_ps{u}{n}", [P, CH]) for n in range(NCH)] for u in range(2)]
        w_loaded = [c.sem(f"w_loaded{u}") for u in range(2)]
        ones_set = c.sem("ones_set")
        high_done = c.sem("w_high_done")
        low_done = c.sem("w_low_done")
        product = c.sem("proj_product")
        sig_done = c.sem("sig_done")
        evac = c.sem("proj_evac")
        stored = [c.sem(f"proj_stored{u}") for u in range(2)]
        block = c.block()

        @block.sync
        def _(sp):
            for u in range(2):
                sp.dma_start(wraw[:, u], w_all[u]).then_inc(w_loaded[u], 16)

            def pair(i, last):
                for u in range(2):
                    b = 2 * i + u
                    if not last:
                        sp.wait_ge(low_done, b + 1)
                        sp.dma_start(wraw[:, u], w_all[bass.ds(b + 2, 1)].squeeze(0)
                                     ).then_inc(w_loaded[u], 16)
                    sp.wait_ge(evac, NCH * (b + 1))
                    sp.dma_start(projT[bass.ds(b, 1)].squeeze(0), stage[:, u]).then_inc(stored[u], 16)

            with sp.Fori(0, NPAIR - 1) as i:
                pair(i, False)
            pair(NPAIR - 1, True)
            for u in range(2):
                sp.wait_ge(stored[u], 16 * NPAIR)

        @block.gpsimd
        def _(pool):
            def pair(i, first):
                for u in range(2):
                    b = 2 * i + u
                    pool.wait_ge(w_loaded[u], 16 * (i + 1))
                    if not first:
                        pool.wait_ge(evac, NCH * (b - 1))
                    pool.tensor_tensor(bias[:, u:u + 1], wraw[:, u, KT * P:], ones[:, 0:1], ALU.mult)
                    pool.tensor_tensor(wh[:, u], wraw[:, u, 0:KT * P], ones_row, ALU.mult
                                       ).then_inc(high_done, 1)
                    pool.wait_ge(high_done, b + 1)
                    pool.tensor_tensor(wl[:, u], wraw[:, u, 0:KT * P], as_f32(wh[:, u]), ALU.subtract
                                       ).then_inc(low_done, 1)

            pool.memset(ones[:], 1.0).then_inc(ones_set, 1)
            pool.wait_ge(ones_set, 1)
            pair(0, True)
            with pool.Fori(1, NPAIR) as i:
                pair(i, False)

        @block.tensor
        def _(pe):
            def pair(i, first):
                for u in range(2):
                    b = 2 * i + u
                    pe.wait_ge(low_done, b + 1)
                    for n in range(NCH):
                        if not first:
                            pe.wait_ge(evac, NCH * (b - 2) + n + 1)
                        cols = slice(n * CH, (n + 1) * CH)
                        for k in range(KT):
                            pe.matmul(acc[u][n][:], wh[:, u, k * P:(k + 1) * P], xTh[:, k, cols],
                                      start=(k == 0), stop=False)
                            pe.matmul(acc[u][n][:], wh[:, u, k * P:(k + 1) * P], xTl[:, k, cols],
                                      start=False, stop=False)
                            mm = pe.matmul(acc[u][n][:], wl[:, u, k * P:(k + 1) * P], xTh[:, k, cols],
                                           start=False, stop=(k == KT - 1))
                        mm.then_inc(product, 1)

            pair(0, True)
            with pe.Fori(1, NPAIR) as i:
                pair(i, False)

        @block.scalar
        def _(act):
            with act.Fori(B_GATE // 2, B_COPY // 2) as i:
                for u in range(2):
                    b = 2 * i + u
                    for n in range(NCH):
                        act.wait_ge(product, NCH * b + n + 1)
                        act.wait_ge(evac, NCH * b + n - 1)
                        act.activation(sig[:, n % 2], acc[u][n][:], ACT.Sigmoid).then_inc(sig_done, 1)
            with act.Fori(B_MERGE // 2, NPAIR) as i:
                for u in range(2):
                    b = 2 * i + u
                    act.wait_ge(stored[u], 16 * i)
                    for n in range(NCH):
                        act.wait_ge(product, NCH * b + n + 1)
                        act.wait_ge(evac, NCH * b + n)
                        act.activation(stage[:, u, n * CH:(n + 1) * CH], acc[u][n][:], ACT.Sigmoid,
                                       bias=bias[:, u:u + 1]).then_inc(evac, 1)

        @block.vector
        def _(dve):
            def copies(i, first):
                for u in range(2):
                    b = 2 * i + u
                    if not first:
                        dve.wait_ge(stored[u], 16 * i)
                    for n in range(NCH):
                        dve.wait_ge(product, NCH * b + n + 1)
                        dve.tensor_copy(stage[:, u, n * CH:(n + 1) * CH], acc[u][n][:]).then_inc(evac, 1)

            copies(0, True)
            with dve.Fori(1, B_GATE // 2) as i:
                copies(i, False)
            with dve.Fori(B_GATE // 2, B_COPY // 2) as i:
                for u in range(2):
                    b = 2 * i + u
                    dve.wait_ge(stored[u], 16 * i)
                    for n in range(NCH):
                        dve.wait_ge(sig_done, NCH * (b - B_GATE) + n + 1)
                        dve.tensor_tensor(stage[:, u, n * CH:(n + 1) * CH], acc[u][n][:], sig[:, n % 2],
                                          ALU.mult).then_inc(evac, 1)
            with dve.Fori(B_COPY // 2, B_MERGE // 2) as i:
                copies(i, False)


def latent_heads(nc, projT, rotary, gains, w_q, w_kv, ident, qn, qp, kn, kp, va, vb):
    QB = 8
    PLAIN = 12
    USES = NCH + PLAIN
    with Scope(nc) as c:
        wq_raw = c.sb("wq_raw", [P, 2, D])
        wq_h = c.sb("wq_h", [P, 2, D], F32R)
        wq_l = c.sb("wq_l", [P, 2, D], F32R)
        wkv_raw = c.sb("wkv_raw", [P, D])
        wkv_h = c.sb("wkv_h", [P, D], F32R)
        wkv_l = c.sb("wkv_l", [P, D], F32R)
        gain = c.sb("gain", [P, 3])
        eps = c.sb("eps", [P, 1])
        ones = c.sb("ones_sq", [P, P])
        lat = c.sb("lat", [P, 2, 3, CH])
        kr = c.sb("k_rope", [ROPE, 2, 2, CH])
        cs = c.sb("cos_sin", [P, 2, 2, CH])
        sq = c.sb("lat_sq", [P, 3, CH])
        rstd = c.sb("lat_rstd", [P, 2, CH])
        norm = c.sb("lat_norm", [P, 3, CH])
        norm_h = c.sb("lat_norm_h", [P, 2, 3, CH], F32R)
        norm_l = c.sb("lat_norm_l", [P, 2, 3, CH], F32R)
        plain = c.sb("plain_out", [P, 2, PLAIN, CH])
        rot = c.sb("rot_out", [P, 2, 2, CH])
        part = c.sb("rot_part", [P, 2, CH])
        krot = c.sb("k_rot_out", [ROPE, 2, CH])
        kpart = c.sb("k_rot_part", [ROPE, 2, CH])
        vT = c.sb("vT", [P, S])
        v_out = c.sb("v_out", [P, 2, NCH, CH])
        ssq = [c.ps(f"ssq{i}", [P, CH]) for i in range(2)]
        pbank = [c.ps(f"plain_ps{i}", [P, CH]) for i in range(4)]
        rbank = [c.ps(f"rot_ps{i}", [P, CH]) for i in range(2)]
        w_loaded = c.sem("lat_w_loaded")
        consts = c.sem("lat_consts")
        w_split = c.sem("lat_w_split")
        lat_loaded = [c.sem(f"lat_loaded{u}") for u in range(2)]
        rope_loaded = [c.sem(f"rope_loaded{u}") for u in range(2)]
        v_loaded = c.sem("vT_loaded")
        sq_done = c.sem("lat_sq_done")
        ssq_done = c.sem("ssq_done")
        root_done = c.sem("root_done")
        rstd_done = c.sem("rstd_done")
        norm_done = c.sem("norm_done")
        norm_high = c.sem("norm_high")
        norm_low = c.sem("norm_low")
        plain_done = c.sem("plain_done")
        plain_out = c.sem("plain_out")
        rot_done = c.sem("rot_done")
        rot_parts = c.sem("rot_parts")
        rot_out = c.sem("rot_out")
        krot_parts = c.sem("krot_parts")
        stored = [c.sem(f"lat_stored{u}") for u in range(2)]
        v_stored = [c.sem(f"vb_stored{u}") for u in range(2)]
        block = c.block()
        NST = 5
        order = [4, 6, 5, 7]

        @block.sync
        def _(sp):
            def load_latents(n):
                u, cols = n % 2, slice(n * CH, (n + 1) * CH)
                if n >= 2:
                    sp.wait_ge(norm_done, 3 * (n - 1))
                sp.dma_start(lat[:, u], projT[0:3, :, cols].rearrange("b p c -> p b c")
                             ).then_inc(lat_loaded[u], 16)

            def load_rotary(n):
                u, cols = n % 2, slice(n * CH, (n + 1) * CH)
                if n >= 2:
                    sp.wait_ge(rot_parts, 4 * (n - 1))
                    sp.wait_ge(krot_parts, 2 * (n - 1))
                sp.dma_start(kr[:, u], projT[3, 0:2 * ROPE, cols].rearrange("(a p) c -> p a c", p=ROPE)
                             ).then_inc(rope_loaded[u], 16)
                sp.dma_start(cs[:, u], rotary[:, :, cols].rearrange("a p c -> p a c")
                             ).then_inc(rope_loaded[u], 16)

            load_latents(0)
            sp.dma_start(wq_raw[:], w_q).then_inc(w_loaded, 16)
            sp.dma_start(wkv_raw[:], w_kv).then_inc(w_loaded, 16)
            sp.dma_start(gain[:], gains).then_inc(w_loaded, 16)
            sp.dma_start(vT[:], projT[B_COPY + 8]).then_inc(v_loaded, 16)
            load_latents(1)
            load_rotary(0)
            load_rotary(1)
            for n in range(NCH):
                u, cols = n % 2, slice(n * CH, (n + 1) * CH)
                if n + 2 < NCH:
                    load_latents(n + 2)
                sp.wait_ge(plain_out, USES * n + NCH)
                sp.dma_start(vb[:, n * P:(n + 1) * P].rearrange("(t p) f -> p t f", p=P),
                             v_out[:, u].rearrange("p n (t f) -> p (n t) f", f=P)).then_inc(v_stored[u], 16)
                if n + 1 < NCH:
                    sp.dma_start(vT[:], projT[B_COPY + 9 + n]).then_inc(v_loaded, 16)
                sp.wait_ge(plain_out, USES * (n + 1))
                for dst, src in ((qn, 0), (kn, 4)):
                    sp.dma_start(dst[:, cols].rearrange("(b p) c -> p b c", p=P),
                                 plain[:, u, src:src + 4]).then_inc(stored[u], 16)
                sp.dma_start(va[cols].rearrange("(t p) f -> p t f", p=P), plain[:, u, 8:12]
                             ).then_inc(stored[u], 16)
                sp.wait_ge(rot_out, 3 * (n + 1))
                sp.dma_start(qp[:, cols].rearrange("(b p) c -> p b c", p=P), rot[:, u]
                             ).then_inc(stored[u], 16)
                sp.dma_start(kp[:, cols], krot[:, u]).then_inc(stored[u], 16)
                if n + 2 < NCH:
                    load_rotary(n + 2)
            for u in range(2):
                sp.wait_ge(stored[u], 16 * NST * 2)
                sp.wait_ge(v_stored[u], 32)

        @block.gpsimd
        def _(pool):
            pool.memset(eps[:], RMS_EPS).then_inc(consts, 1)
            pool.memset(ones[:], 1.0).then_inc(consts, 1)

            def squares(n):
                pool.wait_ge(lat_loaded[n % 2], 16 * (n // 2 + 1))
                if n:
                    pool.wait_ge(ssq_done, 2 * n)
                pool.tensor_tensor(sq[:], lat[:, n % 2], lat[:, n % 2], ALU.mult).then_inc(sq_done, 1)

            squares(0)
            for n in range(NCH):
                u = n % 2
                if n + 1 < NCH:
                    squares(n + 1)
                for j in range(2):
                    if n >= 2:
                        pool.wait_ge(stored[u], 16 * NST * (n // 2))
                    pool.wait_ge(rot_parts, 4 * n + 2 * j + 2)
                    pool.tensor_tensor(rot[:, u, j], rot[:, u, j], part[:, j], ALU.add
                                       ).then_inc(rot_out, 1)
                pool.wait_ge(krot_parts, 2 * (n + 1))
                pool.tensor_tensor(krot[:, u], krot[:, u], kpart[:, u], ALU.add).then_inc(rot_out, 1)

        @block.tensor
        def _(pe):
            pe.wait_ge(consts, 2)

            def sum_squares(n):
                pe.wait_ge(sq_done, n + 1)
                if n:
                    pe.wait_ge(root_done, 2 * n)
                pe.matmul(ssq[0][:], ones[:], sq[:, 0], start=True, stop=False)
                pe.matmul(ssq[0][:], ones[:], sq[:, 1], start=False, stop=True).then_inc(ssq_done, 1)
                pe.matmul(ssq[1][:], ones[:], sq[:, 2], start=True, stop=True).then_inc(ssq_done, 1)

            sum_squares(0)
            for n in range(NCH):
                u = n % 2
                pe.wait_ge(v_loaded, 16 * (n + 1))
                for m in range(NCH):
                    r = USES * n + m
                    if n:
                        pe.wait_ge(plain_out, r - 3)
                    for t in range(4):
                        at = (4 * m + t) * P
                        mm = pe.transpose(pbank[r % 4][:, t * P:(t + 1) * P], vT[:, at:at + P], ident[:])
                    mm.then_inc(plain_done, 1)
                pe.wait_ge(w_split, 2)
                pe.wait_ge(norm_low, 3 * (n + 1))

                def up(bank, pairs, done):
                    last = 3 * len(pairs) - 1
                    at = 0
                    for (ah, al), (bh, bl) in pairs:
                        for a, b in ((ah, bh), (ah, bl), (al, bh)):
                            mm = pe.matmul(bank, a, b, start=(at == 0), stop=(at == last))
                            at += 1
                    mm.then_inc(done, 1)

                for j in range(PLAIN):
                    r = USES * n + NCH + j
                    pe.wait_ge(plain_out, r - 3)
                    cols = slice((j % 4) * P, (j % 4 + 1) * P)
                    if j < 4:
                        pairs = [((wq_h[:, k, cols], wq_l[:, k, cols]), (norm_h[:, u, k], norm_l[:, u, k]))
                                 for k in range(2)]
                    elif j < 8:
                        pairs = [((wkv_h[:, cols], wkv_l[:, cols]), (norm_h[:, u, 2], norm_l[:, u, 2]))]
                    else:
                        pairs = [((norm_h[:, u, 2, cols], norm_l[:, u, 2, cols]), (wkv_h[:, CH:], wkv_l[:, CH:]))]
                    up(pbank[r % 4][:], pairs, plain_done)
                    if j == 1 and n + 1 < NCH:
                        sum_squares(n + 1)
                    if j % 3 == 2:
                        m = j // 3
                        if n or m >= 2:
                            pe.wait_ge(rot_parts, 4 * n + m - 1)
                        cols = slice(order[m] * P, (order[m] + 1) * P)
                        pairs = [((wq_h[:, k, cols], wq_l[:, k, cols]), (norm_h[:, u, k], norm_l[:, u, k]))
                                 for k in range(2)]
                        up(rbank[m % 2][:], pairs, rot_done)

        @block.scalar
        def _(act):
            act.wait_ge(w_loaded, 48)
            act.activation(wq_h[:], wq_raw[:], ACT.Copy).then_inc(norm_high, 1)
            act.activation(wkv_h[:], wkv_raw[:], ACT.Copy).then_inc(norm_high, 1)
            act.wait_ge(consts, 2)

            def roots(n):
                if n:
                    act.wait_ge(norm_done, 3 * n)
                for j, width in ((0, QL), (1, KVL)):
                    act.wait_ge(ssq_done, 2 * n + j + 1)
                    act.activation(rstd[:, j], ssq[j][:], ACT.Sqrt, bias=eps[:, 0:1], scale=1.0 / width
                                   ).then_inc(root_done, 1)

            def high_parts(n):
                for k in range(3):
                    act.wait_ge(norm_done, 3 * n + k + 1)
                    if n >= 2:
                        act.wait_ge(plain_done, USES * (n - 1))
                        act.wait_ge(rot_done, 4 * (n - 1))
                    act.activation(norm_h[:, n % 2, k], norm[:, k], ACT.Copy).then_inc(norm_high, 1)

            roots(0)
            high_parts(0)
            for n in range(NCH):
                u = n % 2
                if n >= 2:
                    act.wait_ge(v_stored[u], 16 * (n // 2))
                for m in range(NCH):
                    r = USES * n + m
                    act.wait_ge(plain_done, r + 1)
                    act.activation(v_out[:, u, m], pbank[r % 4][:], ACT.Copy).then_inc(plain_out, 1)
                if n >= 2:
                    act.wait_ge(stored[u], 16 * NST * (n // 2))
                for j in range(PLAIN):
                    r = USES * n + NCH + j
                    act.wait_ge(plain_done, r + 1)
                    act.activation(plain[:, u, j], pbank[r % 4][:], ACT.Copy).then_inc(plain_out, 1)
                    if j == 2 and n + 1 < NCH:
                        roots(n + 1)
                if n + 1 < NCH:
                    high_parts(n + 1)

        @block.vector
        def _(dve):
            dve.wait_ge(norm_high, 2)
            dve.tensor_tensor(wq_l[:], wq_raw[:], as_f32(wq_h[:]), ALU.subtract).then_inc(w_split, 1)
            dve.tensor_tensor(wkv_l[:], wkv_raw[:], as_f32(wkv_h[:]), ALU.subtract).then_inc(w_split, 1)

            def invert(n, j):
                dve.wait_ge(root_done, 2 * n + j + 1)
                dve.reciprocal(rstd[:, j], rstd[:, j]).then_inc(rstd_done, 1)

            def norms(n):
                dve.wait_ge(lat_loaded[n % 2], 16 * (n // 2 + 1))
                dve.wait_ge(rstd_done, 2 * (n + 1))
                if n:
                    dve.wait_ge(norm_high, 2 + 3 * n)
                for k in range(3):
                    dve.scalar_tensor_tensor(out=norm[:, k], in0=lat[:, n % 2, k], scalar=gain[:, k:k + 1],
                                             in1=rstd[:, k // 2], op0=ALU.mult, op1=ALU.mult
                                             ).then_inc(norm_done, 1)

            def low_parts(n):
                for k in range(3):
                    dve.wait_ge(norm_high, 2 + 3 * n + k + 1)
                    dve.tensor_tensor(norm_l[:, n % 2, k], norm[:, k], as_f32(norm_h[:, n % 2, k]),
                                      ALU.subtract).then_inc(norm_low, 1)

            invert(0, 0)
            invert(0, 1)
            norms(0)
            low_parts(0)
            for n in range(NCH):
                u = n % 2
                dve.wait_ge(rope_loaded[u], 32 * (n // 2 + 1))
                if n >= 2:
                    dve.wait_ge(stored[u], 16 * NST * (n // 2))
                if n:
                    dve.wait_ge(rot_out, 3 * n)
                dve.tensor_tensor(krot[:, u], kr[:, u, 0], cs[0:ROPE, u, 0], ALU.mult
                                  ).then_inc(krot_parts, 1)
                dve.tensor_tensor(kpart[:, u], kr[:, u, 1], cs[0:ROPE, u, 1], ALU.mult
                                  ).then_inc(krot_parts, 1)
                for m in range(4):
                    dve.wait_ge(rot_done, 4 * n + m + 1)
                    dst = part[:, m // 2] if m % 2 else rot[:, u, m // 2]
                    dve.tensor_tensor(dst, rbank[m % 2][:], cs[:, u, m % 2], ALU.mult
                                      ).then_inc(rot_parts, 1)
                    if n + 1 < NCH:
                        if m < 2:
                            invert(n + 1, m)
                        if m == 2:
                            norms(n + 1)
                if n + 1 < NCH:
                    low_parts(n + 1)


ORDER = [1, 3, 2, 0]
START = [sum(4 * (g + 1) for g in ORDER[:o]) for o in range(4)]
PER_HEAD = sum(4 * (g + 1) for g in ORDER)
KEEPS = 4
WT = 4
LATE = 5
EXP_LAG = 5
LEAD, TAIL = 5, 4
PIECES = 12
HEAD = 64


def attend(nc, soft, q_src, k_src, v_src, projT, gate_block, ogT, ident):
    scale = float(NOPE + ROPE) ** -0.5 if soft else float(SBD) ** -0.5
    rows = NOPE + ROPE if soft else P
    score_banks, turn_banks = 2, 4
    loads = 5
    items = PER_HEAD + 4 if soft else PER_HEAD
    per_pos = [4 * (g + 1) + (1 if soft else 0) for g in ORDER]
    item_at = [sum(per_pos[:o]) for o in range(4)]

    with Scope(nc) as c:
        n = "mla_" if soft else "sb_"
        q_raw = c.sb(n + "q_raw", [rows, S])
        k_raw = c.sb(n + "k_raw", [rows, S])
        v_raw = c.sb(n + "v_raw", [P, TT, HEAD])
        q_hi = [c.sb(n + f"q_hi{u}", [rows, S], F32R) for u in range(2)]
        q_lo = [c.sb(n + f"q_lo{u}", [rows, S], F32R) for u in range(2)] if soft else None
        k_hi = [c.sb(n + f"k_hi{u}", [rows, S], F32R) for u in range(2)]
        k_lo = [c.sb(n + f"k_lo{u}", [rows, S], F32R) for u in range(2)]
        v_two = [c.sb(n + f"v_two{u}", [P, TT, 2 * HEAD], F32R) for u in range(2)]
        w = [c.sb(n + "w_even", [P, 4, 3 * CH]), c.sb(n + "w_odd", [P, 4, 4 * CH])]
        wT_hi = [c.sb(n + f"wT_hi{b}", [P, CH], F32R) for b in range(WT)]
        wT_lo = [c.sb(n + f"wT_lo{b}", [P, CH], F32R) for b in range(WT)]
        gate = c.sb(n + "gate", [HEAD, 2, CH])
        o_low = c.sb(n + "o_low", [HEAD, 2, CH])
        o_sum = c.sb(n + "o_sum", [HEAD, 2, CH])
        og = c.sb(n + "og", [HEAD, 2, CH])
        mask = c.sb(n + "mask", [P, P])
        ones = c.sb(n + "ones", [P, P])
        if soft:
            maxes = c.sb(n + "maxes", [P, 16, 4])
            neg_max = c.sb(n + "neg_max", [P, 16])
            sums = c.sb(n + "sums", [P, 16])
            top = c.sb(n + "top", [P, 16])
            inv_sum = c.sb(n + "inv_sum", [P, 16])
            diag = c.sb(n + "diag", [P, 4, P])
            gate_n = c.sb(n + "gate_n", [HEAD, 2, CH])
        else:
            keep = c.sb(n + "keep", [P, KEEPS, CH])
            after = c.sb(n + "after", [P, 2, S + 1])
        score = [c.ps(n + f"score{b}", [P, CH]) for b in range(score_banks)]
        turn = [c.ps(n + f"turn{b}", [P, CH]) for b in range(turn_banks)]
        o_ps = [c.ps(n + f"o_ps{b}", [P, CH]) for b in range(2)]

        consts = c.sem(n + "consts")
        raw_loaded = c.sem(n + "raw_loaded")
        split_high = c.sem(n + "split_high")
        split = c.sem(n + "split")
        scored = c.sem(n + "scored")
        masked = c.sem(n + "masked")
        top_done = c.sem(n + "top_done")
        shift_ready = c.sem(n + "shift_ready")
        freed = c.sem(n + "freed")
        scanned = c.sem(n + "scanned")
        weighted = c.sem(n + "weighted")
        exp_done = c.sem(n + "exp_done")
        inverted = c.sem(n + "inverted")
        diag_ready = c.sem(n + "diag_ready")
        turned = c.sem(n + "turned")
        turn_high = c.sem(n + "turn_high")
        turn_freed = c.sem(n + "turn_freed")
        pv_done = c.sem(n + "pv_done")
        low_copied = c.sem(n + "low_copied")
        o_summed = c.sem(n + "o_summed")
        gated = c.sem(n + "gated")
        gate_loaded = [c.sem(n + f"gate_loaded{b}") for b in range(2)]
        stored = [c.sem(n + f"og_stored{b}") for b in range(2)]
        passed = c.sem(n + "passed")
        block = c.block()

        def weights_ready(h, o):
            return (exp_done, 16 * h + 4 * o + 4) if soft else (weighted, 2 + number(h, o, 3, ORDER[o] + 1))

        def heads(engine, body):
            with engine.Fori(0, H // 2 - 1) as i:
                body(i, 0, False)
                body(i, 1, False)
            body(H // 2 - 1, 0, False)
            body(H // 2 - 1, 1, True)

        def chunks(g, t):
            both = [(k, CH if k < g else (t + 1) * P) for k in range(g + 1)]
            return both if soft else both[::-1]

        def schedule(o, nxt):
            tiles = [("tile", j) for j in range(4 * (ORDER[o] + 1))] + ([("sums",)] if soft else [])
            if not nxt:
                return tiles
            g = ORDER[(o + 1) % 4]
            new = [("chunk", t, j, k, width) for t in range(4) for j, (k, width) in enumerate(chunks(g, t))]
            alone = min(TAIL, len(tiles) - 1)
            mixed, tiles, end = new[:LEAD], tiles[:-alone], tiles[-alone:]
            new, a, b = new[LEAD:], 0, 0
            for _ in range(len(tiles) + len(new)):
                if b < len(new) and (a == len(tiles) or b * len(tiles) < a * len(new)):
                    mixed.append(new[b])
                    b += 1
                else:
                    mixed.append(tiles[a])
                    a += 1
            return mixed + end

        def timeline(last, **lags):
            steps, base = [], 0
            for o in range(4):
                slots = schedule(o, o < 3 or not last)
                end = base + len(slots)
                for s, (what, *args) in enumerate(slots, base):
                    if what == "chunk":
                        kinds = ("scores", "to_sbuf", "exp", "sigmoids", "scan", "weigh")
                        args = [(o + 1) % 4] + args
                    elif what == "sums":
                        kinds, args = ("sums", "gate_n"), [o]
                    else:
                        kinds = ("turn", "high", "low", "times_v")
                        if args[0] == 0:
                            kinds += ("invert", "diagonal")
                        if args[0] == 4 * ORDER[o] + 3:
                            kinds += ("o_low", "o_sum", "gated")
                        args = [o] + args
                    for kind in kinds:
                        if kind in lags:
                            at = s + lags[kind]
                            steps.append((min(at, end - 0.5) if what == "chunk" else at, at, (kind, *args)))
                if "piece" in lags and o < 3 and not last:
                    for p in range(4):
                        at = base + len(slots) * p / 4 + lags["piece"]
                        steps.append((at, at, ("piece", o, 4 * o + p)))
                base = end
            return [step for *_, step in sorted(steps, key=lambda step: step[:2])]

        def all_chunks(o):
            return [(t, j, k, width) for t in range(4) for j, (k, width) in enumerate(chunks(ORDER[o], t))]

        def number(h, o, t, j=0):
            return PER_HEAD * h + START[o] + t * (ORDER[o] + 1) + j

        def following(h, u, o, last):
            if o < 3:
                return h, u, o + 1
            return None if last else (h + 1, 1 - u, 0)

        def piece(u, p):
            if p >= 8:
                tiles = slice((p - 8) * 4, (p - 7) * 4)
                src, high = v_raw[:, tiles], v_two[u][:, tiles, 0:HEAD]
                return (src, high), (src, high, v_two[u][:, tiles, HEAD:])
            cols = slice(p // 2 * CH, (p // 2 + 1) * CH)
            raw, hi, lo = ((q_raw, q_hi, q_lo), (k_raw, k_hi, k_lo))[p % 2]
            src, high = raw[:, cols], hi[u][:, cols]
            if lo is None:
                return (src, high), (raw[SBD:, cols], hi[u][SBD:, cols], hi[u][SBD:, cols])
            return (src, high), (src, high, lo[u][:, cols])

        def piece_free(engine, h, p):
            if p == 0:
                engine.wait_ge(raw_loaded, 16 * loads * (h + 2))
                engine.wait_ge(scored, number(h, 0, 3, ORDER[0] + 1))
            if p == 8:
                engine.wait_ge(pv_done, WT + PER_HEAD * h)

        @block.sync
        def _(sp):
            def load_operands(h):
                if soft:
                    sp.dma_start(q_raw[0:NOPE], q_src[0][bass.ds(h * NOPE, NOPE)]).then_inc(raw_loaded, 16)
                    sp.dma_start(q_raw[NOPE:], q_src[1][bass.ds(h * ROPE, ROPE)]).then_inc(raw_loaded, 16)
                    sp.dma_start(k_raw[0:NOPE], k_src[0][bass.ds(h * NOPE, NOPE)]).then_inc(raw_loaded, 16)
                    sp.dma_start(k_raw[NOPE:], k_src[1]).then_inc(raw_loaded, 16)
                else:
                    for half in range(2):
                        part = slice(half * SBD, (half + 1) * SBD)
                        sp.dma_start(q_raw[part], q_src[bass.ds(h * SBD, SBD)]).then_inc(raw_loaded, 16)
                        sp.dma_start(k_raw[part], k_src[bass.ds(h * SBD, SBD)]).then_inc(raw_loaded, 16)
                sp.dma_start(v_raw[:], v_src[:, bass.ds(h * HEAD, HEAD)].rearrange("(t p) f -> p t f", p=P)
                             ).then_inc(raw_loaded, 16)

            def load_gate(i, u, o):
                g = ORDER[o]
                sp.wait_ge(gated, 4 * (2 * i + u) + o + 1)
                sp.sem_inc(passed, 1)
                sp.dma_start(gate[:, o % 2],
                             projT[bass.ds(gate_block + i, 1), u * HEAD:(u + 1) * HEAD, g * CH:(g + 1) * CH
                                   ].squeeze(0)).then_inc(gate_loaded[o % 2], 16)

            def body(i, u, last):
                h = 2 * i + u
                for o in range(4):
                    g = ORDER[o]
                    nxt = following(h, u, o, last)
                    if nxt:
                        load_gate(i + int(o == 3 and u == 1), nxt[1], nxt[2])
                    sp.wait_ge(gated, 2 + 4 * h + o + 1)
                    sp.sem_inc(passed, 1)
                    sp.dma_start(ogT[bass.ds(h * HEAD, HEAD), g * CH:(g + 1) * CH], og[:, o % 2]
                                 ).then_inc(stored[o % 2], 16)
                    if o == 2 and not last and not (isinstance(i, int) and u == 0):
                        sp.wait_ge(split, PIECES * (h + 2))
                        sp.sem_inc(passed, 1)
                        load_operands(h + 2)

            for b in range(2):
                sp.sem_inc(stored[b], 16)
            load_operands(0)
            load_gate(0, 0, 0)
            sp.wait_ge(split, PIECES)
            load_operands(1)
            heads(sp, body)
            for b in range(2):
                sp.wait_ge(stored[b], 16 + 16 * 2 * H)

        @block.gpsimd
        def _(pool):
            pool.sem_inc(weighted, 2)
            pool.sem_inc(gated, 2)
            pool.memset(mask[:], BIG).then_inc(consts, 1)
            pool.memset(ones[:], 1.0).then_inc(consts, 1)
            if not soft:
                pool.memset(after[:, :, S:S + 1], 1.0).then_inc(consts, 1)
            pool.wait_ge(consts, 2 if soft else 3)
            pool.affine_select(out=mask[:], in_=mask[:], compare_op=ALU.is_ge if soft else ALU.is_gt,
                               fill=-BIG, base=0, pattern=[[-1, P]], channel_multiplier=1
                               ).then_inc(consts, 1)

            def weigh(h, o, t, j, k, width):
                at, off = k * CH, S - (4 * ORDER[o] + t + 1) * P
                pool.wait_ge(scanned, KEEPS + number(h, o, t, j) + 1)
                pool.tensor_tensor(w[o % 2][:, t, at:at + width], w[o % 2][:, t, at:at + width],
                                   after[:, t % 2, off + at + 1:off + at + width + 1], ALU.mult
                                   ).then_inc(weighted, 1)

            def body(i, u, last):
                h = 2 * i + u
                weighed = number(h, 0, 3, ORDER[0] + 1)
                for kind, o, *args in timeline(last, piece=0, diagonal=2, weigh=4, gated=LATE + 3):
                    if kind == "piece":
                        p = args[0]
                        (src, high), (src_l, high_l, low) = piece(1 - u, p)
                        if soft:
                            piece_free(pool, h, p)
                            one = ones[0:src.shape[0], 0:1]
                            one = (one.broadcast_to([src.shape[0], CH]) if p < 8
                                   else one.unsqueeze(2).broadcast_to([P, 4, HEAD]))
                            pool.tensor_tensor(high, src, one, ALU.mult).then_inc(split_high, 1)
                        elif p % 2 == 0 and p < 8:
                            pool.wait_ge(weighted, 2 + weighed)
                        pool.wait_ge(split_high, PIECES * (h + 1) + p + 1)
                        pool.tensor_tensor(low, src_l, as_f32(high_l), ALU.subtract).then_inc(split, 1)
                        if p < 8 and not soft:
                            pool.wait_ge(split, PIECES * (h + 1) + p + 1)
                    if kind == "diagonal" and soft:
                        for tt in range(4):
                            pool.wait_ge(inverted, 4 * h + o + 1)
                            pool.wait_ge(turned, items * h + item_at[o] + 1)
                            at = 4 * o + tt
                            pool.tensor_tensor(diag[:, tt], ident[:],
                                               inv_sum[:, at:at + 1].broadcast_to([P, P]), ALU.mult
                                               ).then_inc(diag_ready, 1)
                    if kind == "weigh" and not soft:
                        nxt = following(h, u, (o - 1) % 4, last)
                        weigh(nxt[0], *([o] + args))
                        weighed = number(nxt[0], o, *args[:2]) + 1
                    if kind == "gated":
                        seq = 4 * h + o
                        pool.wait_ge(stored[o % 2], 16 * (2 * h + o // 2 + 1))
                        if soft:
                            pool.wait_ge(turn_freed, turn_banks + items * h + item_at[o] + per_pos[o])
                        else:
                            pool.wait_ge(gate_loaded[o % 2], 16 * (2 * h + o // 2 + 1))
                        pool.wait_ge(o_summed, 2 + seq + 1)
                        by = gate_n if soft else gate
                        pool.tensor_tensor(og[:, o % 2], o_sum[:, o % 2], by[:, o % 2], ALU.mult
                                           ).then_inc(gated, 1)

            if not soft:
                for it in all_chunks(0):
                    weigh(0, 0, *it)
            heads(pool, body)

        @block.tensor
        def _(pe):
            pe.sem_inc(pv_done, WT)
            pe.wait_ge(consts, 3 if soft else 4)

            def scores(h, u, o, t, j, key, width):
                g = ORDER[o]
                q_cols = slice((4 * g + t) * P, (4 * g + t + 1) * P)
                if t == 0 and j == 0 and o < 2:
                    pe.wait_ge(split, PIECES * h + 2 * (g + 1))
                pe.wait_ge(freed, number(h, o, t, j) + 1)
                bank = score[number(0, o, t, j) % score_banks][:, 0:width]
                keys = slice(key * CH, key * CH + width)
                if soft:
                    passes = [(q_hi, k_hi), (q_hi, k_lo), (q_lo, k_hi)]
                else:
                    passes = [(q_hi, k_hi), (q_hi, k_lo)]
                for m, (a, b) in enumerate(passes):
                    mm = pe.matmul(bank, a[u][:, q_cols], b[u][:, keys], start=(m == 0),
                                   stop=(m == len(passes) - 1))
                mm.then_inc(scored, 1)

            def times_v(h, u, o, j):
                g = ORDER[o]
                seq = PER_HEAD * h + START[o] + j
                b = (START[o] + j) % WT
                first = max(0, j - 4 * g) * P
                pe.wait_ge(turn_freed, turn_banks + items * h + item_at[o] + j + 1)
                if j == 0 and o == 0:
                    pe.wait_ge(split, PIECES * (h + 1))
                if j == 0:
                    pe.wait_ge(o_summed, 4 * h + o + 1)
                for m, part in enumerate((wT_hi, wT_lo)):
                    mm = pe.matmul(o_ps[o % 2][:, first:], v_two[u][:, j], part[b][:, first:],
                                   start=(j == 0 and m == 0), stop=(j == 4 * g + 3 and m == 1))
                mm.then_inc(pv_done, 1)

            def body(i, u, last):
                h = 2 * i + u
                for kind, o, *args in timeline(last, scores=0, turn=0, sums=0, times_v=LATE):
                    if kind == "scores":
                        nxt = following(h, u, (o - 1) % 4, last)
                        scores(nxt[0], nxt[1], *([o] + args))
                    if kind == "sums":
                        it = item_at[o] + 4 * (ORDER[o] + 1)
                        pe.wait_ge(turn_freed, items * h + it + 1)
                        pe.wait_ge(diag_ready, 16 * h + 4 * o + 4)
                        for tt in range(4):
                            mm = pe.matmul(turn[it % turn_banks][:, tt * P:(tt + 1) * P], ones[:], diag[:, tt],
                                           start=True, stop=True)
                        mm.then_inc(turned, 1)
                    if kind == "turn":
                        j = args[0]
                        it = item_at[o] + j
                        if j == 0:
                            pe.wait_ge(*weights_ready(h, o))
                        pe.wait_ge(turn_freed, items * h + it + 1)
                        for tt in range(max(0, j - 4 * ORDER[o]), 4):
                            mm = pe.transpose(turn[it % turn_banks][:, tt * P:(tt + 1) * P],
                                              w[o % 2][:, tt, j * P:(j + 1) * P], ident[:])
                        mm.then_inc(turned, 1)
                    if kind == "times_v":
                        times_v(h, u, o, args[0])

            for it in all_chunks(0):
                scores(0, 0, 0, *it)
            heads(pe, body)

        @block.scalar
        def _(act):
            if not soft:
                act.sem_inc(freed, score_banks)

            def weights(h, o, t, j, key, width):
                g, pos = ORDER[o], 4 * o + t
                if soft:
                    if j == g:
                        row = w[o % 2][:, t, 0:(4 * g + t + 1) * P]
                        act.wait_ge(shift_ready, 16 * h + pos + 1)
                        act.activation(row, row, ACT.Exp, scale=scale, bias=neg_max[:, pos:pos + 1],
                                       accum_out=sums[:, pos:pos + 1]).then_inc(exp_done, 1)
                    return
                if key == g:
                    act.wait_ge(masked, 16 * h + pos + 1)
                else:
                    act.wait_ge(scored, number(h, o, t, j) + 1)
                act.wait_ge(scanned, number(h, o, t, j) + 1)
                r = number(0, o, t, j) % KEEPS
                bank = score[number(0, o, t, j) % score_banks][:, 0:width]
                act.activation(keep[:, r, 0:width], bank, ACT.Sigmoid, scale=-scale)
                act.activation(w[o % 2][:, t, key * CH:key * CH + width], bank, ACT.Sigmoid, scale=scale
                               ).then_inc(freed, 1)

            def body(i, u, last):
                h = 2 * i + u
                for kind, o, *args in timeline(last, high=0.5, o_low=LATE + 1, **({"exp": EXP_LAG} if soft
                                               else {"sigmoids": 2, "piece": 0})):
                    if kind == "piece":
                        piece_free(act, h, args[0])
                        src, high = piece(1 - u, args[0])[0]
                        act.activation(high, src, ACT.Copy).then_inc(split_high, 1)
                    if kind in ("exp", "sigmoids"):
                        nxt = following(h, u, (o - 1) % 4, last)
                        weights(nxt[0], *([o] + args))
                    if kind == "high":
                        j = args[0]
                        it, b = item_at[o] + j, (START[o] + j) % WT
                        first = max(0, j - 4 * ORDER[o]) * P
                        act.wait_ge(turned, items * h + it + 1)
                        act.wait_ge(pv_done, PER_HEAD * h + START[o] + j + 1)
                        act.activation(wT_hi[b][:, first:], turn[it % turn_banks][:, first:], ACT.Copy
                                       ).then_inc(turn_high, 1)
                    if kind == "o_low":
                        act.wait_ge(pv_done, WT + PER_HEAD * h + START[o] + 4 * (ORDER[o] + 1))
                        act.activation(o_low[:, o % 2], o_ps[o % 2][HEAD:], ACT.Copy).then_inc(low_copied, 1)

            act.wait_ge(raw_loaded, 16 * loads)
            for p in range(PIECES):
                src, high = piece(0, p)[0]
                act.activation(high, src, ACT.Copy).then_inc(split_high, 1)
            for it in all_chunks(0):
                weights(0, 0, *it)
            heads(act, body)

        @block.vector
        def _(dve):
            dve.sem_inc(turn_freed, turn_banks)
            dve.sem_inc(o_summed, 2)
            if not soft:
                dve.sem_inc(scanned, KEEPS)
            dve.wait_ge(consts, 3 if soft else 4)

            def after_scores(h, o, t, j, key, width):
                g, pos = ORDER[o], 4 * o + t
                bank = score[number(0, o, t, j) % score_banks]
                dve.wait_ge(scored, number(h, o, t, j) + 1)
                if key == g:
                    diagonal = bank[:, t * P:(t + 1) * P]
                    dve.tensor_tensor(diagonal, diagonal, mask[:], ALU.min).then_inc(masked, 1)
                if soft:
                    if key == g:
                        dve.wait_ge(masked, 16 * h + pos + 1)
                    dve.tensor_scalar(w[o % 2][:, t, key * CH:key * CH + width], bank[:, 0:width], 1.0, None,
                                      ALU.mult, ALU.max, accum_out=maxes[:, pos, key:key + 1]
                                      ).then_inc(freed, 1)
                    if key == g:
                        dve.wait_ge(freed, score_banks + number(h, o, t, g + 1))
                        dve.tensor_reduce(top[:, pos:pos + 1], maxes[:, pos, 0:g + 1], AX_X, ALU.max
                                          ).then_inc(top_done, 1)
                        dve.wait_ge(top_done, 16 * h + pos + 1)
                        dve.tensor_scalar(neg_max[:, pos:pos + 1], top[:, pos:pos + 1], -scale, None,
                                          ALU.mult).then_inc(shift_ready, 1)

            def scan(h, o, t, j, key, width):
                g = ORDER[o]
                off = S - (4 * g + t + 1) * P
                r = number(0, o, t, j) % KEEPS
                dve.wait_ge(freed, score_banks + number(h, o, t, j) + 1)
                if j == 0:
                    prev = number(h, o, t - 2) if t >= 2 else (
                        number(h, o - 1, t + 2) if o else number(h, 0, 0) - (2 - t) * (ORDER[3] + 1))
                    size = ORDER[o if t >= 2 else o - 1] + 1
                    dve.wait_ge(weighted, 2 + prev + size)
                else:
                    dve.wait_ge(scanned, KEEPS + number(h, o, t, j))
                at = off + key * CH
                dve.tensor_tensor_scan(after[:, t % 2, at:at + width][:, ::-1], keep[:, r, 0:width][:, ::-1],
                                       keep[:, r, 0:width][:, ::-1],
                                       after[:, t % 2, at + width:at + width + 1], ALU.mult, ALU.bypass
                                       ).then_inc(scanned, 1)

            def body(i, u, last):
                h = 2 * i + u
                for kind, o, *args in timeline(last, to_sbuf=0.5, scan=3, low=1, invert=1.5, gate_n=1,
                                               o_sum=LATE + 2):
                    if kind == "to_sbuf":
                        nxt = following(h, u, (o - 1) % 4, last)
                        after_scores(nxt[0], *([o] + args))
                    if kind == "scan" and not soft:
                        nxt = following(h, u, (o - 1) % 4, last)
                        scan(nxt[0], *([o] + args))
                    if kind == "low":
                        j = args[0]
                        it, b = item_at[o] + j, (START[o] + j) % WT
                        first = max(0, j - 4 * ORDER[o]) * P
                        dve.wait_ge(turn_high, PER_HEAD * h + START[o] + j + 1)
                        dve.tensor_tensor(wT_lo[b][:, first:], turn[it % turn_banks][:, first:],
                                          as_f32(wT_hi[b][:, first:]), ALU.subtract
                                          ).then_inc(turn_freed, 1)
                    if kind == "invert" and soft:
                        at = 4 * o
                        dve.wait_ge(*weights_ready(h, o))
                        dve.reciprocal(inv_sum[:, at:at + 4], sums[:, at:at + 4]).then_inc(inverted, 1)
                    if kind == "gate_n":
                        it = item_at[o] + 4 * (ORDER[o] + 1)
                        dve.wait_ge(gate_loaded[o % 2], 16 * (2 * h + o // 2 + 1))
                        dve.wait_ge(gated, 4 * h + o + 1)
                        dve.wait_ge(turned, items * h + it + 1)
                        dve.tensor_tensor(gate_n[:, o % 2], turn[it % turn_banks][0:HEAD], gate[:, o % 2],
                                          ALU.mult).then_inc(turn_freed, 1)
                    if kind == "o_sum":
                        dve.wait_ge(low_copied, 4 * h + o + 1)
                        dve.wait_ge(gated, 4 * h + o + 1)
                        dve.tensor_tensor(o_sum[:, o % 2], o_ps[o % 2][0:HEAD], o_low[:, o % 2], ALU.add
                                          ).then_inc(o_summed, 1)

            if soft:
                dve.sem_inc(freed, score_banks)
            for p in range(PIECES):
                dve.wait_ge(split_high, p + 1)
                src, high, low = piece(0, p)[1]
                dve.tensor_tensor(low, src, as_f32(high), ALU.subtract).then_inc(split, 1)
            for it in all_chunks(0):
                after_scores(0, 0, *it)
                if not soft:
                    scan(0, 0, *it)
            heads(dve, body)


def attend_memory(nc, mem, w_mem, projT, ogT, ident):
    scale = float(MD) ** -0.5
    ITEMS = MT + 1
    with Scope(nc) as c:
        mem_raw = c.sb("mem_raw", [P, MT, D])
        memT_hi = c.sb("memT_hi", [P, KT, MEM], F32R)
        memT_lo = c.sb("memT_lo", [P, KT, MEM], F32R)
        w_raw = c.sb("wm_raw", [P, 2, D])
        w_hi = c.sb("wm_hi", [P, KT, D], F32R)
        w_lo = c.sb("wm_lo", [P, KT, D], F32R)
        k_hi = c.sb("mem_k_hi", [P, MH, MEM], F32R)
        k_lo = c.sb("mem_k_lo", [P, MH, MEM], F32R)
        v_hi = c.sb("mem_v_hi", [P, MT, MH * MD], F32R)
        v_lo = c.sb("mem_v_lo", [P, MT, MH * MD], F32R)
        q_raw = c.sb("mem_q_raw", [P, MH, CH])
        q_hi = [c.sb(f"mem_q_hi{b}", [P, CH], F32R) for b in range(MH)]
        q_lo = [c.sb(f"mem_q_lo{b}", [P, CH], F32R) for b in range(MH)]
        gate = c.sb("mem_gate", [P, MH, CH])
        w = c.sb("mem_w", [P, 2, 4, MEM])
        wT_hi = [c.sb(f"mem_wT_hi{b}", [P, CH], F32R) for b in range(2)]
        wT_lo = [c.sb(f"mem_wT_lo{b}", [P, CH], F32R) for b in range(2)]
        top = c.sb("mem_top", [P, 2, 4])
        neg_max = c.sb("mem_neg_max", [P, 2, 4])
        sums = c.sb("mem_sums", [P, 2, 4])
        inv_sum = c.sb("mem_inv_sum", [P, 2, 4])
        diag = c.sb("mem_diag", [P, 2, 4, P])
        gate_n = c.sb("mem_gate_n", [P, 2, CH])
        og = c.sb("mem_og", [P, 2, CH])
        ones = c.sb("mem_ones", [P, P])
        score = [c.ps(f"mem_score{b}", [P, 2, 2, MEM]) for b in range(2)]
        turn = [c.ps(f"mem_turn{b}", [P, CH]) for b in range(2)]
        o_ps = [c.ps(f"mem_o{b}", [P, CH]) for b in range(2)]

        mem_loaded = c.sem("mem_loaded")
        wm_loaded = [c.sem(f"wm_loaded{b}") for b in range(2)]
        ones_set = c.sem("mem_ones_set")
        wm_high = c.sem("wm_high")
        wm_low = c.sem("wm_low")
        mem_turned = c.sem("mem_turned")
        mem_high = c.sem("mem_high")
        mem_low = c.sem("mem_low")
        kv_done = c.sem("mem_kv_done")
        kv_high = c.sem("mem_kv_high")
        kv_low = c.sem("mem_kv_low")
        q_loaded = [c.sem(f"mem_q_loaded{b}") for b in range(MH)]
        gate_loaded = [c.sem(f"mem_gate_loaded{b}") for b in range(MH)]
        q_high = c.sem("mem_q_high")
        q_split = c.sem("mem_q_split")
        scored = c.sem("mem_scored")
        top_done = c.sem("mem_top_done")
        shift_ready = c.sem("mem_shift_ready")
        exp_done = c.sem("mem_exp_done")
        inverted = c.sem("mem_inverted")
        diag_ready = c.sem("mem_diag_ready")
        turned = c.sem("mem_item_turned")
        turn_high = c.sem("mem_turn_high")
        turn_freed = c.sem("mem_turn_freed")
        pv_done = c.sem("mem_pv_done")
        gated = c.sem("mem_gated")
        stored = [c.sem(f"mem_stored{b}") for b in range(2)]
        passed = c.sem("mem_passed")
        block = c.block()

        prep = [turn[0], turn[1], o_ps[0], o_ps[1]]
        NPREP = KT // 2

        def chunks_of(engine, body):
            with engine.Fori(0, NCH - 1) as n:
                body(n, False)
            body(NCH - 1, True)

        def following(n, h, last):
            if h < MH - 1:
                return n, h + 1
            return None if last else (n + 1, 0)

        @block.sync
        def _(sp):
            sp.dma_start(mem_raw[:], mem.rearrange("b (t p) d -> p (b t) d", p=P)).then_inc(mem_loaded, 16)
            for k in range(KT):
                if k >= 2:
                    sp.wait_ge(wm_low, k - 1)
                sp.dma_start(w_raw[:, k % 2], w_mem[k]).then_inc(wm_loaded[k % 2], 16)
            for b in range(2):
                sp.sem_inc(stored[b], 16)

            def load(n, h):
                cols = bass.ds(n * CH, CH)
                sp.dma_start(q_raw[:, h], projT[B_COPY + 12 + h, :, cols]).then_inc(q_loaded[h], 16)
                sp.dma_start(gate[:, h], projT[B_GATE + 8 + h, :, cols]).then_inc(gate_loaded[h], 16)

            def body(n, last):
                for h in range(MH):
                    sp.wait_ge(gated, 2 + MH * n + h + 1)
                    sp.sem_inc(passed, 1)
                    sp.dma_start(ogT[h * MD:(h + 1) * MD, bass.ds(n * CH, CH)], og[:, h % 2]
                                 ).then_inc(stored[h % 2], 16)
                    if not last:
                        load(n + 1, h)

            for h in range(MH):
                load(0, h)
            chunks_of(sp, body)
            for b in range(2):
                sp.wait_ge(stored[b], 16 + 16 * NCH * MH // 2)

        @block.gpsimd
        def _(pool):
            pool.memset(ones[:], 1.0).then_inc(ones_set, 1)
            pool.wait_ge(ones_set, 1)

            def split_q(n, h):
                pool.wait_ge(q_loaded[h], 16 * (n + 1))
                pool.tensor_tensor(q_hi[h][:], q_raw[:, h], ones[:, 0:1].broadcast_to([P, CH]), ALU.mult
                                   ).then_inc(q_high, 1)
                pool.wait_ge(q_high, MH * n + h + 1)
                pool.tensor_tensor(q_lo[h][:], q_raw[:, h], as_f32(q_hi[h][:]), ALU.subtract
                                   ).then_inc(q_split, 1)

            def body(n, last):
                for h in range(MH):
                    b, unit = h % 2, MH * n + h
                    for t in range(4):
                        pool.wait_ge(inverted, unit + 1)
                        pool.tensor_tensor(diag[:, b, t], ident[:],
                                           inv_sum[:, b, t:t + 1].broadcast_to([P, P]), ALU.mult
                                           ).then_inc(diag_ready, 1)
                    if not (last and h >= MH - 2):
                        split_q(n + int(h >= MH - 2), (h + 2) % MH)

            split_q(0, 0)
            split_q(0, 1)
            chunks_of(pool, body)

        @block.tensor
        def _(pe):
            pe.sem_inc(pv_done, 2)
            pe.wait_ge(mem_loaded, 16)
            for m in range(NPREP):
                for j in range(2):
                    for t in range(MT):
                        at = (2 * j + t) * P
                        k = 2 * m + j
                        mm = pe.transpose(prep[m][:, at:at + P], mem_raw[:, t, k * P:(k + 1) * P], ident[:])
                mm.then_inc(mem_turned, 1)
            for m in range(MH + MT):
                bank = prep[m % 4][:]
                if m < 4:
                    pe.wait_ge(mem_low, m + 1)
                    bank = bank[:, 0:MEM]
                else:
                    pe.wait_ge(kv_low, m - 3)
                for k in range(KT):
                    if m == 0:
                        pe.wait_ge(mem_low, k // 2 + 1)
                        pe.wait_ge(wm_low, k + 1)
                    if m < MH:
                        cols = slice(m * MD, (m + 1) * MD)
                        a, b = (w_hi[:, k, cols], w_lo[:, k, cols]), (memT_hi[:, k], memT_lo[:, k])
                    else:
                        rows, cols = slice((m - MH) * P, (m - MH + 1) * P), slice(MH * MD, D)
                        a = memT_hi[:, k, rows], memT_lo[:, k, rows]
                        b = w_hi[:, k, cols], w_lo[:, k, cols]
                    pe.matmul(bank, a[0], b[0], start=(k == 0), stop=False)
                    pe.matmul(bank, a[0], b[1], start=False, stop=False)
                    mm = pe.matmul(bank, a[1], b[0], start=False, stop=(k == KT - 1))
                mm.then_inc(kv_done, 1)
            pe.wait_ge(kv_low, MH + MT)

            def scores(n, h):
                b, unit = h % 2, MH * n + h
                pe.wait_ge(q_split, unit + 1)
                pe.wait_ge(exp_done, unit + 1)
                for t in range(4):
                    rows = slice(t * P, (t + 1) * P)
                    bank = score[b][:, t // 2, t % 2]
                    pe.matmul(bank, q_hi[h][:, rows], k_hi[:, h], start=True, stop=False)
                    pe.matmul(bank, q_hi[h][:, rows], k_lo[:, h], start=False, stop=False)
                    mm = pe.matmul(bank, q_lo[h][:, rows], k_hi[:, h], start=False, stop=True)
                mm.then_inc(scored, 1)

            def body(n, last):
                for h in range(MH):
                    b, unit = h % 2, MH * n + h
                    nxt = following(n, h, last)
                    feat = slice(h * MD, (h + 1) * MD)
                    pe.wait_ge(exp_done, 2 + unit + 1)
                    for m in range(MT):
                        it = ITEMS * h + m
                        pe.wait_ge(turn_freed, ITEMS * MH * n + it + 1)
                        for t in range(4):
                            mm = pe.transpose(turn[it % 2][:, t * P:(t + 1) * P],
                                              w[:, b, t, m * P:(m + 1) * P], ident[:])
                        mm.then_inc(turned, 1)
                    if nxt:
                        scores(*nxt)
                    it = ITEMS * h + MT
                    pe.wait_ge(turn_freed, ITEMS * MH * n + it + 1)
                    pe.wait_ge(diag_ready, 4 * (unit + 1))
                    for t in range(4):
                        mm = pe.matmul(turn[it % 2][:, t * P:(t + 1) * P], ones[:], diag[:, b, t],
                                       start=True, stop=True)
                    mm.then_inc(turned, 1)
                    pe.wait_ge(gated, unit + 1)
                    for m in range(MT):
                        it = ITEMS * h + m
                        pe.wait_ge(turn_freed, 2 + ITEMS * MH * n + it + 1)
                        pe.matmul(o_ps[b][:], v_hi[:, m, feat], wT_hi[m][:], start=(m == 0), stop=False)
                        pe.matmul(o_ps[b][:], v_hi[:, m, feat], wT_lo[m][:], start=False, stop=False)
                        mm = pe.matmul(o_ps[b][:], v_lo[:, m, feat], wT_hi[m][:], start=False,
                                       stop=(m == MT - 1))
                        mm.then_inc(pv_done, 1)

            pe.wait_ge(ones_set, 1)
            scores(0, 0)
            chunks_of(pe, body)

        @block.scalar
        def _(act):
            for m in range(NPREP):
                act.wait_ge(mem_turned, m + 1)
                act.activation(memT_hi[:, 2 * m:2 * m + 2].rearrange("p k s -> p (k s)"), prep[m][:], ACT.Copy
                               ).then_inc(mem_high, 1)
            for k in range(KT):
                act.wait_ge(wm_loaded[k % 2], 16 * (k // 2 + 1))
                act.activation(w_hi[:, k], w_raw[:, k % 2], ACT.Copy).then_inc(wm_high, 1)
            for m in range(MH + MT):
                act.wait_ge(kv_done, m + 1)
                src, dst = ((prep[m % 4][:, 0:MEM], k_hi[:, m]) if m < MH
                            else (prep[m % 4][:], v_hi[:, m - MH]))
                act.activation(dst, src, ACT.Copy).then_inc(kv_high, 1)

            def exps(n, h):
                b, unit = h % 2, MH * n + h
                act.wait_ge(shift_ready, unit + 1)
                for t in range(4):
                    ex = act.activation(w[:, b, t], score[b][:, t // 2, t % 2], ACT.Exp, scale=scale,
                                        bias=neg_max[:, b, t:t + 1], accum_out=sums[:, b, t:t + 1])
                ex.then_inc(exp_done, 1)

            def body(n, last):
                for h in range(MH):
                    nxt = following(n, h, last)
                    for m in range(MT):
                        it = ITEMS * h + m
                        act.wait_ge(turned, ITEMS * MH * n + it + 1)
                        act.wait_ge(pv_done, MT * (MH * n + h) + m + 1)
                        act.activation(wT_hi[m][:], turn[it % 2][:], ACT.Copy).then_inc(turn_high, 1)
                    if nxt:
                        exps(*nxt)

            act.sem_inc(exp_done, 2)
            exps(0, 0)
            chunks_of(act, body)

        @block.vector
        def _(dve):
            dve.sem_inc(turn_freed, 2)
            dve.sem_inc(gated, 2)
            for m in range(NPREP):
                dve.wait_ge(mem_high, m + 1)
                part = slice(2 * m, 2 * m + 2)
                dve.tensor_tensor(memT_lo[:, part].rearrange("p k s -> p (k s)"), prep[m][:],
                                  as_f32(memT_hi[:, part]).rearrange("p k s -> p (k s)"), ALU.subtract
                                  ).then_inc(mem_low, 1)
            for k in range(KT):
                dve.wait_ge(wm_high, k + 1)
                dve.tensor_tensor(w_lo[:, k], w_raw[:, k % 2], as_f32(w_hi[:, k]), ALU.subtract
                                  ).then_inc(wm_low, 1)
            for m in range(MH + MT):
                dve.wait_ge(kv_high, m + 1)
                src, hi, lo = ((prep[m % 4][:, 0:MEM], k_hi[:, m], k_lo[:, m]) if m < MH
                               else (prep[m % 4][:], v_hi[:, m - MH], v_lo[:, m - MH]))
                dve.tensor_tensor(lo, src, as_f32(hi), ALU.subtract).then_inc(kv_low, 1)

            def maxima(n, h):
                b, unit = h % 2, MH * n + h
                dve.wait_ge(scored, unit + 1)
                for half in range(2):
                    dve.tensor_reduce(top[:, b, 2 * half:2 * half + 2], score[b][:, half], AX_X, ALU.max
                                      ).then_inc(top_done, 1)
                dve.wait_ge(top_done, 2 * (unit + 1))
                dve.tensor_scalar(neg_max[:, b], top[:, b], -scale, None, ALU.mult).then_inc(shift_ready, 1)

            def body(n, last):
                for h in range(MH):
                    b, unit = h % 2, MH * n + h
                    dve.wait_ge(exp_done, 2 + unit + 1)
                    dve.reciprocal(inv_sum[:, b], sums[:, b]).then_inc(inverted, 1)
                    nxt = following(n, h, last)
                    for m in range(MT):
                        it = ITEMS * h + m
                        dve.wait_ge(turn_high, MT * unit + m + 1)
                        dve.tensor_tensor(wT_lo[m][:], turn[it % 2][:], as_f32(wT_hi[m][:]), ALU.subtract
                                          ).then_inc(turn_freed, 1)
                    if nxt:
                        maxima(*nxt)
                    it = ITEMS * h + MT
                    dve.wait_ge(gate_loaded[h], 16 * (n + 1))
                    dve.wait_ge(turned, ITEMS * MH * n + it + 1)
                    dve.tensor_tensor(gate_n[:, b], turn[it % 2][:], gate[:, h], ALU.mult
                                      ).then_inc(turn_freed, 1)
                    dve.wait_ge(stored[b], 16 * (2 * n + h // 2 + 1))
                    dve.wait_ge(turn_freed, 2 + ITEMS * MH * n + it + 1)
                    dve.wait_ge(pv_done, 2 + MT * (unit + 1))
                    dve.tensor_tensor(og[:, b], o_ps[b][:], gate_n[:, b], ALU.mult).then_inc(gated, 1)

            maxima(0, 0)
            chunks_of(dve, body)


def merge_branches(nc, ogT, w_branch, projT, mergedT):
    NBR, KB, FB = 3, 4, D // P
    PARTS = NBR * KB
    with Scope(nc) as c:
        w_raw = c.sb("wb_raw", [P, 2, D])
        w_hi = c.sb("wb_hi", [P, PARTS, D], F32R)
        w_lo = c.sb("wb_lo", [P, PARTS, D], F32R)
        o_raw = c.sb("mo_raw", [P, 2, KB, CH])
        o_hi = c.sb("mo_hi", [P, PARTS, CH], F32R)
        o_lo = c.sb("mo_lo", [P, PARTS, CH], F32R)
        gate = c.sb("mg_gate", [P, 2, NBR, CH])
        prod = c.sb("mg_prod", [P, NBR, CH])
        merged = c.sb("merged", [P, CH])
        m_hi = c.sb("merged_hi", [P, 2, CH], F32R)
        m_lo = c.sb("merged_lo", [P, 2, CH], F32R)
        ps = [[c.ps(f"mg_ps{s}{b}", [P, CH]) for b in range(NBR)] for s in range(2)]
        w_loaded = [c.sem(f"wb_loaded{b}") for b in range(2)]
        w_high = c.sem("wb_high")
        w_low = c.sem("wb_low")
        o_loaded = [c.sem(f"mo_loaded{b}") for b in range(2)]
        o_high = c.sem("mo_high")
        o_split = c.sem("mo_split")
        g_loaded = [c.sem(f"mg_loaded{b}") for b in range(2)]
        product = c.sem("mg_product")
        scaled = c.sem("mg_scaled")
        added = c.sem("mg_added")
        high = c.sem("mg_high")
        low = c.sem("mg_low")
        stored = [c.sem(f"mg_stored{b}") for b in range(2)]
        passed = c.sem("mg_passed")
        block = c.block()
        gates = projT[B_MERGE:].rearrange("(b f) p s -> f p b s", b=NBR)

        def chunks_of(engine, body):
            body(0, True)
            with engine.Fori(1, NCH) as n:
                body(n, False)

        @block.sync
        def _(sp):
            def load_gates(n, f):
                sp.dma_start(gate[:, f % 2], gates[f][:, :, bass.ds(n * CH, CH)]).then_inc(g_loaded[f % 2], 16)

            def load_outputs(n, b, slot):
                sp.dma_start(o_raw[:, slot],
                             ogT[b, :, bass.ds(n * CH, CH)].rearrange("(k p) s -> p k s", p=P)
                             ).then_inc(o_loaded[slot], 16)

            def body(n, first):
                for b in range(NBR):
                    if not (first and b < 2):
                        sp.wait_ge(o_split, PARTS * n + KB * (0, -1, 1)[b])
                        sp.sem_inc(passed, 1)
                    load_outputs(n, b, b % 2)
                    if first:
                        for k in range(KB):
                            part = b * KB + k
                            if part >= 2:
                                sp.wait_ge(w_low, part - 1)
                            sp.dma_start(w_raw[:, part % 2], w_branch[part]).then_inc(w_loaded[part % 2], 16)
                for f in range(FB):
                    unit = FB * n + f
                    if not (first and f < 2):
                        sp.wait_ge(scaled, 3 * unit + 3)
                        sp.sem_inc(passed, 1)
                    load_gates(n, f)
                    if f:
                        store(n, f - 1)
                store(n, FB - 1)

            def store(n, f):
                cols = bass.ds(n * CH, CH)
                sp.wait_ge(low, FB * n + f + 1)
                sp.sem_inc(passed, 1)
                for part, src in ((0, m_hi), (1, m_lo)):
                    sp.dma_start(mergedT[part, f * P:(f + 1) * P, cols], as_f32(src[:, f % 2])
                                 ).then_inc(stored[f % 2], 16)

            chunks_of(sp, body)
            for b in range(2):
                sp.wait_ge(stored[b], 32 + 16 * NCH * FB)

        @block.tensor
        def _(pe):
            def body(n, first):
                for f in range(FB):
                    unit = FB * n + f
                    cols = slice(f * P, (f + 1) * P)
                    for b in range(NBR):
                        bank = ps[f % 2][b]
                        pe.wait_ge(scaled, 3 * unit + b + 1)
                        for k in range(KB):
                            part = b * KB + k
                            if f == 0:
                                pe.wait_ge(o_split, PARTS * n + part + 1)
                                if first:
                                    pe.wait_ge(w_low, part + 1)
                            pe.matmul(bank[:], w_hi[:, part, cols], o_hi[:, part], start=(k == 0), stop=False)
                            pe.matmul(bank[:], w_hi[:, part, cols], o_lo[:, part], start=False, stop=False)
                            mm = pe.matmul(bank[:], w_lo[:, part, cols], o_hi[:, part], start=False,
                                           stop=(k == KB - 1))
                        mm.then_inc(product, 1)

            chunks_of(pe, body)

        def slot_loads(n, b):
            return 2 * n + b // 2 + 1 if b % 2 == 0 else n + 1

        @block.scalar
        def _(act):
            for b in range(2):
                act.sem_inc(stored[b], 32)

            def body(n, first):
                for part in range(PARTS):
                    b, k = divmod(part, KB)
                    if first:
                        act.wait_ge(w_loaded[part % 2], 16 * (part // 2 + 1))
                        act.activation(w_hi[:, part], w_raw[:, part % 2], ACT.Copy).then_inc(w_high, 1)
                    act.wait_ge(o_loaded[b % 2], 16 * slot_loads(n, b))
                    if not first:
                        act.wait_ge(product, NBR * FB * n)
                    act.activation(o_hi[:, part], o_raw[:, b % 2, k], ACT.Copy).then_inc(o_high, 1)
                for f in range(FB):
                    act.wait_ge(added, 2 * (FB * n + f + 1))
                    act.wait_ge(stored[f % 2], 32 * (FB // 2 * n + f // 2 + 1))
                    act.activation(m_hi[:, f % 2], merged[:], ACT.Copy).then_inc(high, 1)

            chunks_of(act, body)

        @block.vector
        def _(dve):
            dve.sem_inc(scaled, 6)

            def body(n, first):
                for part in range(PARTS):
                    b, k = divmod(part, KB)
                    if first:
                        dve.wait_ge(w_high, part + 1)
                        dve.tensor_tensor(w_lo[:, part], w_raw[:, part % 2], as_f32(w_hi[:, part]),
                                          ALU.subtract).then_inc(w_low, 1)
                    dve.wait_ge(o_high, PARTS * n + part + 1)
                    dve.tensor_tensor(o_lo[:, part], o_raw[:, b % 2, k], as_f32(o_hi[:, part]), ALU.subtract
                                      ).then_inc(o_split, 1)
                for f in range(FB):
                    unit = FB * n + f
                    dve.wait_ge(g_loaded[f % 2], 16 * (FB // 2 * n + f // 2 + 1))
                    if not (first and f == 0):
                        dve.wait_ge(added, 2 * unit)
                    for b in range(NBR):
                        dve.wait_ge(product, NBR * unit + b + 1)
                        dve.tensor_tensor(prod[:, b], ps[f % 2][b][:], gate[:, f % 2, b], ALU.mult
                                          ).then_inc(scaled, 1)

            chunks_of(dve, body)

        @block.gpsimd
        def _(pool):
            def body(n, first):
                for f in range(FB):
                    unit = FB * n + f
                    pool.wait_ge(scaled, 6 + 3 * unit + 2)
                    if not (first and f == 0):
                        pool.wait_ge(low, unit)
                    pool.tensor_tensor(merged[:], prod[:, 0], prod[:, 1], ALU.add).then_inc(added, 1)
                    pool.wait_ge(scaled, 6 + 3 * unit + 3)
                    pool.wait_ge(added, 2 * unit + 1)
                    pool.tensor_tensor(merged[:], merged[:], prod[:, 2], ALU.add).then_inc(added, 1)
                    pool.wait_ge(high, unit + 1)
                    pool.tensor_tensor(m_lo[:, f % 2], merged[:], as_f32(m_hi[:, f % 2]), ALU.subtract
                                       ).then_inc(low, 1)

            chunks_of(pool, body)


def project_out(nc, mergedT, w_out, x, ln, out):
    with Scope(nc) as c:
        w_raw = c.sb("wo_raw", [P, 2, D])
        w_hi = c.sb("wo_hi", [P, KT, D], F32R)
        w_lo = c.sb("wo_lo", [P, KT, D], F32R)
        m_hi = [c.sb(f"m_hi{u}", [P, KT, CH], F32R) for u in range(2)]
        m_lo = [c.sb(f"m_lo{u}", [P, KT, CH], F32R) for u in range(2)]
        x_sb = c.sb("x_out", [P, 2, D])
        ln_sb = c.sb("ln_gain_bias", [P, 2, D])
        y = c.sb("y", [P, 2, D])
        sq = c.sb("y_sq", [P, D])
        z = c.sb("z", [P, 2, D])
        stat = c.sb("ln_stat", [P, 2, 5])
        eps = c.sb("ln_eps", [P, 1])
        SUM, NEG_MEAN, SSQ, STD, RSTD = range(5)
        ps = [c.ps(f"out_ps{s}", [P, D]) for s in range(4)]
        w_loaded = [c.sem(f"wo_loaded{b}") for b in range(2)]
        ln_loaded = c.sem("ln_loaded")
        eps_set = c.sem("ln_eps_set")
        w_high = c.sem("wo_high")
        w_low = c.sem("wo_low")
        m_loaded = [c.sem(f"m_loaded{u}") for u in range(2)]
        x_loaded = [c.sem(f"x_out_loaded{u}") for u in range(2)]
        product = c.sem("out_product")
        y_done = c.sem("y_done")
        mean_done = c.sem("mean_done")
        ssq_done = c.sem("ln_ssq_done")
        std_done = c.sem("std_done")
        rstd_done = c.sem("ln_rstd_done")
        normed = c.sem("normed")
        gained = c.sem("gained")
        shifted = c.sem("shifted")
        stored = [c.sem(f"out_stored{u}") for u in range(2)]
        passed = c.sem("out_passed")
        block = c.block()
        xf = x.rearrange("b s d -> (b s) d")
        of = out.rearrange("b s d -> (b s) d")
        NT = 8

        def turns(engine, body):
            with engine.Fori(0, NCH // 2) as i:
                body(i)

        @block.sync
        def _(sp):
            sp.dma_start(ln_sb[:], ln).then_inc(ln_loaded, 16)

            def load_chunk(n, u):
                for src, dst in ((0, m_hi), (1, m_lo)):
                    sp.dma_start(as_f32(dst[u][:]),
                                 mergedT[src, :, n * CH:(n + 1) * CH].rearrange("(k p) s -> p k s", p=P)
                                 ).then_inc(m_loaded[u], 16)

            load_chunk(0, 0)
            for k in range(KT):
                if k >= 2:
                    sp.wait_ge(w_low, k - 1)
                sp.dma_start(w_raw[:, k % 2], w_out[k]).then_inc(w_loaded[k % 2], 16)
            load_chunk(1, 1)
            for u in range(2):
                sp.sem_inc(stored[u], 16)

            def body(i):
                for j in range(NT):
                    tile = NT * i + j
                    sp.wait_ge(shifted, tile + 1)
                    sp.sem_inc(passed, 1)
                    sp.dma_start(x_sb[:, j % 2], xf[bass.ds(tile * P, P)]).then_inc(x_loaded[j % 2], 16)
                    if j:
                        store(i, j - 1)
                store(i, NT - 1)

            def store(i, j):
                tile = NT * i + j
                sp.wait_ge(shifted, 2 + tile + 1)
                sp.sem_inc(passed, 1)
                sp.dma_start(of[bass.ds(tile * P, P)], z[:, j % 2]).then_inc(stored[j % 2], 16)

            body(0)
            sp.wait_ge(product, 4)
            load_chunk(2, 0)
            sp.wait_ge(product, 8)
            load_chunk(3, 1)
            body(1)
            for u in range(2):
                sp.wait_ge(stored[u], 16 + 16 * TT // 2)

        @block.tensor
        def _(pe):
            def body(i):
                for j in range(NT):
                    tile, u = NT * i + j, j // 4
                    rows = slice(j % 4 * P, (j % 4 + 1) * P)
                    if j % 4 == 0:
                        pe.wait_ge(m_loaded[u], 32 * (i + 1))
                    pe.wait_ge(y_done, tile + 1)
                    for half in range(2):
                        bank = ps[j % 4][:, half * CH:(half + 1) * CH]
                        cols = slice(half * CH, (half + 1) * CH)
                        for k in range(KT):
                            pe.matmul(bank, m_hi[u][:, k, rows], w_hi[:, k, cols], start=(k == 0), stop=False)
                            pe.matmul(bank, m_hi[u][:, k, rows], w_lo[:, k, cols], start=False, stop=False)
                            mm = pe.matmul(bank, m_lo[u][:, k, rows], w_hi[:, k, cols], start=False,
                                           stop=(k == KT - 1))
                    mm.then_inc(product, 1)

            pe.wait_ge(w_low, KT)
            turns(pe, body)

        @block.scalar
        def _(act):
            for k in range(KT):
                act.wait_ge(w_loaded[k % 2], 16 * (k // 2 + 1))
                act.activation(w_hi[:, k], w_raw[:, k % 2], ACT.Copy).then_inc(w_high, 1)
            act.wait_ge(eps_set, 1)

            def body(i):
                for j in range(NT):
                    tile, u = NT * i + j, j % 2
                    act.wait_ge(mean_done, tile + 1)
                    act.activation(sq[:], y[:, u], ACT.Square, bias=stat[:, u, NEG_MEAN:NEG_MEAN + 1],
                                   accum_out=stat[:, u, SSQ:SSQ + 1]).then_inc(ssq_done, 1)
                    act.wait_ge(ssq_done, tile + 1)
                    act.activation(stat[:, u, STD:STD + 1], stat[:, u, SSQ:SSQ + 1], ACT.Sqrt,
                                   bias=eps[:, 0:1], scale=1.0 / D).then_inc(std_done, 1)

            turns(act, body)

        @block.vector
        def _(dve):
            dve.sem_inc(y_done, 4)
            for k in range(KT):
                dve.wait_ge(w_high, k + 1)
                dve.tensor_tensor(w_lo[:, k], w_raw[:, k % 2], as_f32(w_hi[:, k]), ALU.subtract
                                  ).then_inc(w_low, 1)

            def body(i):
                for j in range(NT):
                    tile, u = NT * i + j, j % 2

                    def s(at):
                        return stat[:, u, at:at + 1]

                    dve.wait_ge(x_loaded[u], 16 * (NT // 2 * i + j // 2 + 1))
                    dve.wait_ge(product, tile + 1)
                    dve.scalar_tensor_tensor(out=y[:, u], in0=x_sb[:, u], scalar=ALPHA, in1=ps[j % 4][:],
                                             op0=ALU.mult, op1=ALU.add, accum_out=s(SUM)).then_inc(y_done, 1)
                    dve.wait_ge(y_done, 4 + tile + 1)
                    dve.tensor_scalar(s(NEG_MEAN), s(SUM), -1.0 / D, None, ALU.mult).then_inc(mean_done, 1)
                    dve.wait_ge(std_done, tile + 1)
                    dve.reciprocal(s(RSTD), s(STD)).then_inc(rstd_done, 1)
                    dve.wait_ge(rstd_done, tile + 1)
                    dve.wait_ge(stored[u], 16 * (NT // 2 * i + j // 2 + 1))
                    dve.tensor_scalar(z[:, u], y[:, u], s(NEG_MEAN), s(RSTD), ALU.add, ALU.mult
                                      ).then_inc(normed, 1)

            turns(dve, body)

        @block.gpsimd
        def _(pool):
            pool.memset(eps[:], LN_EPS).then_inc(eps_set, 1)
            pool.sem_inc(shifted, 2)
            pool.wait_ge(ln_loaded, 16)

            def body(i):
                for j in range(NT):
                    tile, u = NT * i + j, j % 2
                    pool.wait_ge(normed, tile + 1)
                    pool.tensor_tensor(z[:, u], z[:, u], ln_sb[:, 0], ALU.mult).then_inc(gained, 1)
                    pool.wait_ge(gained, tile + 1)
                    pool.tensor_tensor(z[:, u], z[:, u], ln_sb[:, 1], ALU.add).then_inc(shifted, 1)

            turns(pool, body)


def build(nc, x, mem, w_all, rotary, gains, w_q, w_kv, w_mem, w_branch, w_out, ln, out, scratch):
    projT, qn, qp, kn, kp, va, vb, ogT, mergedT = scratch
    with Scope(nc) as c:
        ident = c.sb("ident", [P, P])
        with Scope(nc) as r:
            xTh = r.sb("xTh", [P, KT, S], F32R)
            xTl = r.sb("xTl", [P, KT, S], F32R)
            load_x_transposed(nc, x, ident, xTh, xTl)
            project_x(nc, w_all, projT, xTh, xTl)
        latent_heads(nc, projT, rotary, gains, w_q, w_kv, ident, qn, qp, kn, kp, va, vb)
        attend(nc, True, (qn, qp), (kn, kp), va, projT, B_GATE, ogT[0], ident)
        sb_q = projT[B_COPY:B_COPY + 4].rearrange("b p s -> (b p) s")
        sb_k = projT[B_COPY + 4:B_COPY + 8].rearrange("b p s -> (b p) s")
        attend(nc, False, sb_q, sb_k, vb, projT, B_GATE + 4, ogT[1], ident)
        attend_memory(nc, mem, w_mem, projT, ogT[2], ident)
    merge_branches(nc, ogT, w_branch, projT, mergedT)
    project_out(nc, mergedT, w_out, x, ln, out)


def rotary_table():
    half = ROPE // 2
    freqs = np.float32(10000.0) ** (-np.arange(half, dtype=np.float32) / np.float32(half))
    ang = freqs[:, None] * np.arange(S, dtype=np.float32)[None, :]
    cos, sin = np.cos(ang), np.sin(ang)
    return np.stack([np.tile(np.concatenate([cos, cos]), (4, 1)),
                     np.tile(np.concatenate([-sin, sin]), (4, 1))]).astype(np.float32)


def lay_out(inputs):
    w = np.asarray(inputs["w_in"])[0]
    rope = w[:, 384:416]
    swapped = np.concatenate([rope[:, 16:], rope[:, :16]], axis=1)
    col = lambda a, b: w[:, a:b]
    g = 416
    parts = [col(0, 384), rope, swapped, rope, swapped,
             col(g, g + 512), col(g + 2048, g + 2560), col(g + 3072, g + 3584),
             col(g + 512, g + 2048), col(g + 2560, g + 3072),
             np.asarray(inputs["w_merge_gate"])[0]]
    w_all = np.concatenate(parts, axis=1)
    w_all = w_all.reshape(KT, P, NBLK, P).transpose(2, 1, 0, 3).reshape(NBLK, P, KT * P)
    bias = np.zeros((NBLK, P, 1), w_all.dtype)
    bias[B_MERGE:, :, 0] = np.asarray(inputs["b_merge_gate"])[0].reshape(NB_MERGE, P)
    w_all = np.concatenate([w_all, bias], axis=2)
    q = np.asarray(inputs["w_q_b"])[0].reshape(QL, H, NOPE + ROPE)
    pe = q[..., NOPE:]
    swapped = np.concatenate([pe[..., ROPE // 2:], pe[..., :ROPE // 2]], axis=-1)
    w_q = np.concatenate([q[..., :NOPE].reshape(QL, -1), pe.reshape(QL, -1), swapped.reshape(QL, -1)], axis=1)
    kv = np.asarray(inputs["w_kv_b"])[0].reshape(KVL, H, NOPE + VD)
    w_kv = np.concatenate([kv[..., :NOPE].reshape(KVL, -1), kv[..., NOPE:].reshape(KVL, -1)], axis=1)
    gains = np.concatenate([np.asarray(inputs["q_a_gain"])[0], np.asarray(inputs["kv_a_gain"])[0]])
    gains = gains.reshape(3, P).T
    w_branch = np.concatenate([np.asarray(inputs[n])[0] for n in
                               ("w_branch_mla", "w_branch_sb", "w_branch_mem")])
    ln = np.stack([np.asarray(inputs["ln_gain"])[0], np.asarray(inputs["ln_bias"])[0]])
    return {
        "x": inputs["x"],
        "mem": inputs["mem"],
        "w_all": w_all,
        "rotary": rotary_table(),
        "gains": gains,
        "w_q": w_q.reshape(2, P, D).transpose(1, 0, 2),
        "w_kv": w_kv,
        "w_mem": np.asarray(inputs["w_mem_kv"])[0].reshape(KT, P, D),
        "w_branch": w_branch.reshape(12, P, D),
        "w_out": np.asarray(inputs["w_out"])[0].reshape(KT, P, D),
        "ln": np.broadcast_to(ln, (P, 2, D)),
    }


def kernel(**inputs):
    import concourse.bacc as bacc
    from concourse.bass_utils import run_bass_kernel_spmd
    nc = bacc.Bacc("TRN2", target_bir_lowering=False, num_devices=1)
    arrays, args = {}, []
    for name, a in lay_out(inputs).items():
        a = np.ascontiguousarray(a)
        arrays[f"in_{name}_dram"] = a
        args.append(nc.dram_tensor(f"in_{name}_dram", a.shape, mybir.dt.from_np(a.dtype),
                                   kind="ExternalInput").ap())
    shapes = dict(projT=(NBLK, P, S), qn=(512, S), qp=(256, S), kn=(512, S), kp=(ROPE, S), va=(S, 512),
                  vb=(S, 512), ogT=(3, 512, S), mergedT=(2, D, S))
    scratch = [nc.dram_tensor(n, sh, F32).ap() for n, sh in shapes.items()]
    out = nc.dram_tensor("out_dram", (1, S, D), F32, kind="ExternalOutput").ap()
    build(nc, *args, out, scratch)
    r = run_bass_kernel_spmd(nc, [arrays], core_ids=[0])
    return r.results[0]["out_dram"]
```

```python
from contextlib import ExitStack

import numpy as np
import concourse.bass as bass
from concourse import mybir

P = 128
D = 1024
S = 2048
KT = D // P
CH = 512
NCH = S // CH
TT = S // P
MEM = 256
MT = MEM // P
QL, KVL, ROPE, NOPE, VD, H = 256, 128, 32, 64, 64, 8
SBD = 64
MH, MD = 4, 128
NB_LAT, NB_GATE, NB_COPY, NB_MERGE = 4, 12, 16, 24
NBLK = NB_LAT + NB_GATE + NB_COPY + NB_MERGE
B_GATE, B_COPY, B_MERGE = NB_LAT, NB_LAT + NB_GATE, NB_LAT + NB_GATE + NB_COPY
RMS_EPS, LN_EPS = 1e-6, 1e-5
ALPHA = 2.0 ** 0.25
BIG = 3.0e38

F32 = mybir.dt.float32
F32R = mybir.dt.float32r
ALU = mybir.AluOpType
ACT = mybir.ActivationFunctionType
AX_X = mybir.AxisListType.X


def as_f32(ap):
    return ap.bitcast(F32)


class Scope:

    def __init__(self, nc):
        self.nc, self.ctx, self.sems = nc, ExitStack(), []

    def __enter__(self):
        return self

    def __exit__(self, *a):
        self.ctx.__exit__(*a)
        if self.sems and a[0] is None:
            self.nc.clear_and_free_semaphores(self.sems)
            self.nc.all_engine_barrier()

    def sb(self, name, shape, dt=F32):
        return self.ctx.enter_context(self.nc.sbuf_tensor(name, shape, dt))

    def ps(self, name, shape, dt=F32):
        return self.ctx.enter_context(self.nc.psum_tensor(name, shape, dt))

    def sem(self, name):
        self.sems.append(self.nc.alloc_semaphore(name=name))
        return self.sems[-1]

    def block(self):
        return self.ctx.enter_context(self.nc.Block())


def split_weights(pool, w, u, ones, high_done, low_done, count):
    ones_row = ones[:, 0:1].broadcast_to([P, KT * P])
    pool.tensor_tensor(w["bias"][:, u:u + 1], w["raw"][:, u, KT * P:], ones[:, 0:1], ALU.mult)
    pool.tensor_tensor(w["high"][:, u], w["raw"][:, u, 0:KT * P], ones_row, ALU.mult).then_inc(high_done, 1)
    pool.wait_ge(high_done, count + 1)
    pool.tensor_tensor(w["low"][:, u], w["raw"][:, u, 0:KT * P], as_f32(w["high"][:, u]), ALU.subtract
                       ).then_inc(low_done, 1)


def load_x_transposed(nc, x, w_all, w, ones, ident, xTh, xTl):
    NBANK = 8
    NIN = 3
    with Scope(nc) as c:
        xin = c.sb("xin", [P, NIN, 4, D])
        bank = [c.ps(f"xT_ps{i}", [P, CH]) for i in range(NBANK)]
        loaded = [c.sem(f"x_loaded{i}") for i in range(NIN)]
        w_loaded = [c.sem(f"first_w_loaded{u}") for u in range(2)]
        w_high = c.sem("first_w_high")
        w_low = c.sem("first_w_low")
        ones_set = c.sem("ones_set")
        turned = c.sem("x_turned")
        high_done = c.sem("x_high_done")
        low_done = c.sem("x_low_done")
        ident_zero = c.sem("ident_zero")
        ident_ready = c.sem("ident_ready")
        block = c.block()
        xg = x.rearrange("b (g t p) d -> (b g) p t d", t=4, p=P)

        @block.sync
        def _(sp):
            for g in range(NCH):
                if g >= NIN:
                    sp.wait_ge(turned, KT * (g - NIN + 1))
                sp.dma_start(xin[:, g % NIN], xg[g]).then_inc(loaded[g % NIN], 16)
            for u in range(2):
                sp.dma_start(w["raw"][:, u], w_all[u]).then_inc(w_loaded[u], 16)

        @block.gpsimd
        def _(pool):
            pool.memset(ident[:], 0.0).then_inc(ident_zero, 1)
            pool.wait_ge(ident_zero, 1)
            pool.affine_select(out=ident[:], in_=ident[:], compare_op=ALU.not_equal, fill=1.0, base=0,
                               pattern=[[-1, P]], channel_multiplier=1).then_inc(ident_ready, 1)
            pool.memset(ones[:], 1.0).then_inc(ones_set, 1)
            pool.wait_ge(ones_set, 1)
            for u in range(2):
                pool.wait_ge(w_loaded[u], 16)
                split_weights(pool, w, u, ones, w_high, w_low, u)

        @block.tensor
        def _(pe):
            pe.wait_ge(ident_ready, 1)
            for g in range(NCH):
                pe.wait_ge(loaded[g % NIN], 16 * (g // NIN + 1))
                for k in range(KT):
                    n = g * KT + k
                    if n >= NBANK:
                        pe.wait_ge(low_done, n - NBANK + 1)
                    for t in range(4):
                        mm = pe.transpose(bank[n % NBANK][:, t * P:(t + 1) * P],
                                          xin[:, g % NIN, t, k * P:(k + 1) * P], ident[:])
                    mm.then_inc(turned, 1)

        @block.scalar
        def _(act):
            for n in range(NCH * KT):
                g, k = divmod(n, KT)
                act.wait_ge(turned, n + 1)
                act.activation(xTh[:, k, g * CH:(g + 1) * CH], bank[n % NBANK][:],
                               ACT.Copy).then_inc(high_done, 1)

        @block.vector
        def _(dve):
            for n in range(NCH * KT):
                g, k = divmod(n, KT)
                cols = slice(g * CH, (g + 1) * CH)
                dve.wait_ge(high_done, n + 1)
                dve.tensor_tensor(xTl[:, k, cols], bank[n % NBANK][:], as_f32(xTh[:, k, cols]),
                                  ALU.subtract).then_inc(low_done, 1)


def project_x(nc, w_all, w, ones, projT, xTh, xTl):
    NPAIR = NBLK // 2
    wh, wl, bias = w["high"], w["low"], w["bias"]
    with Scope(nc) as c:
        stage = c.sb("proj_stage", [P, 2, S])
        sig = c.sb("gate_sigmoid", [P, 2, CH])
        acc = [[c.ps(f"proj_ps{u}{n}", [P, CH]) for n in range(NCH)] for u in range(2)]
        w_loaded = [c.sem(f"w_loaded{u}") for u in range(2)]
        high_done = c.sem("w_high_done")
        low_done = c.sem("w_low_done")
        product = c.sem("proj_product")
        sig_done = c.sem("sig_done")
        evac = c.sem("proj_evac")
        stored = [c.sem(f"proj_stored{u}") for u in range(2)]
        block = c.block()

        @block.sync
        def _(sp):
            def pair(i, last):
                for u in range(2):
                    b = 2 * i + u
                    if not last:
                        sp.wait_ge(low_done, b + 1)
                        sp.dma_start(w["raw"][:, u], w_all[bass.ds(b + 2, 1)].squeeze(0)
                                     ).then_inc(w_loaded[u], 16)
                    sp.wait_ge(evac, NCH * (b + 1))
                    sp.dma_start(projT[bass.ds(b, 1)].squeeze(0), stage[:, u]).then_inc(stored[u], 16)

            with sp.Fori(0, NPAIR - 1) as i:
                pair(i, False)
            pair(NPAIR - 1, True)
            for u in range(2):
                sp.wait_ge(stored[u], 16 * NPAIR)

        @block.gpsimd
        def _(pool):
            pool.sem_inc(high_done, 2)
            pool.sem_inc(low_done, 2)
            with pool.Fori(1, NPAIR) as i:
                for u in range(2):
                    b = 2 * i + u
                    pool.wait_ge(w_loaded[u], 16 * i)
                    pool.wait_ge(evac, NCH * (b - 1))
                    split_weights(pool, w, u, ones, high_done, low_done, b)

        @block.tensor
        def _(pe):
            def pair(i, first):
                for u in range(2):
                    b = 2 * i + u
                    pe.wait_ge(low_done, b + 1)
                    for n in range(NCH):
                        if not first:
                            pe.wait_ge(evac, NCH * (b - 2) + n + 1)
                        cols = slice(n * CH, (n + 1) * CH)
                        for k in range(KT):
                            pe.matmul(acc[u][n][:], wh[:, u, k * P:(k + 1) * P], xTh[:, k, cols],
                                      start=(k == 0), stop=False)
                            pe.matmul(acc[u][n][:], wh[:, u, k * P:(k + 1) * P], xTl[:, k, cols],
                                      start=False, stop=False)
                            mm = pe.matmul(acc[u][n][:], wl[:, u, k * P:(k + 1) * P], xTh[:, k, cols],
                                           start=False, stop=(k == KT - 1))
                        mm.then_inc(product, 1)

            pair(0, True)
            with pe.Fori(1, NPAIR) as i:
                pair(i, False)

        @block.scalar
        def _(act):
            with act.Fori(B_GATE // 2, B_COPY // 2) as i:
                for u in range(2):
                    b = 2 * i + u
                    for n in range(NCH):
                        act.wait_ge(product, NCH * b + n + 1)
                        act.wait_ge(evac, NCH * b + n - 1)
                        act.activation(sig[:, n % 2], acc[u][n][:], ACT.Sigmoid).then_inc(sig_done, 1)
            with act.Fori(B_MERGE // 2, NPAIR) as i:
                for u in range(2):
                    b = 2 * i + u
                    act.wait_ge(stored[u], 16 * i)
                    for n in range(NCH):
                        act.wait_ge(product, NCH * b + n + 1)
                        act.wait_ge(evac, NCH * b + n)
                        act.activation(stage[:, u, n * CH:(n + 1) * CH], acc[u][n][:], ACT.Sigmoid,
                                       bias=bias[:, u:u + 1]).then_inc(evac, 1)

        @block.vector
        def _(dve):
            def copies(i, first):
                for u in range(2):
                    b = 2 * i + u
                    if not first:
                        dve.wait_ge(stored[u], 16 * i)
                    for n in range(NCH):
                        dve.wait_ge(product, NCH * b + n + 1)
                        dve.tensor_copy(stage[:, u, n * CH:(n + 1) * CH], acc[u][n][:]).then_inc(evac, 1)

            copies(0, True)
            with dve.Fori(1, B_GATE // 2) as i:
                copies(i, False)
            with dve.Fori(B_GATE // 2, B_COPY // 2) as i:
                for u in range(2):
                    b = 2 * i + u
                    dve.wait_ge(stored[u], 16 * i)
                    for n in range(NCH):
                        dve.wait_ge(sig_done, NCH * (b - B_GATE) + n + 1)
                        dve.tensor_tensor(stage[:, u, n * CH:(n + 1) * CH], acc[u][n][:], sig[:, n % 2],
                                          ALU.mult).then_inc(evac, 1)
            with dve.Fori(B_COPY // 2, B_MERGE // 2) as i:
                copies(i, False)


def latent_heads(nc, projT, rotary, gains, w_q, w_kv, ident, qn, qp, kn, kp, va, vb):
    PLAIN = 12
    USES = NCH + PLAIN
    with Scope(nc) as c:
        wq_raw = c.sb("wq_raw", [P, 2, D])
        wq_h = c.sb("wq_h", [P, 2, D], F32R)
        wq_l = c.sb("wq_l", [P, 2, D], F32R)
        wkv_raw = c.sb("wkv_raw", [P, D])
        wkv_h = c.sb("wkv_h", [P, D], F32R)
        wkv_l = c.sb("wkv_l", [P, D], F32R)
        gain = c.sb("gain", [P, 3])
        eps = c.sb("eps", [P, 1])
        ones = c.sb("ones_sq", [P, P])
        lat = c.sb("lat", [P, 2, 3, CH])
        kr = c.sb("k_rope", [ROPE, 2, 2, CH])
        cs = c.sb("cos_sin", [P, 2, 2, CH])
        sq = c.sb("lat_sq", [P, 3, CH])
        rstd = c.sb("lat_rstd", [P, 2, CH])
        norm = c.sb("lat_norm", [P, 3, CH])
        norm_h = c.sb("lat_norm_h", [P, 2, 3, CH], F32R)
        norm_l = c.sb("lat_norm_l", [P, 2, 3, CH], F32R)
        plain = c.sb("plain_out", [P, 2, PLAIN, CH])
        rot = c.sb("rot_out", [P, 2, 2, CH])
        part = c.sb("rot_part", [P, 2, CH])
        krot = c.sb("k_rot_out", [ROPE, 2, CH])
        kpart = c.sb("k_rot_part", [ROPE, 2, CH])
        vT = c.sb("vT", [P, S])
        v_out = c.sb("v_out", [P, 2, NCH, CH])
        ssq = [c.ps(f"ssq{i}", [P, CH]) for i in range(2)]
        pbank = [c.ps(f"plain_ps{i}", [P, CH]) for i in range(4)]
        rbank = [c.ps(f"rot_ps{i}", [P, CH]) for i in range(2)]
        w_loaded = c.sem("lat_w_loaded")
        consts = c.sem("lat_consts")
        w_split = c.sem("lat_w_split")
        lat_loaded = [c.sem(f"lat_loaded{u}") for u in range(2)]
        rope_loaded = [c.sem(f"rope_loaded{u}") for u in range(2)]
        v_loaded = c.sem("vT_loaded")
        sq_done = c.sem("lat_sq_done")
        ssq_done = c.sem("ssq_done")
        root_done = c.sem("root_done")
        rstd_done = c.sem("rstd_done")
        norm_done = c.sem("norm_done")
        norm_high = c.sem("norm_high")
        norm_low = c.sem("norm_low")
        plain_done = c.sem("plain_done")
        plain_out = c.sem("plain_out")
        rot_done = c.sem("rot_done")
        rot_parts = c.sem("rot_parts")
        rot_out = c.sem("rot_out")
        krot_parts = c.sem("krot_parts")
        stored = [c.sem(f"lat_stored{u}") for u in range(2)]
        v_stored = [c.sem(f"vb_stored{u}") for u in range(2)]
        block = c.block()
        NST = 5
        order = [4, 6, 5, 7]

        @block.sync
        def _(sp):
            def load_latents(n):
                u, cols = n % 2, slice(n * CH, (n + 1) * CH)
                if n >= 2:
                    sp.wait_ge(norm_done, 3 * (n - 1))
                sp.dma_start(lat[:, u], projT[0:3, :, cols].rearrange("b p c -> p b c")
                             ).then_inc(lat_loaded[u], 16)

            def load_rotary(n):
                u, cols = n % 2, slice(n * CH, (n + 1) * CH)
                if n >= 2:
                    sp.wait_ge(rot_parts, 4 * (n - 1))
                    sp.wait_ge(krot_parts, 2 * (n - 1))
                sp.dma_start(kr[:, u], projT[3, 0:2 * ROPE, cols].rearrange("(a p) c -> p a c", p=ROPE)
                             ).then_inc(rope_loaded[u], 16)
                sp.dma_start(cs[:, u], rotary[:, :, cols].rearrange("a p c -> p a c")
                             ).then_inc(rope_loaded[u], 16)

            load_latents(0)
            sp.dma_start(wq_raw[:], w_q).then_inc(w_loaded, 16)
            sp.dma_start(wkv_raw[:], w_kv).then_inc(w_loaded, 16)
            sp.dma_start(gain[:], gains).then_inc(w_loaded, 16)
            sp.dma_start(vT[:], projT[B_COPY + 8]).then_inc(v_loaded, 16)
            load_latents(1)
            load_rotary(0)
            load_rotary(1)
            for n in range(NCH):
                u, cols = n % 2, slice(n * CH, (n + 1) * CH)
                if n + 2 < NCH:
                    load_latents(n + 2)
                sp.wait_ge(plain_out, USES * n + NCH)
                sp.dma_start(vb[:, n * P:(n + 1) * P].rearrange("(t p) f -> p t f", p=P),
                             v_out[:, u].rearrange("p n (t f) -> p (n t) f", f=P)).then_inc(v_stored[u], 16)
                if n + 1 < NCH:
                    sp.dma_start(vT[:], projT[B_COPY + 9 + n]).then_inc(v_loaded, 16)
                for dst, src in ((qn, 0), (kn, 4)):
                    sp.wait_ge(plain_out, USES * n + NCH + src + 4)
                    sp.dma_start(dst[:, cols].rearrange("(b p) c -> p b c", p=P),
                                 plain[:, u, src:src + 4]).then_inc(stored[u], 16)
                sp.wait_ge(plain_out, USES * (n + 1))
                sp.dma_start(va[cols].rearrange("(t p) f -> p t f", p=P), plain[:, u, 8:12]
                             ).then_inc(stored[u], 16)
                sp.wait_ge(rot_out, 3 * (n + 1))
                sp.dma_start(qp[:, cols].rearrange("(b p) c -> p b c", p=P), rot[:, u]
                             ).then_inc(stored[u], 16)
                sp.dma_start(kp[:, cols], krot[:, u]).then_inc(stored[u], 16)
                if n + 2 < NCH:
                    load_rotary(n + 2)
            for u in range(2):
                sp.wait_ge(stored[u], 16 * NST * 2)
                sp.wait_ge(v_stored[u], 32)

        @block.gpsimd
        def _(pool):
            pool.memset(eps[:], RMS_EPS).then_inc(consts, 1)
            pool.memset(ones[:], 1.0).then_inc(consts, 1)

            def squares(n):
                pool.wait_ge(lat_loaded[n % 2], 16 * (n // 2 + 1))
                if n:
                    pool.wait_ge(ssq_done, 2 * n)
                pool.tensor_tensor(sq[:], lat[:, n % 2], lat[:, n % 2], ALU.mult).then_inc(sq_done, 1)

            squares(0)
            for n in range(NCH):
                u = n % 2
                if n + 1 < NCH:
                    squares(n + 1)
                for j in range(2):
                    if n >= 2:
                        pool.wait_ge(stored[u], 16 * NST * (n // 2))
                    pool.wait_ge(rot_parts, 4 * n + 2 * j + 2)
                    pool.tensor_tensor(rot[:, u, j], rot[:, u, j], part[:, j], ALU.add
                                       ).then_inc(rot_out, 1)
                pool.wait_ge(krot_parts, 2 * (n + 1))
                pool.tensor_tensor(krot[:, u], krot[:, u], kpart[:, u], ALU.add).then_inc(rot_out, 1)

        @block.tensor
        def _(pe):
            pe.wait_ge(consts, 2)

            def sum_squares(n):
                pe.wait_ge(sq_done, n + 1)
                if n:
                    pe.wait_ge(root_done, 2 * n)
                pe.matmul(ssq[0][:], ones[:], sq[:, 0], start=True, stop=False)
                pe.matmul(ssq[0][:], ones[:], sq[:, 1], start=False, stop=True).then_inc(ssq_done, 1)
                pe.matmul(ssq[1][:], ones[:], sq[:, 2], start=True, stop=True).then_inc(ssq_done, 1)

            sum_squares(0)
            for n in range(NCH):
                u = n % 2
                pe.wait_ge(v_loaded, 16 * (n + 1))
                for m in range(NCH):
                    r = USES * n + m
                    if n:
                        pe.wait_ge(plain_out, r - 3)
                    for t in range(4):
                        at = (4 * m + t) * P
                        mm = pe.transpose(pbank[r % 4][:, t * P:(t + 1) * P], vT[:, at:at + P], ident[:])
                    mm.then_inc(plain_done, 1)
                pe.wait_ge(w_split, 2)
                pe.wait_ge(norm_low, 3 * (n + 1))

                def up(bank, pairs, done):
                    last = 3 * len(pairs) - 1
                    at = 0
                    for (ah, al), (bh, bl) in pairs:
                        for a, b in ((ah, bh), (ah, bl), (al, bh)):
                            mm = pe.matmul(bank, a, b, start=(at == 0), stop=(at == last))
                            at += 1
                    mm.then_inc(done, 1)

                for j in range(PLAIN):
                    r = USES * n + NCH + j
                    pe.wait_ge(plain_out, r - 3)
                    cols = slice((j % 4) * P, (j % 4 + 1) * P)
                    if j < 4:
                        pairs = [((wq_h[:, k, cols], wq_l[:, k, cols]), (norm_h[:, u, k], norm_l[:, u, k]))
                                 for k in range(2)]
                    elif j < 8:
                        pairs = [((wkv_h[:, cols], wkv_l[:, cols]), (norm_h[:, u, 2], norm_l[:, u, 2]))]
                    else:
                        pairs = [((norm_h[:, u, 2, cols], norm_l[:, u, 2, cols]), (wkv_h[:, CH:], wkv_l[:, CH:]))]
                    up(pbank[r % 4][:], pairs, plain_done)
                    if j == 1 and n + 1 < NCH:
                        sum_squares(n + 1)
                    if j % 3 == 2:
                        m = j // 3
                        if n or m >= 2:
                            pe.wait_ge(rot_parts, 4 * n + m - 1)
                        cols = slice(order[m] * P, (order[m] + 1) * P)
                        pairs = [((wq_h[:, k, cols], wq_l[:, k, cols]), (norm_h[:, u, k], norm_l[:, u, k]))
                                 for k in range(2)]
                        up(rbank[m % 2][:], pairs, rot_done)

        @block.scalar
        def _(act):
            act.wait_ge(w_loaded, 48)
            act.activation(wq_h[:], wq_raw[:], ACT.Copy).then_inc(norm_high, 1)
            act.activation(wkv_h[:], wkv_raw[:], ACT.Copy).then_inc(norm_high, 1)
            act.wait_ge(consts, 2)

            def roots(n):
                if n:
                    act.wait_ge(norm_done, 3 * n)
                for j, width in ((0, QL), (1, KVL)):
                    act.wait_ge(ssq_done, 2 * n + j + 1)
                    act.activation(rstd[:, j], ssq[j][:], ACT.Sqrt, bias=eps[:, 0:1], scale=1.0 / width
                                   ).then_inc(root_done, 1)

            def high_parts(n):
                for k in range(3):
                    act.wait_ge(norm_done, 3 * n + k + 1)
                    if n >= 2:
                        act.wait_ge(plain_done, USES * (n - 1))
                        act.wait_ge(rot_done, 4 * (n - 1))
                    act.activation(norm_h[:, n % 2, k], norm[:, k], ACT.Copy).then_inc(norm_high, 1)

            roots(0)
            high_parts(0)
            for n in range(NCH):
                u = n % 2
                if n >= 2:
                    act.wait_ge(v_stored[u], 16 * (n // 2))
                for m in range(NCH):
                    r = USES * n + m
                    act.wait_ge(plain_done, r + 1)
                    act.activation(v_out[:, u, m], pbank[r % 4][:], ACT.Copy).then_inc(plain_out, 1)
                if n >= 2:
                    act.wait_ge(stored[u], 16 * NST * (n // 2))
                for j in range(PLAIN):
                    r = USES * n + NCH + j
                    act.wait_ge(plain_done, r + 1)
                    act.activation(plain[:, u, j], pbank[r % 4][:], ACT.Copy).then_inc(plain_out, 1)
                    if j == 2 and n + 1 < NCH:
                        roots(n + 1)
                if n + 1 < NCH:
                    high_parts(n + 1)

        @block.vector
        def _(dve):
            dve.wait_ge(norm_high, 2)
            dve.tensor_tensor(wq_l[:], wq_raw[:], as_f32(wq_h[:]), ALU.subtract).then_inc(w_split, 1)
            dve.tensor_tensor(wkv_l[:], wkv_raw[:], as_f32(wkv_h[:]), ALU.subtract).then_inc(w_split, 1)

            def invert(n, j):
                dve.wait_ge(root_done, 2 * n + j + 1)
                dve.reciprocal(rstd[:, j], rstd[:, j]).then_inc(rstd_done, 1)

            def norms(n):
                dve.wait_ge(lat_loaded[n % 2], 16 * (n // 2 + 1))
                dve.wait_ge(rstd_done, 2 * (n + 1))
                if n:
                    dve.wait_ge(norm_high, 2 + 3 * n)
                for k in range(3):
                    dve.scalar_tensor_tensor(out=norm[:, k], in0=lat[:, n % 2, k], scalar=gain[:, k:k + 1],
                                             in1=rstd[:, k // 2], op0=ALU.mult, op1=ALU.mult
                                             ).then_inc(norm_done, 1)

            def low_parts(n):
                for k in range(3):
                    dve.wait_ge(norm_high, 2 + 3 * n + k + 1)
                    dve.tensor_tensor(norm_l[:, n % 2, k], norm[:, k], as_f32(norm_h[:, n % 2, k]),
                                      ALU.subtract).then_inc(norm_low, 1)

            invert(0, 0)
            invert(0, 1)
            norms(0)
            low_parts(0)
            for n in range(NCH):
                u = n % 2
                dve.wait_ge(rope_loaded[u], 32 * (n // 2 + 1))
                if n >= 2:
                    dve.wait_ge(stored[u], 16 * NST * (n // 2))
                if n:
                    dve.wait_ge(rot_out, 3 * n)
                dve.tensor_tensor(krot[:, u], kr[:, u, 0], cs[0:ROPE, u, 0], ALU.mult
                                  ).then_inc(krot_parts, 1)
                dve.tensor_tensor(kpart[:, u], kr[:, u, 1], cs[0:ROPE, u, 1], ALU.mult
                                  ).then_inc(krot_parts, 1)
                for m in range(4):
                    dve.wait_ge(rot_done, 4 * n + m + 1)
                    dst = part[:, m // 2] if m % 2 else rot[:, u, m // 2]
                    dve.tensor_tensor(dst, rbank[m % 2][:], cs[:, u, m % 2], ALU.mult
                                      ).then_inc(rot_parts, 1)
                    if n + 1 < NCH:
                        if m < 2:
                            invert(n + 1, m)
                        if m == 2:
                            norms(n + 1)
                if n + 1 < NCH:
                    low_parts(n + 1)


ORDER = [1, 3, 2, 0]
START = [sum(4 * (g + 1) for g in ORDER[:o]) for o in range(4)]
PER_HEAD = sum(4 * (g + 1) for g in ORDER)
KEEPS = 4
WT = 4
LATE = 5
EXP_LAG = 5
LEAD, TAIL = 5, 4
PIECES = 12
HEAD = 64
SPLIT_IN = [(0, 0), (0, 4), (4, 12), (12, 12)]


def attend(nc, soft, q_src, k_src, v_src, projT, gate_block, ogT, ident):
    scale = float(NOPE + ROPE) ** -0.5 if soft else float(SBD) ** -0.5
    rows = NOPE + ROPE if soft else P
    score_banks, turn_banks = 2, 4
    loads = 5
    items = PER_HEAD + 4 if soft else PER_HEAD
    per_pos = [4 * (g + 1) + (1 if soft else 0) for g in ORDER]
    item_at = [sum(per_pos[:o]) for o in range(4)]

    with Scope(nc) as c:
        n = "mla_" if soft else "sb_"
        q_raw = c.sb(n + "q_raw", [rows, S])
        k_raw = c.sb(n + "k_raw", [rows, S])
        v_raw = c.sb(n + "v_raw", [P, TT, HEAD])
        q_hi = [c.sb(n + f"q_hi{u}", [rows, S], F32R) for u in range(2)]
        q_lo = [c.sb(n + f"q_lo{u}", [rows, S], F32R) for u in range(2)] if soft else None
        k_hi = [c.sb(n + f"k_hi{u}", [rows, S], F32R) for u in range(2)]
        k_lo = [c.sb(n + f"k_lo{u}", [rows, S], F32R) for u in range(2)]
        v_two = [c.sb(n + f"v_two{u}", [P, TT, 2 * HEAD], F32R) for u in range(2)]
        w = [c.sb(n + f"w{o}", [P, 4, (max(ORDER[o::2]) + 1) * CH]) for o in range(2)]
        wT_hi = [c.sb(n + f"wT_hi{b}", [P, CH], F32R) for b in range(WT)]
        wT_lo = [c.sb(n + f"wT_lo{b}", [P, CH], F32R) for b in range(WT)]
        gate = c.sb(n + "gate", [HEAD, 2, CH])
        o_low = c.sb(n + "o_low", [HEAD, 2, CH])
        o_sum = c.sb(n + "o_sum", [HEAD, 2, CH])
        og = c.sb(n + "og", [HEAD, 2, CH])
        mask = c.sb(n + "mask", [P, P])
        ones = c.sb(n + "ones", [P, P])
        if soft:
            maxes = c.sb(n + "maxes", [P, 16, 4])
            neg_max = c.sb(n + "neg_max", [P, 16])
            sums = c.sb(n + "sums", [P, 16])
            top = c.sb(n + "top", [P, 16])
            inv_sum = c.sb(n + "inv_sum", [P, 16])
            diag = c.sb(n + "diag", [P, 4, P])
            gate_n = c.sb(n + "gate_n", [HEAD, 2, CH])
        else:
            keep = c.sb(n + "keep", [P, KEEPS, CH])
            after = c.sb(n + "after", [P, 2, S + 1])
        score = [c.ps(n + f"score{b}", [P, CH]) for b in range(score_banks)]
        turn = [c.ps(n + f"turn{b}", [P, CH]) for b in range(turn_banks)]
        o_ps = [c.ps(n + f"o_ps{b}", [P, CH]) for b in range(2)]

        consts = c.sem(n + "consts")
        raw_loaded = c.sem(n + "raw_loaded")
        first_loaded = c.sem(n + "first_loaded")
        split_high = c.sem(n + "split_high")
        split = c.sem(n + "split")
        scored = c.sem(n + "scored")
        masked = c.sem(n + "masked")
        top_done = c.sem(n + "top_done")
        shift_ready = c.sem(n + "shift_ready")
        freed = c.sem(n + "freed")
        scanned = c.sem(n + "scanned")
        weighted = c.sem(n + "weighted")
        exp_done = c.sem(n + "exp_done")
        inverted = c.sem(n + "inverted")
        diag_ready = c.sem(n + "diag_ready")
        turned = c.sem(n + "turned")
        turn_high = c.sem(n + "turn_high")
        turn_freed = c.sem(n + "turn_freed")
        pv_done = c.sem(n + "pv_done")
        low_copied = c.sem(n + "low_copied")
        o_summed = c.sem(n + "o_summed")
        gated = c.sem(n + "gated")
        gate_loaded = [c.sem(n + f"gate_loaded{b}") for b in range(2)]
        stored = [c.sem(n + f"og_stored{b}") for b in range(2)]
        passed = c.sem(n + "passed")
        block = c.block()

        def weights_ready(h, o):
            return (exp_done, 16 * h + 4 * o + 4) if soft else (weighted, 2 + number(h, o, 3, ORDER[o] + 1))

        def heads(engine, body):
            with engine.Fori(0, H // 2 - 1) as i:
                body(i, 0, False)
                body(i, 1, False)
            body(H // 2 - 1, 0, False)
            body(H // 2 - 1, 1, True)

        def chunks(g, t):
            both = [(k, CH if k < g else (t + 1) * P) for k in range(g + 1)]
            return both if soft else both[::-1]

        def schedule(o, nxt):
            tiles = [("tile", j) for j in range(4 * (ORDER[o] + 1))] + ([("sums",)] if soft else [])
            if not nxt:
                return tiles
            g = ORDER[(o + 1) % 4]
            new = [("chunk", t, j, k, width) for t in range(4) for j, (k, width) in enumerate(chunks(g, t))]
            alone = min(TAIL, len(tiles) - 1)
            mixed, tiles, end = new[:LEAD], tiles[:-alone], tiles[-alone:]
            new, a, b = new[LEAD:], 0, 0
            for _ in range(len(tiles) + len(new)):
                if b < len(new) and (a == len(tiles) or b * len(tiles) < a * len(new)):
                    mixed.append(new[b])
                    b += 1
                else:
                    mixed.append(tiles[a])
                    a += 1
            return mixed + end

        def timeline(last, **lags):
            steps, base = [], 0
            for o in range(4):
                slots = schedule(o, o < 3 or not last)
                end = base + len(slots)
                for s, (what, *args) in enumerate(slots, base):
                    if what == "chunk":
                        kinds = ("scores", "to_sbuf", "exp", "sigmoids", "scan", "weigh")
                        args = [(o + 1) % 4] + args
                    elif what == "sums":
                        kinds, args = ("sums", "gate_n"), [o]
                    else:
                        kinds = ("turn", "high", "low", "times_v")
                        if args[0] == 0:
                            kinds += ("invert", "diagonal")
                        if args[0] == 4 * ORDER[o] + 3:
                            kinds += ("o_low", "o_sum", "gated")
                        args = [o] + args
                    for kind in kinds:
                        if kind in lags:
                            at = s + lags[kind]
                            steps.append((min(at, end - 0.5) if what == "chunk" else at, at, (kind, *args)))
                if "piece" in lags and not last:
                    for p in range(*SPLIT_IN[o]):
                        at = base + len(slots) * (p - SPLIT_IN[o][0]) / (SPLIT_IN[o][1] - SPLIT_IN[o][0])
                        steps.append((at + lags["piece"], at, ("piece", o, p)))
                base = end
            return [step for *_, step in sorted(steps, key=lambda step: step[:2])]

        def all_chunks(o):
            return [(t, j, k, width) for t in range(4) for j, (k, width) in enumerate(chunks(ORDER[o], t))]

        def number(h, o, t, j=0):
            return PER_HEAD * h + START[o] + t * (ORDER[o] + 1) + j

        def following(h, u, o, last):
            if o < 3:
                return h, u, o + 1
            return None if last else (h + 1, 1 - u, 0)

        def piece(u, p):
            if p >= 8:
                tiles = slice((p - 8) * 4, (p - 7) * 4)
                src, high = v_raw[:, tiles], v_two[u][:, tiles, 0:HEAD]
                return (src, high), (src, high, v_two[u][:, tiles, HEAD:])
            cols = slice(p // 2 * CH, (p // 2 + 1) * CH)
            raw, hi, lo = ((q_raw, q_hi, q_lo), (k_raw, k_hi, k_lo))[p % 2]
            src, high = raw[:, cols], hi[u][:, cols]
            if lo is None:
                return (src, high), (raw[SBD:, cols], hi[u][SBD:, cols], hi[u][SBD:, cols])
            return (src, high), (src, high, lo[u][:, cols])

        def piece_free(engine, h, p):
            if p == 0:
                engine.wait_ge(raw_loaded, 16 * loads * (h + 2))
                engine.wait_ge(scored, number(h, 0, 3, ORDER[0] + 1))
            if p == 8:
                engine.wait_ge(pv_done, WT + PER_HEAD * h)

        @block.sync
        def _(sp):
            def load_operands(h, cols=slice(0, S), done=raw_loaded):
                if soft:
                    sp.dma_start(q_raw[0:NOPE, cols], q_src[0][bass.ds(h * NOPE, NOPE), cols]).then_inc(done, 16)
                    sp.dma_start(q_raw[NOPE:, cols], q_src[1][bass.ds(h * ROPE, ROPE), cols]).then_inc(done, 16)
                    sp.dma_start(k_raw[0:NOPE, cols], k_src[0][bass.ds(h * NOPE, NOPE), cols]).then_inc(done, 16)
                    sp.dma_start(k_raw[NOPE:, cols], k_src[1][:, cols]).then_inc(done, 16)
                else:
                    for half in range(2):
                        part = slice(half * SBD, (half + 1) * SBD)
                        sp.dma_start(q_raw[part, cols], q_src[bass.ds(h * SBD, SBD), cols]).then_inc(done, 16)
                        sp.dma_start(k_raw[part, cols], k_src[bass.ds(h * SBD, SBD), cols]).then_inc(done, 16)

            def load_v(h):
                sp.dma_start(v_raw[:], v_src[:, bass.ds(h * HEAD, HEAD)].rearrange("(t p) f -> p t f", p=P)
                             ).then_inc(raw_loaded, 16)

            def load_gate(i, u, o):
                g = ORDER[o]
                sp.wait_ge(gated, 4 * (2 * i + u) + o + 1)
                sp.sem_inc(passed, 1)
                sp.dma_start(gate[:, o % 2],
                             projT[bass.ds(gate_block + i, 1), u * HEAD:(u + 1) * HEAD, g * CH:(g + 1) * CH
                                   ].squeeze(0)).then_inc(gate_loaded[o % 2], 16)

            def body(i, u, last):
                h = 2 * i + u
                for o in range(4):
                    g = ORDER[o]
                    nxt = following(h, u, o, last)
                    if nxt:
                        load_gate(i + int(o == 3 and u == 1), nxt[1], nxt[2])
                    sp.wait_ge(gated, 2 + 4 * h + o + 1)
                    sp.sem_inc(passed, 1)
                    sp.dma_start(ogT[bass.ds(h * HEAD, HEAD), g * CH:(g + 1) * CH], og[:, o % 2]
                                 ).then_inc(stored[o % 2], 16)
                    if o == 3 and not last and not (isinstance(i, int) and u == 0):
                        sp.wait_ge(split, PIECES * (h + 2))
                        sp.sem_inc(passed, 1)
                        load_operands(h + 2)
                        load_v(h + 2)

            for b in range(2):
                sp.sem_inc(stored[b], 16)
            load_operands(0, slice(0, S // 2), first_loaded)
            load_operands(0, slice(S // 2, S))
            load_v(0)
            load_gate(0, 0, 0)
            sp.wait_ge(split, PIECES)
            load_operands(1)
            load_v(1)
            heads(sp, body)
            for b in range(2):
                sp.wait_ge(stored[b], 16 + 16 * 2 * H)

        @block.gpsimd
        def _(pool):
            pool.sem_inc(weighted, 2)
            pool.sem_inc(gated, 2)
            pool.memset(mask[:], BIG).then_inc(consts, 1)
            pool.memset(ones[:], 1.0).then_inc(consts, 1)
            if not soft:
                pool.memset(after[:, :, S:S + 1], 1.0).then_inc(consts, 1)
            pool.wait_ge(consts, 2 if soft else 3)
            pool.affine_select(out=mask[:], in_=mask[:], compare_op=ALU.is_ge if soft else ALU.is_gt,
                               fill=-BIG, base=0, pattern=[[-1, P]], channel_multiplier=1
                               ).then_inc(consts, 1)

            def weigh(h, o, t, j, k, width):
                at, off = k * CH, S - (4 * ORDER[o] + t + 1) * P
                pool.wait_ge(scanned, KEEPS + number(h, o, t, j) + 1)
                pool.tensor_tensor(w[o % 2][:, t, at:at + width], w[o % 2][:, t, at:at + width],
                                   after[:, t % 2, off + at + 1:off + at + width + 1], ALU.mult
                                   ).then_inc(weighted, 1)

            def body(i, u, last):
                h = 2 * i + u
                weighed = number(h, 0, 3, ORDER[0] + 1)
                for kind, o, *args in timeline(last, piece=0, diagonal=2, weigh=4, gated=LATE + 3):
                    if kind == "piece":
                        p = args[0]
                        (src, high), (src_l, high_l, low) = piece(1 - u, p)
                        if soft:
                            piece_free(pool, h, p)
                            one = ones[0:src.shape[0], 0:1]
                            one = (one.broadcast_to([src.shape[0], CH]) if p < 8
                                   else one.unsqueeze(2).broadcast_to([P, 4, HEAD]))
                            pool.tensor_tensor(high, src, one, ALU.mult).then_inc(split_high, 1)
                        elif p % 2 == 0 and p < 8:
                            pool.wait_ge(weighted, 2 + weighed)
                        pool.wait_ge(split_high, PIECES * (h + 1) + p + 1)
                        pool.tensor_tensor(low, src_l, as_f32(high_l), ALU.subtract).then_inc(split, 1)
                        if p < 8 and not soft:
                            pool.wait_ge(split, PIECES * (h + 1) + p + 1)
                    if kind == "diagonal" and soft:
                        for tt in range(4):
                            pool.wait_ge(inverted, 4 * h + o + 1)
                            pool.wait_ge(turned, items * h + item_at[o] + 1)
                            at = 4 * o + tt
                            pool.tensor_tensor(diag[:, tt], ident[:],
                                               inv_sum[:, at:at + 1].broadcast_to([P, P]), ALU.mult
                                               ).then_inc(diag_ready, 1)
                    if kind == "weigh" and not soft:
                        nxt = following(h, u, (o - 1) % 4, last)
                        weigh(nxt[0], *([o] + args))
                        weighed = number(nxt[0], o, *args[:2]) + 1
                    if kind == "gated":
                        seq = 4 * h + o
                        pool.wait_ge(stored[o % 2], 16 * (2 * h + o // 2 + 1))
                        if soft:
                            pool.wait_ge(turn_freed, turn_banks + items * h + item_at[o] + per_pos[o])
                        else:
                            pool.wait_ge(gate_loaded[o % 2], 16 * (2 * h + o // 2 + 1))
                        pool.wait_ge(o_summed, 2 + seq + 1)
                        by = gate_n if soft else gate
                        pool.tensor_tensor(og[:, o % 2], o_sum[:, o % 2], by[:, o % 2], ALU.mult
                                           ).then_inc(gated, 1)

            if not soft:
                for it in all_chunks(0):
                    weigh(0, 0, *it)
            heads(pool, body)

        @block.tensor
        def _(pe):
            pe.sem_inc(pv_done, WT)
            pe.wait_ge(consts, 3 if soft else 4)

            def scores(h, u, o, t, j, key, width):
                g = ORDER[o]
                q_cols = slice((4 * g + t) * P, (4 * g + t + 1) * P)
                if t == 0 and j == 0 and o < 3:
                    pe.wait_ge(split, PIECES * h + 2 * (max(ORDER[:o + 1]) + 1))
                pe.wait_ge(freed, number(h, o, t, j) + 1)
                bank = score[number(0, o, t, j) % score_banks][:, 0:width]
                keys = slice(key * CH, key * CH + width)
                if soft:
                    passes = [(q_hi, k_hi), (q_hi, k_lo), (q_lo, k_hi)]
                else:
                    passes = [(q_hi, k_hi), (q_hi, k_lo)]
                for m, (a, b) in enumerate(passes):
                    mm = pe.matmul(bank, a[u][:, q_cols], b[u][:, keys], start=(m == 0),
                                   stop=(m == len(passes) - 1))
                mm.then_inc(scored, 1)

            def times_v(h, u, o, j):
                g = ORDER[o]
                seq = PER_HEAD * h + START[o] + j
                b = (START[o] + j) % WT
                first = max(0, j - 4 * g) * P
                pe.wait_ge(turn_freed, turn_banks + items * h + item_at[o] + j + 1)
                if j == 0 and o == 0:
                    pe.wait_ge(split, PIECES * (h + 1))
                if j == 0:
                    pe.wait_ge(o_summed, 4 * h + o + 1)
                for m, part in enumerate((wT_hi, wT_lo)):
                    mm = pe.matmul(o_ps[o % 2][:, first:], v_two[u][:, j], part[b][:, first:],
                                   start=(j == 0 and m == 0), stop=(j == 4 * g + 3 and m == 1))
                mm.then_inc(pv_done, 1)

            def body(i, u, last):
                h = 2 * i + u
                for kind, o, *args in timeline(last, scores=0, turn=0, sums=0, times_v=LATE):
                    if kind == "scores":
                        nxt = following(h, u, (o - 1) % 4, last)
                        scores(nxt[0], nxt[1], *([o] + args))
                    if kind == "sums":
                        it = item_at[o] + 4 * (ORDER[o] + 1)
                        pe.wait_ge(turn_freed, items * h + it + 1)
                        pe.wait_ge(diag_ready, 16 * h + 4 * o + 4)
                        for tt in range(4):
                            mm = pe.matmul(turn[it % turn_banks][:, tt * P:(tt + 1) * P], ones[:], diag[:, tt],
                                           start=True, stop=True)
                        mm.then_inc(turned, 1)
                    if kind == "turn":
                        j = args[0]
                        it = item_at[o] + j
                        if j == 0:
                            pe.wait_ge(*weights_ready(h, o))
                        pe.wait_ge(turn_freed, items * h + it + 1)
                        for tt in range(max(0, j - 4 * ORDER[o]), 4):
                            mm = pe.transpose(turn[it % turn_banks][:, tt * P:(tt + 1) * P],
                                              w[o % 2][:, tt, j * P:(j + 1) * P], ident[:])
                        mm.then_inc(turned, 1)
                    if kind == "times_v":
                        times_v(h, u, o, args[0])

            for it in all_chunks(0):
                scores(0, 0, 0, *it)
            heads(pe, body)

        @block.scalar
        def _(act):
            if not soft:
                act.sem_inc(freed, score_banks)

            def weights(h, o, t, j, key, width):
                g, pos = ORDER[o], 4 * o + t
                if soft:
                    if j == g:
                        row = w[o % 2][:, t, 0:(4 * g + t + 1) * P]
                        act.wait_ge(shift_ready, 16 * h + pos + 1)
                        act.activation(row, row, ACT.Exp, scale=scale, bias=neg_max[:, pos:pos + 1],
                                       accum_out=sums[:, pos:pos + 1]).then_inc(exp_done, 1)
                    return
                if key == g:
                    act.wait_ge(masked, 16 * h + pos + 1)
                else:
                    act.wait_ge(scored, number(h, o, t, j) + 1)
                act.wait_ge(scanned, number(h, o, t, j) + 1)
                r = number(0, o, t, j) % KEEPS
                bank = score[number(0, o, t, j) % score_banks][:, 0:width]
                act.activation(keep[:, r, 0:width], bank, ACT.Sigmoid, scale=-scale)
                act.activation(w[o % 2][:, t, key * CH:key * CH + width], bank, ACT.Sigmoid, scale=scale
                               ).then_inc(freed, 1)

            def body(i, u, last):
                h = 2 * i + u
                for kind, o, *args in timeline(last, high=1.5, o_low=LATE + 1, **({"exp": EXP_LAG} if soft
                                               else {"sigmoids": 2, "piece": 0})):
                    if kind == "piece":
                        piece_free(act, h, args[0])
                        src, high = piece(1 - u, args[0])[0]
                        act.activation(high, src, ACT.Copy).then_inc(split_high, 1)
                    if kind in ("exp", "sigmoids"):
                        nxt = following(h, u, (o - 1) % 4, last)
                        weights(nxt[0], *([o] + args))
                    if kind == "high":
                        j = args[0]
                        it, b = item_at[o] + j, (START[o] + j) % WT
                        first = max(0, j - 4 * ORDER[o]) * P
                        act.wait_ge(turned, items * h + it + 1)
                        act.wait_ge(pv_done, PER_HEAD * h + START[o] + j + 1)
                        act.activation(wT_hi[b][:, first:], turn[it % turn_banks][:, first:], ACT.Copy
                                       ).then_inc(turn_high, 1)
                    if kind == "o_low":
                        act.wait_ge(pv_done, WT + PER_HEAD * h + START[o] + 4 * (ORDER[o] + 1))
                        act.activation(o_low[:, o % 2], o_ps[o % 2][HEAD:], ACT.Copy).then_inc(low_copied, 1)

            act.wait_ge(first_loaded, 16 * (loads - 1))
            for p in range(PIECES):
                if p == 4:
                    act.wait_ge(raw_loaded, 16 * loads)
                src, high = piece(0, p)[0]
                act.activation(high, src, ACT.Copy).then_inc(split_high, 1)
            for it in all_chunks(0):
                weights(0, 0, *it)
            heads(act, body)

        @block.vector
        def _(dve):
            dve.sem_inc(turn_freed, turn_banks)
            dve.sem_inc(o_summed, 2)
            if not soft:
                dve.sem_inc(scanned, KEEPS)
            dve.wait_ge(consts, 3 if soft else 4)

            def after_scores(h, o, t, j, key, width):
                g, pos = ORDER[o], 4 * o + t
                bank = score[number(0, o, t, j) % score_banks]
                dve.wait_ge(scored, number(h, o, t, j) + 1)
                if key == g:
                    diagonal = bank[:, t * P:(t + 1) * P]
                    dve.tensor_tensor(diagonal, diagonal, mask[:], ALU.min).then_inc(masked, 1)
                if soft:
                    if key == g:
                        dve.wait_ge(masked, 16 * h + pos + 1)
                    dve.tensor_scalar(w[o % 2][:, t, key * CH:key * CH + width], bank[:, 0:width], 1.0, None,
                                      ALU.mult, ALU.max, accum_out=maxes[:, pos, key:key + 1]
                                      ).then_inc(freed, 1)
                    if key == g:
                        dve.wait_ge(freed, score_banks + number(h, o, t, g + 1))
                        dve.tensor_reduce(top[:, pos:pos + 1], maxes[:, pos, 0:g + 1], AX_X, ALU.max
                                          ).then_inc(top_done, 1)
                        dve.wait_ge(top_done, 16 * h + pos + 1)
                        dve.tensor_scalar(neg_max[:, pos:pos + 1], top[:, pos:pos + 1], -scale, None,
                                          ALU.mult).then_inc(shift_ready, 1)

            def scan(h, o, t, j, key, width):
                g = ORDER[o]
                off = S - (4 * g + t + 1) * P
                r = number(0, o, t, j) % KEEPS
                dve.wait_ge(freed, score_banks + number(h, o, t, j) + 1)
                if j == 0:
                    prev = number(h, o, t - 2) if t >= 2 else (
                        number(h, o - 1, t + 2) if o else number(h, 0, 0) - (2 - t) * (ORDER[3] + 1))
                    size = ORDER[o if t >= 2 else o - 1] + 1
                    dve.wait_ge(weighted, 2 + prev + size)
                else:
                    dve.wait_ge(scanned, KEEPS + number(h, o, t, j))
                at = off + key * CH
                dve.tensor_tensor_scan(after[:, t % 2, at:at + width][:, ::-1], keep[:, r, 0:width][:, ::-1],
                                       keep[:, r, 0:width][:, ::-1],
                                       after[:, t % 2, at + width:at + width + 1], ALU.mult, ALU.bypass
                                       ).then_inc(scanned, 1)

            def body(i, u, last):
                h = 2 * i + u
                for kind, o, *args in timeline(last, to_sbuf=0.5, scan=3, low=2, invert=1.5, gate_n=1,
                                               o_sum=LATE + 2):
                    if kind == "to_sbuf":
                        nxt = following(h, u, (o - 1) % 4, last)
                        after_scores(nxt[0], *([o] + args))
                    if kind == "scan" and not soft:
                        nxt = following(h, u, (o - 1) % 4, last)
                        scan(nxt[0], *([o] + args))
                    if kind == "low":
                        j = args[0]
                        it, b = item_at[o] + j, (START[o] + j) % WT
                        first = max(0, j - 4 * ORDER[o]) * P
                        dve.wait_ge(turn_high, PER_HEAD * h + START[o] + j + 1)
                        dve.tensor_tensor(wT_lo[b][:, first:], turn[it % turn_banks][:, first:],
                                          as_f32(wT_hi[b][:, first:]), ALU.subtract
                                          ).then_inc(turn_freed, 1)
                    if kind == "invert" and soft:
                        at = 4 * o
                        dve.wait_ge(*weights_ready(h, o))
                        dve.reciprocal(inv_sum[:, at:at + 4], sums[:, at:at + 4]).then_inc(inverted, 1)
                    if kind == "gate_n":
                        it = item_at[o] + 4 * (ORDER[o] + 1)
                        dve.wait_ge(gate_loaded[o % 2], 16 * (2 * h + o // 2 + 1))
                        dve.wait_ge(gated, 4 * h + o + 1)
                        dve.wait_ge(turned, items * h + it + 1)
                        dve.tensor_tensor(gate_n[:, o % 2], turn[it % turn_banks][0:HEAD], gate[:, o % 2],
                                          ALU.mult).then_inc(turn_freed, 1)
                    if kind == "o_sum":
                        dve.wait_ge(low_copied, 4 * h + o + 1)
                        dve.wait_ge(gated, 4 * h + o + 1)
                        dve.tensor_tensor(o_sum[:, o % 2], o_ps[o % 2][0:HEAD], o_low[:, o % 2], ALU.add
                                          ).then_inc(o_summed, 1)

            if soft:
                dve.sem_inc(freed, score_banks)
            for p in range(PIECES):
                dve.wait_ge(split_high, p + 1)
                src, high, low = piece(0, p)[1]
                dve.tensor_tensor(low, src, as_f32(high), ALU.subtract).then_inc(split, 1)
            for it in all_chunks(0):
                after_scores(0, 0, *it)
                if not soft:
                    scan(0, 0, *it)
            heads(dve, body)


def attend_memory(nc, mem, w_mem, projT, ogT, ident):
    scale = float(MD) ** -0.5
    ITEMS = MT + 1
    with Scope(nc) as c:
        mem_raw = c.sb("mem_raw", [P, MT, D])
        memT_hi = c.sb("memT_hi", [P, KT, MEM], F32R)
        memT_lo = c.sb("memT_lo", [P, KT, MEM], F32R)
        w_raw = c.sb("wm_raw", [P, 4, D])
        w_hi = c.sb("wm_hi", [P, KT, D], F32R)
        w_lo = c.sb("wm_lo", [P, KT, D], F32R)
        k_hi = c.sb("mem_k_hi", [P, MH, MEM], F32R)
        k_lo = c.sb("mem_k_lo", [P, MH, MEM], F32R)
        v_hi = c.sb("mem_v_hi", [P, MT, MH * MD], F32R)
        v_lo = c.sb("mem_v_lo", [P, MT, MH * MD], F32R)
        q_raw = c.sb("mem_q_raw", [P, MH, CH])
        q_hi = [c.sb(f"mem_q_hi{b}", [P, CH], F32R) for b in range(MH)]
        q_lo = [c.sb(f"mem_q_lo{b}", [P, CH], F32R) for b in range(MH)]
        gate = c.sb("mem_gate", [P, MH, CH])
        w = c.sb("mem_w", [P, 2, 4, MEM])
        wT_hi = [c.sb(f"mem_wT_hi{b}", [P, CH], F32R) for b in range(2)]
        wT_lo = [c.sb(f"mem_wT_lo{b}", [P, CH], F32R) for b in range(2)]
        top = c.sb("mem_top", [P, 2, 4])
        neg_max = c.sb("mem_neg_max", [P, 2, 4])
        sums = c.sb("mem_sums", [P, 2, 4])
        inv_sum = c.sb("mem_inv_sum", [P, 2, 4])
        diag = c.sb("mem_diag", [P, 2, 4, P])
        gate_n = c.sb("mem_gate_n", [P, 2, CH])
        og = c.sb("mem_og", [P, 2, CH])
        ones = c.sb("mem_ones", [P, P])
        score = [c.ps(f"mem_score{b}", [P, 2, 2, MEM]) for b in range(2)]
        turn = [c.ps(f"mem_turn{b}", [P, CH]) for b in range(2)]
        o_ps = [c.ps(f"mem_o{b}", [P, CH]) for b in range(2)]

        mem_loaded = c.sem("mem_loaded")
        wm_loaded = [c.sem(f"wm_loaded{b}") for b in range(4)]
        ones_set = c.sem("mem_ones_set")
        wm_high = c.sem("wm_high")
        wm_low = c.sem("wm_low")
        mem_turned = c.sem("mem_turned")
        mem_high = c.sem("mem_high")
        mem_low = c.sem("mem_low")
        kv_done = c.sem("mem_kv_done")
        kv_high = c.sem("mem_kv_high")
        kv_low = c.sem("mem_kv_low")
        q_loaded = [c.sem(f"mem_q_loaded{b}") for b in range(MH)]
        gate_loaded = [c.sem(f"mem_gate_loaded{b}") for b in range(MH)]
        q_high = c.sem("mem_q_high")
        q_split = c.sem("mem_q_split")
        scored = c.sem("mem_scored")
        top_done = c.sem("mem_top_done")
        shift_ready = c.sem("mem_shift_ready")
        exp_done = c.sem("mem_exp_done")
        inverted = c.sem("mem_inverted")
        diag_ready = c.sem("mem_diag_ready")
        turned = c.sem("mem_item_turned")
        turn_high = c.sem("mem_turn_high")
        turn_freed = c.sem("mem_turn_freed")
        pv_done = c.sem("mem_pv_done")
        gated = c.sem("mem_gated")
        stored = [c.sem(f"mem_stored{b}") for b in range(2)]
        passed = c.sem("mem_passed")
        block = c.block()

        prep = [turn[0], turn[1], o_ps[0], o_ps[1]]
        NPREP = KT // 2

        def chunks_of(engine, body):
            with engine.Fori(0, NCH - 1) as n:
                body(n, False)
            body(NCH - 1, True)

        def ahead(n, h, last, by):
            if h + by < MH:
                return n, h + by
            return None if last else (n + 1, h + by - MH)

        @block.sync
        def _(sp):
            sp.dma_start(mem_raw[:], mem.rearrange("b (t p) d -> p (b t) d", p=P)).then_inc(mem_loaded, 16)
            for k in range(KT):
                if k >= 4:
                    sp.wait_ge(wm_low, k - 3)
                sp.dma_start(w_raw[:, k % 4], w_mem[k]).then_inc(wm_loaded[k % 4], 16)
            for b in range(2):
                sp.sem_inc(stored[b], 16)

            def load(n, h):
                cols = bass.ds(n * CH, CH)
                sp.dma_start(q_raw[:, h], projT[B_COPY + 12 + h, :, cols]).then_inc(q_loaded[h], 16)
                sp.dma_start(gate[:, h], projT[B_GATE + 8 + h, :, cols]).then_inc(gate_loaded[h], 16)

            def body(n, last):
                for h in range(MH):
                    sp.wait_ge(gated, 2 + MH * n + h + 1)
                    sp.sem_inc(passed, 1)
                    sp.dma_start(ogT[h * MD:(h + 1) * MD, bass.ds(n * CH, CH)], og[:, h % 2]
                                 ).then_inc(stored[h % 2], 16)
                    if not last:
                        load(n + 1, h)

            for h in range(MH):
                load(0, h)
            chunks_of(sp, body)
            for b in range(2):
                sp.wait_ge(stored[b], 16 + 16 * NCH * MH // 2)

        @block.gpsimd
        def _(pool):
            pool.memset(ones[:], 1.0).then_inc(ones_set, 1)
            pool.wait_ge(ones_set, 1)

            def split_q(n, h):
                pool.wait_ge(q_loaded[h], 16 * (n + 1))
                pool.tensor_tensor(q_hi[h][:], q_raw[:, h], ones[:, 0:1].broadcast_to([P, CH]), ALU.mult
                                   ).then_inc(q_high, 1)
                pool.wait_ge(q_high, MH * n + h + 1)
                pool.tensor_tensor(q_lo[h][:], q_raw[:, h], as_f32(q_hi[h][:]), ALU.subtract
                                   ).then_inc(q_split, 1)

            def body(n, last):
                for h in range(MH):
                    b, unit = h % 2, MH * n + h
                    for t in range(4):
                        pool.wait_ge(inverted, unit + 1)
                        pool.tensor_tensor(diag[:, b, t], ident[:],
                                           inv_sum[:, b, t:t + 1].broadcast_to([P, P]), ALU.mult
                                           ).then_inc(diag_ready, 1)
                    if not (last and h >= MH - 3):
                        split_q(*ahead(n, h, last, 3))

            for h in range(3):
                split_q(0, h)
            chunks_of(pool, body)

        @block.tensor
        def _(pe):
            pe.sem_inc(pv_done, 2)
            pe.wait_ge(mem_loaded, 16)
            for m in range(NPREP):
                for j in range(2):
                    for t in range(MT):
                        at = (2 * j + t) * P
                        k = 2 * m + j
                        mm = pe.transpose(prep[m][:, at:at + P], mem_raw[:, t, k * P:(k + 1) * P], ident[:])
                mm.then_inc(mem_turned, 1)
            for m in range(MH + MT):
                bank = prep[m % 4][:]
                if m < 4:
                    pe.wait_ge(mem_low, m + 1)
                    bank = bank[:, 0:MEM]
                else:
                    pe.wait_ge(kv_low, m - 3)
                for k in range(KT):
                    if m == 0:
                        pe.wait_ge(mem_low, k // 2 + 1)
                        pe.wait_ge(wm_low, k + 1)
                    if m < MH:
                        cols = slice(m * MD, (m + 1) * MD)
                        a, b = (w_hi[:, k, cols], w_lo[:, k, cols]), (memT_hi[:, k], memT_lo[:, k])
                    else:
                        rows, cols = slice((m - MH) * P, (m - MH + 1) * P), slice(MH * MD, D)
                        a = memT_hi[:, k, rows], memT_lo[:, k, rows]
                        b = w_hi[:, k, cols], w_lo[:, k, cols]
                    pe.matmul(bank, a[0], b[0], start=(k == 0), stop=False)
                    pe.matmul(bank, a[0], b[1], start=False, stop=False)
                    mm = pe.matmul(bank, a[1], b[0], start=False, stop=(k == KT - 1))
                mm.then_inc(kv_done, 1)
            pe.wait_ge(kv_low, MH + MT)

            def scores(n, h):
                b, unit = h % 2, MH * n + h
                pe.wait_ge(q_split, unit + 1)
                pe.wait_ge(exp_done, unit + 1)
                for t in range(4):
                    rows = slice(t * P, (t + 1) * P)
                    bank = score[b][:, t // 2, t % 2]
                    pe.matmul(bank, q_hi[h][:, rows], k_hi[:, h], start=True, stop=False)
                    pe.matmul(bank, q_hi[h][:, rows], k_lo[:, h], start=False, stop=False)
                    mm = pe.matmul(bank, q_lo[h][:, rows], k_hi[:, h], start=False, stop=True)
                mm.then_inc(scored, 1)

            def body(n, last):
                for h in range(MH):
                    b, unit = h % 2, MH * n + h
                    nxt = ahead(n, h, last, 2)
                    feat = slice(h * MD, (h + 1) * MD)
                    pe.wait_ge(exp_done, 2 + unit + 1)
                    for m in range(MT):
                        it = ITEMS * h + m
                        pe.wait_ge(turn_freed, ITEMS * MH * n + it + 1)
                        for t in range(4):
                            mm = pe.transpose(turn[it % 2][:, t * P:(t + 1) * P],
                                              w[:, b, t, m * P:(m + 1) * P], ident[:])
                        mm.then_inc(turned, 1)
                    if nxt:
                        scores(*nxt)
                    it = ITEMS * h + MT
                    pe.wait_ge(turn_freed, ITEMS * MH * n + it + 1)
                    pe.wait_ge(diag_ready, 4 * (unit + 1))
                    for t in range(4):
                        mm = pe.matmul(turn[it % 2][:, t * P:(t + 1) * P], ones[:], diag[:, b, t],
                                       start=True, stop=True)
                    mm.then_inc(turned, 1)
                    pe.wait_ge(gated, unit + 1)
                    for m in range(MT):
                        it = ITEMS * h + m
                        pe.wait_ge(turn_freed, 2 + ITEMS * MH * n + it + 1)
                        pe.matmul(o_ps[b][:], v_hi[:, m, feat], wT_hi[m][:], start=(m == 0), stop=False)
                        pe.matmul(o_ps[b][:], v_hi[:, m, feat], wT_lo[m][:], start=False, stop=False)
                        mm = pe.matmul(o_ps[b][:], v_lo[:, m, feat], wT_hi[m][:], start=False,
                                       stop=(m == MT - 1))
                        mm.then_inc(pv_done, 1)

            pe.wait_ge(ones_set, 1)
            scores(0, 0)
            scores(0, 1)
            chunks_of(pe, body)

        @block.scalar
        def _(act):
            for m in range(NPREP):
                act.wait_ge(mem_turned, m + 1)
                act.activation(memT_hi[:, 2 * m:2 * m + 2].rearrange("p k s -> p (k s)"), prep[m][:], ACT.Copy
                               ).then_inc(mem_high, 1)
            for k in range(KT):
                act.wait_ge(wm_loaded[k % 4], 16 * (k // 4 + 1))
                act.activation(w_hi[:, k], w_raw[:, k % 4], ACT.Copy).then_inc(wm_high, 1)
            for m in range(MH + MT):
                act.wait_ge(kv_done, m + 1)
                src, dst = ((prep[m % 4][:, 0:MEM], k_hi[:, m]) if m < MH
                            else (prep[m % 4][:], v_hi[:, m - MH]))
                act.activation(dst, src, ACT.Copy).then_inc(kv_high, 1)

            def exps(n, h):
                b, unit = h % 2, MH * n + h
                act.wait_ge(shift_ready, unit + 1)
                for t in range(4):
                    ex = act.activation(w[:, b, t], score[b][:, t // 2, t % 2], ACT.Exp, scale=scale,
                                        bias=neg_max[:, b, t:t + 1], accum_out=sums[:, b, t:t + 1])
                ex.then_inc(exp_done, 1)

            def body(n, last):
                for h in range(MH):
                    nxt = ahead(n, h, last, 1)
                    for m in range(MT):
                        it = ITEMS * h + m
                        act.wait_ge(turned, ITEMS * MH * n + it + 1)
                        act.wait_ge(pv_done, MT * (MH * n + h) + m + 1)
                        act.activation(wT_hi[m][:], turn[it % 2][:], ACT.Copy).then_inc(turn_high, 1)
                    if nxt:
                        exps(*nxt)

            act.sem_inc(exp_done, 2)
            exps(0, 0)
            chunks_of(act, body)

        @block.vector
        def _(dve):
            dve.sem_inc(turn_freed, 2)
            dve.sem_inc(gated, 2)
            for m in range(NPREP):
                dve.wait_ge(mem_high, m + 1)
                part = slice(2 * m, 2 * m + 2)
                dve.tensor_tensor(memT_lo[:, part].rearrange("p k s -> p (k s)"), prep[m][:],
                                  as_f32(memT_hi[:, part]).rearrange("p k s -> p (k s)"), ALU.subtract
                                  ).then_inc(mem_low, 1)
            for k in range(KT):
                dve.wait_ge(wm_high, k + 1)
                dve.tensor_tensor(w_lo[:, k], w_raw[:, k % 4], as_f32(w_hi[:, k]), ALU.subtract
                                  ).then_inc(wm_low, 1)
            for m in range(MH + MT):
                dve.wait_ge(kv_high, m + 1)
                src, hi, lo = ((prep[m % 4][:, 0:MEM], k_hi[:, m], k_lo[:, m]) if m < MH
                               else (prep[m % 4][:], v_hi[:, m - MH], v_lo[:, m - MH]))
                dve.tensor_tensor(lo, src, as_f32(hi), ALU.subtract).then_inc(kv_low, 1)

            def maxima(n, h):
                b, unit = h % 2, MH * n + h
                dve.wait_ge(scored, unit + 1)
                for half in range(2):
                    dve.tensor_reduce(top[:, b, 2 * half:2 * half + 2], score[b][:, half], AX_X, ALU.max
                                      ).then_inc(top_done, 1)
                dve.wait_ge(top_done, 2 * (unit + 1))
                dve.tensor_scalar(neg_max[:, b], top[:, b], -scale, None, ALU.mult).then_inc(shift_ready, 1)

            def body(n, last):
                for h in range(MH):
                    b, unit = h % 2, MH * n + h
                    dve.wait_ge(exp_done, 2 + unit + 1)
                    dve.reciprocal(inv_sum[:, b], sums[:, b]).then_inc(inverted, 1)
                    nxt = ahead(n, h, last, 1)
                    if nxt:
                        maxima(*nxt)
                    for m in range(MT):
                        it = ITEMS * h + m
                        dve.wait_ge(turn_high, MT * unit + m + 1)
                        dve.tensor_tensor(wT_lo[m][:], turn[it % 2][:], as_f32(wT_hi[m][:]), ALU.subtract
                                          ).then_inc(turn_freed, 1)
                    it = ITEMS * h + MT
                    dve.wait_ge(gate_loaded[h], 16 * (n + 1))
                    dve.wait_ge(turned, ITEMS * MH * n + it + 1)
                    dve.tensor_tensor(gate_n[:, b], turn[it % 2][:], gate[:, h], ALU.mult
                                      ).then_inc(turn_freed, 1)
                    dve.wait_ge(stored[b], 16 * (2 * n + h // 2 + 1))
                    dve.wait_ge(turn_freed, 2 + ITEMS * MH * n + it + 1)
                    dve.wait_ge(pv_done, 2 + MT * (unit + 1))
                    dve.tensor_tensor(og[:, b], o_ps[b][:], gate_n[:, b], ALU.mult).then_inc(gated, 1)

            maxima(0, 0)
            chunks_of(dve, body)


def merge_branches(nc, ogT, w_branch, projT, mergedT):
    NBR, KB, FB = 3, 4, D // P
    PARTS = NBR * KB
    with Scope(nc) as c:
        w_raw = c.sb("wb_raw", [P, 2, PARTS, P])
        w_hi = c.sb("wb_hi", [P, FB, PARTS, P], F32R)
        w_lo = c.sb("wb_lo", [P, FB, PARTS, P], F32R)
        o_raw = c.sb("mo_raw", [P, 2, KB, CH])
        o_hi = c.sb("mo_hi", [P, PARTS, CH], F32R)
        o_lo = c.sb("mo_lo", [P, PARTS, CH], F32R)
        gate = c.sb("mg_gate", [P, 2, NBR, CH])
        prod = c.sb("mg_prod", [P, 2, NBR, CH])
        merged = c.sb("merged", [P, 2, CH])
        ps = [[c.ps(f"mg_ps{s}{b}", [P, CH]) for b in range(NBR)] for s in range(2)]
        w_loaded = [c.sem(f"wb_loaded{b}") for b in range(2)]
        w_high = c.sem("wb_high")
        w_low = c.sem("wb_low")
        o_loaded = [c.sem(f"mo_loaded{b}") for b in range(2)]
        o_high = c.sem("mo_high")
        o_split = c.sem("mo_split")
        g_loaded = [c.sem(f"mg_loaded{b}") for b in range(2)]
        product = c.sem("mg_product")
        scaled = c.sem("mg_scaled")
        added = c.sem("mg_added")
        stored = [c.sem(f"mg_stored{b}") for b in range(2)]
        passed = c.sem("mg_passed")
        block = c.block()
        gates = projT[B_MERGE:].rearrange("(b f) p s -> f p b s", b=NBR)

        def chunks_of(engine, body):
            body(0, True, False)
            with engine.Fori(1, NCH - 1) as n:
                body(n, False, False)
            body(NCH - 1, False, True)

        @block.sync
        def _(sp):
            def load_gates(n, f):
                sp.dma_start(gate[:, f % 2], gates[f][:, :, bass.ds(n * CH, CH)]).then_inc(g_loaded[f % 2], 16)

            def load_outputs(n, b):
                sp.dma_start(o_raw[:, b % 2],
                             ogT[b, :, bass.ds(n * CH, CH)].rearrange("(k p) s -> p k s", p=P)
                             ).then_inc(o_loaded[b % 2], 16)

            def load_weights(f):
                sp.dma_start(w_raw[:, f % 2], w_branch[f]).then_inc(w_loaded[f % 2], 16)

            def store(n, f):
                sp.wait_ge(added, 2 * (FB * n + f + 1))
                sp.sem_inc(passed, 1)
                sp.dma_start(mergedT[f * P:(f + 1) * P, bass.ds(n * CH, CH)], merged[:, f % 2]
                             ).then_inc(stored[f % 2], 16)

            def body(n, first, last):
                if first:
                    load_outputs(0, 0)
                    load_weights(0)
                    load_outputs(0, 1)
                    load_weights(1)
                sp.wait_ge(o_split, PARTS * n + KB)
                sp.sem_inc(passed, 1)
                load_outputs(n, 2)
                for f in range(FB):
                    unit = FB * n + f
                    if not (first and f < 2):
                        sp.wait_ge(scaled, 3 * unit + 3)
                        sp.sem_inc(passed, 1)
                    load_gates(n, f)
                    if first and f + 2 < FB:
                        sp.wait_ge(w_low, f + 1)
                        load_weights(f + 2)
                    if f:
                        store(n, f - 1)
                    elif not first:
                        store(n - 1, FB - 1)
                    if f == 2 and not last:
                        sp.wait_ge(o_split, PARTS * (n + 1))
                        sp.sem_inc(passed, 1)
                        load_outputs(n + 1, 0)
                        load_outputs(n + 1, 1)
                if last:
                    store(n, FB - 1)

            chunks_of(sp, body)
            for b in range(2):
                sp.wait_ge(stored[b], 16 + 16 * NCH * FB // 2)

        @block.tensor
        def _(pe):
            def body(n, first, last):
                for f in range(FB):
                    unit = FB * n + f
                    if first:
                        pe.wait_ge(w_low, f + 1)
                    for b in range(NBR):
                        bank = ps[f % 2][b]
                        pe.wait_ge(scaled, 3 * unit + b + 1)
                        for k in range(KB):
                            part = b * KB + k
                            if f == 0:
                                pe.wait_ge(o_split, PARTS * n + part + 1)
                            pe.matmul(bank[:], w_hi[:, f, part], o_hi[:, part], start=(k == 0), stop=False)
                            pe.matmul(bank[:], w_hi[:, f, part], o_lo[:, part], start=False, stop=False)
                            mm = pe.matmul(bank[:], w_lo[:, f, part], o_hi[:, part], start=False,
                                           stop=(k == KB - 1))
                        mm.then_inc(product, 1)

            chunks_of(pe, body)

        def slot_loads(n, b):
            return 2 * n + b // 2 + 1 if b % 2 == 0 else n + 1

        @block.scalar
        def _(act):
            def body(n, first, last):
                for part in range(PARTS):
                    b, k = divmod(part, KB)
                    if first and part in (KB, 2 * KB):
                        weights(part // KB - 1)
                    act.wait_ge(o_loaded[b % 2], 16 * slot_loads(n, b))
                    if not first:
                        act.wait_ge(product, NBR * (FB * n - 1) + b + 1)
                    act.activation(o_hi[:, part], o_raw[:, b % 2, k], ACT.Copy).then_inc(o_high, 1)
                if first:
                    for f in range(2, FB):
                        weights(f)

            def weights(f):
                act.wait_ge(w_loaded[f % 2], 16 * (f // 2 + 1))
                act.activation(w_hi[:, f], w_raw[:, f % 2], ACT.Copy).then_inc(w_high, 1)

            chunks_of(act, body)

        @block.vector
        def _(dve):
            dve.sem_inc(scaled, 6)

            def weights(f):
                dve.wait_ge(w_high, f + 1)
                dve.tensor_tensor(w_lo[:, f], w_raw[:, f % 2], as_f32(w_hi[:, f]), ALU.subtract
                                  ).then_inc(w_low, 1)

            def body(n, first, last):
                for part in range(PARTS):
                    b, k = divmod(part, KB)
                    if first and part in (KB, 2 * KB):
                        weights(part // KB - 1)
                    dve.wait_ge(o_high, PARTS * n + part + 1)
                    dve.tensor_tensor(o_lo[:, part], o_raw[:, b % 2, k], as_f32(o_hi[:, part]), ALU.subtract
                                      ).then_inc(o_split, 1)
                for f in range(FB):
                    unit = FB * n + f
                    if first and f + 2 < FB:
                        weights(f + 2)
                    dve.wait_ge(g_loaded[f % 2], 16 * (FB // 2 * n + f // 2 + 1))
                    if not (first and f < 2):
                        dve.wait_ge(added, 2 * unit - 2)
                    for b in range(NBR):
                        dve.wait_ge(product, NBR * unit + b + 1)
                        dve.tensor_tensor(prod[:, f % 2, b], ps[f % 2][b][:], gate[:, f % 2, b], ALU.mult
                                          ).then_inc(scaled, 1)

            chunks_of(dve, body)

        @block.gpsimd
        def _(pool):
            for b in range(2):
                pool.sem_inc(stored[b], 16)

            def body(n, first, last):
                for f in range(FB):
                    unit, u = FB * n + f, f % 2
                    pool.wait_ge(stored[u], 16 * (FB // 2 * n + f // 2 + 1))
                    pool.wait_ge(scaled, 6 + 3 * unit + 2)
                    pool.tensor_tensor(merged[:, u], prod[:, u, 0], prod[:, u, 1], ALU.add
                                       ).then_inc(added, 1)
                    pool.wait_ge(scaled, 6 + 3 * unit + 3)
                    pool.wait_ge(added, 2 * unit + 1)
                    pool.tensor_tensor(merged[:, u], merged[:, u], prod[:, u, 2], ALU.add
                                       ).then_inc(added, 1)

            chunks_of(pool, body)


def project_out(nc, mergedT, w_out, x, ln, out):
    PIECES_W = 8
    RT = 4
    with Scope(nc) as c:
        w_raw = c.sb("wo_raw", [P, 4, 2, CH])
        w_hi = c.sb("wo_hi", [P, 2, KT, CH], F32R)
        w_lo = c.sb("wo_lo", [P, 2, KT, CH], F32R)
        m_raw = c.sb("m_raw", [P, RT, KT, P])
        m_hi = c.sb("m_hi", [P, RT, KT, P], F32R)
        m_lo = c.sb("m_lo", [P, RT, KT, P], F32R)
        x_sb = c.sb("x_out", [P, RT, D])
        ln_sb = c.sb("ln_gain_bias", [P, 2, D])
        y = c.sb("y", [P, 2, D])
        sq = c.sb("y_sq", [P, D])
        z = c.sb("z", [P, 2, D])
        stat = c.sb("ln_stat", [P, 2, 5])
        eps = c.sb("ln_eps", [P, 1])
        SUM, NEG_MEAN, SSQ, STD, RSTD = range(5)
        ps = [c.ps(f"out_ps{s}", [P, D]) for s in range(RT)]
        w_loaded = [c.sem(f"wo_loaded{b}") for b in range(4)]
        ln_loaded = c.sem("ln_loaded")
        eps_set = c.sem("ln_eps_set")
        w_high = c.sem("wo_high")
        w_low = c.sem("wo_low")
        m_loaded = [c.sem(f"m_loaded{u}") for u in range(RT)]
        m_high = c.sem("m_high")
        m_low = c.sem("m_low")
        x_loaded = [c.sem(f"x_out_loaded{u}") for u in range(RT)]
        product = c.sem("out_product")
        y_done = c.sem("y_done")
        mean_done = c.sem("mean_done")
        ssq_done = c.sem("ln_ssq_done")
        std_done = c.sem("std_done")
        rstd_done = c.sem("ln_rstd_done")
        gained = c.sem("gained")
        shifted = c.sem("shifted")
        stored = [c.sem(f"out_stored{u}") for u in range(2)]
        passed = c.sem("out_passed")
        block = c.block()
        xf = x.rearrange("b s d -> (b s) d")
        of = out.rearrange("b s d -> (b s) d")

        def turns(engine, body):
            with engine.Fori(0, TT // RT - 1) as i:
                body(i, False)
            body(TT // RT - 1, True)

        def w_piece(t, q):
            return t[:, q // 4, q % 4 * 2:q % 4 * 2 + 2]

        @block.sync
        def _(sp):
            def load_m(i, j):
                sp.dma_start(m_raw[:, j], mergedT[:, bass.ds((RT * i + j) * P, P)
                                                  ].rearrange("(k p) s -> p k s", p=P)).then_inc(m_loaded[j], 16)

            def load_x(i, j):
                sp.dma_start(x_sb[:, j], xf[bass.ds((RT * i + j) * P, P)]).then_inc(x_loaded[j], 16)

            load_m(0, 0)
            for q in range(PIECES_W):
                if q >= 4:
                    sp.wait_ge(w_low, q - 3)
                sp.dma_start(w_raw[:, q % 4], w_out[q // 4, :, q % 4 * 2:q % 4 * 2 + 2]
                             ).then_inc(w_loaded[q % 4], 16)
                if q == 3:
                    load_m(0, 1)
                    load_x(0, 0)
            sp.dma_start(ln_sb[:], ln).then_inc(ln_loaded, 16)
            for j in range(1, RT):
                load_x(0, j)
                if j > 1:
                    load_m(0, j)
            for u in range(2):
                sp.sem_inc(stored[u], 16)

            def body(i, last):
                for j in range(RT):
                    tile = RT * i + j
                    sp.wait_ge(shifted, tile + 1)
                    sp.sem_inc(passed, 1)
                    sp.dma_start(of[bass.ds(tile * P, P)], z[:, j % 2]).then_inc(stored[j % 2], 16)
                    if not last:
                        load_m(i + 1, j)
                        load_x(i + 1, j)

            turns(sp, body)
            for u in range(2):
                sp.wait_ge(stored[u], 16 + 16 * TT // 2)

        @block.tensor
        def _(pe):
            def product_tile(i, j, first):
                tile = RT * i + j
                pe.wait_ge(m_low, tile + 1)
                pe.wait_ge(y_done, tile + 1)
                for half in range(2):
                    bank = ps[j][:, half * CH:(half + 1) * CH]
                    for k in range(KT):
                        if first and k % 2 == 0:
                            pe.wait_ge(w_low, 4 * half + k // 2 + 1)
                        pe.matmul(bank, m_hi[:, j, k], w_hi[:, half, k], start=(k == 0), stop=False)
                        pe.matmul(bank, m_hi[:, j, k], w_lo[:, half, k], start=False, stop=False)
                        mm = pe.matmul(bank, m_lo[:, j, k], w_hi[:, half, k], start=False,
                                       stop=(k == KT - 1))
                mm.then_inc(product, 1)

            for j in range(RT):
                product_tile(0, j, j == 0)
            with pe.Fori(1, TT // RT) as i:
                for j in range(RT):
                    product_tile(i, j, False)

        @block.scalar
        def _(act):
            def high_m(i, j):
                act.wait_ge(m_loaded[j], 16 * (i + 1))
                act.activation(m_hi[:, j], m_raw[:, j], ACT.Copy).then_inc(m_high, 1)

            high_m(0, 0)
            for q in range(PIECES_W):
                act.wait_ge(w_loaded[q % 4], 16 * (q // 4 + 1))
                act.activation(w_piece(w_hi, q), w_raw[:, q % 4], ACT.Copy).then_inc(w_high, 1)
            high_m(0, 1)
            act.wait_ge(eps_set, 1)

            def body(i, last):
                for j in range(RT):
                    tile, u = RT * i + j, j % 2
                    if not (last and j >= 2):
                        high_m(i + j // 2, (j + 2) % RT)
                    act.wait_ge(mean_done, tile + 1)
                    act.activation(sq[:], y[:, u], ACT.Square, bias=stat[:, u, NEG_MEAN:NEG_MEAN + 1],
                                   accum_out=stat[:, u, SSQ:SSQ + 1]).then_inc(ssq_done, 1)
                    act.wait_ge(ssq_done, tile + 1)
                    act.activation(stat[:, u, STD:STD + 1], stat[:, u, SSQ:SSQ + 1], ACT.Sqrt,
                                   bias=eps[:, 0:1], scale=1.0 / D).then_inc(std_done, 1)

            turns(act, body)

        @block.vector
        def _(dve):
            dve.memset(eps[:], LN_EPS).then_inc(eps_set, 1)
            dve.sem_inc(y_done, RT)

            def low_m(i, j):
                dve.wait_ge(m_high, RT * i + j + 1)
                dve.tensor_tensor(m_lo[:, j], m_raw[:, j], as_f32(m_hi[:, j]), ALU.subtract
                                  ).then_inc(m_low, 1)

            low_m(0, 0)
            for q in range(PIECES_W):
                dve.wait_ge(w_high, q + 1)
                dve.tensor_tensor(w_piece(w_lo, q), w_raw[:, q % 4], as_f32(w_piece(w_hi, q)), ALU.subtract
                                  ).then_inc(w_low, 1)
            low_m(0, 1)
            dve.wait_ge(ln_loaded, 16)

            def body(i, last):
                for j in range(RT):
                    tile, u = RT * i + j, j % 2

                    def s(at):
                        return stat[:, u, at:at + 1]

                    if not (last and j >= 2):
                        low_m(i + j // 2, (j + 2) % RT)
                    dve.wait_ge(x_loaded[j], 16 * (i + 1))
                    dve.wait_ge(product, tile + 1)
                    dve.scalar_tensor_tensor(out=y[:, u], in0=x_sb[:, j], scalar=ALPHA, in1=ps[j][:],
                                             op0=ALU.mult, op1=ALU.add, accum_out=s(SUM)).then_inc(y_done, 1)
                    dve.wait_ge(y_done, RT + tile + 1)
                    dve.tensor_scalar(s(NEG_MEAN), s(SUM), -1.0 / D, None, ALU.mult).then_inc(mean_done, 1)
                    dve.wait_ge(mean_done, tile + 1)
                    dve.wait_ge(stored[u], 16 * (RT // 2 * i + j // 2 + 1))
                    dve.scalar_tensor_tensor(out=z[:, u], in0=y[:, u], scalar=s(NEG_MEAN), in1=ln_sb[:, 0],
                                             op0=ALU.add, op1=ALU.mult).then_inc(gained, 1)
                    dve.wait_ge(std_done, tile + 1)
                    dve.reciprocal(s(RSTD), s(STD)).then_inc(rstd_done, 1)
                    dve.wait_ge(rstd_done, tile + 1)
                    dve.wait_ge(gained, tile + 1)
                    dve.scalar_tensor_tensor(out=z[:, u], in0=z[:, u], scalar=s(RSTD), in1=ln_sb[:, 1],
                                             op0=ALU.mult, op1=ALU.add).then_inc(shifted, 1)

            turns(dve, body)


def build(nc, x, mem, w_all, rotary, gains, w_q, w_kv, w_mem, w_branch, w_out, ln, out, scratch):
    projT, qn, qp, kn, kp, va, vb, ogT, mergedT = scratch
    with Scope(nc) as c:
        ident = c.sb("ident", [P, P])
        with Scope(nc) as r:
            xTh = r.sb("xTh", [P, KT, S], F32R)
            xTl = r.sb("xTl", [P, KT, S], F32R)
            w = {"raw": r.sb("w_raw", [P, 2, KT * P + 1]),
                 "high": r.sb("w_high", [P, 2, KT * P], F32R),
                 "low": r.sb("w_low", [P, 2, KT * P], F32R),
                 "bias": r.sb("proj_bias", [P, 2])}
            ones = r.sb("ones", [P, 1])
            load_x_transposed(nc, x, w_all, w, ones, ident, xTh, xTl)
            project_x(nc, w_all, w, ones, projT, xTh, xTl)
        latent_heads(nc, projT, rotary, gains, w_q, w_kv, ident, qn, qp, kn, kp, va, vb)
        attend(nc, True, (qn, qp), (kn, kp), va, projT, B_GATE, ogT[0], ident)
        sb_q = projT[B_COPY:B_COPY + 4].rearrange("b p s -> (b p) s")
        sb_k = projT[B_COPY + 4:B_COPY + 8].rearrange("b p s -> (b p) s")
        attend(nc, False, sb_q, sb_k, vb, projT, B_GATE + 4, ogT[1], ident)
        attend_memory(nc, mem, w_mem, projT, ogT[2], ident)
    merge_branches(nc, ogT, w_branch, projT, mergedT)
    project_out(nc, mergedT, w_out, x, ln, out)


def rotary_table():
    half = ROPE // 2
    freqs = np.float32(10000.0) ** (-np.arange(half, dtype=np.float32) / np.float32(half))
    ang = freqs[:, None] * np.arange(S, dtype=np.float32)[None, :]
    cos, sin = np.cos(ang), np.sin(ang)
    return np.stack([np.tile(np.concatenate([cos, cos]), (4, 1)),
                     np.tile(np.concatenate([-sin, sin]), (4, 1))]).astype(np.float32)


def lay_out(inputs):
    w = np.asarray(inputs["w_in"])[0]
    rope = w[:, 384:416]
    swapped = np.concatenate([rope[:, 16:], rope[:, :16]], axis=1)
    col = lambda a, b: w[:, a:b]
    g = 416
    parts = [col(0, 384), rope, swapped, rope, swapped,
             col(g, g + 512), col(g + 2048, g + 2560), col(g + 3072, g + 3584),
             col(g + 512, g + 2048), col(g + 2560, g + 3072),
             np.asarray(inputs["w_merge_gate"])[0]]
    w_all = np.concatenate(parts, axis=1)
    w_all = w_all.reshape(KT, P, NBLK, P).transpose(2, 1, 0, 3).reshape(NBLK, P, KT * P)
    bias = np.zeros((NBLK, P, 1), w_all.dtype)
    bias[B_MERGE:, :, 0] = np.asarray(inputs["b_merge_gate"])[0].reshape(NB_MERGE, P)
    w_all = np.concatenate([w_all, bias], axis=2)
    q = np.asarray(inputs["w_q_b"])[0].reshape(QL, H, NOPE + ROPE)
    pe = q[..., NOPE:]
    swapped = np.concatenate([pe[..., ROPE // 2:], pe[..., :ROPE // 2]], axis=-1)
    w_q = np.concatenate([q[..., :NOPE].reshape(QL, -1), pe.reshape(QL, -1), swapped.reshape(QL, -1)], axis=1)
    kv = np.asarray(inputs["w_kv_b"])[0].reshape(KVL, H, NOPE + VD)
    w_kv = np.concatenate([kv[..., :NOPE].reshape(KVL, -1), kv[..., NOPE:].reshape(KVL, -1)], axis=1)
    gains = np.concatenate([np.asarray(inputs["q_a_gain"])[0], np.asarray(inputs["kv_a_gain"])[0]])
    gains = gains.reshape(3, P).T
    w_branch = np.concatenate([np.asarray(inputs[n])[0] for n in
                               ("w_branch_mla", "w_branch_sb", "w_branch_mem")])
    ln = np.stack([np.asarray(inputs["ln_gain"])[0], np.asarray(inputs["ln_bias"])[0]])
    return {
        "x": inputs["x"],
        "mem": inputs["mem"],
        "w_all": w_all,
        "rotary": rotary_table(),
        "gains": gains,
        "w_q": w_q.reshape(2, P, D).transpose(1, 0, 2),
        "w_kv": w_kv,
        "w_mem": np.asarray(inputs["w_mem_kv"])[0].reshape(KT, P, D),
        "w_branch": w_branch.reshape(12, P, KT, P).transpose(2, 1, 0, 3),
        "w_out": np.asarray(inputs["w_out"])[0].reshape(KT, P, 2, CH).transpose(2, 1, 0, 3),
        "ln": np.broadcast_to(ln, (P, 2, D)),
    }


def kernel(**inputs):
    import concourse.bacc as bacc
    from concourse.bass_utils import run_bass_kernel_spmd
    nc = bacc.Bacc("TRN2", target_bir_lowering=False, num_devices=1)
    arrays, args = {}, []
    for name, a in lay_out(inputs).items():
        a = np.ascontiguousarray(a)
        arrays[f"in_{name}_dram"] = a
        args.append(nc.dram_tensor(f"in_{name}_dram", a.shape, mybir.dt.from_np(a.dtype),
                                   kind="ExternalInput").ap())
    shapes = dict(projT=(NBLK, P, S), qn=(512, S), qp=(256, S), kn=(512, S), kp=(ROPE, S), va=(S, 512),
                  vb=(S, 512), ogT=(3, 512, S), mergedT=(D, S))
    scratch = [nc.dram_tensor(n, sh, F32).ap() for n, sh in shapes.items()]
    out = nc.dram_tensor("out_dram", (1, S, D), F32, kind="ExternalOutput").ap()
    build(nc, *args, out, scratch)
    r = run_bass_kernel_spmd(nc, [arrays], core_ids=[0])
    return r.results[0]["out_dram"]
```
